# Optimizing a Trainium2 kernel written in Bass

```python
import jax, jax.numpy as jnp
from jax import lax
import numpy as np

D_MODEL = 1024
BATCH = 1
SEQ = 256
DEPTH = 2
DEC_BATCH = 8
DEC_SEQ = 4
PAST_LEN = 1024
PAGE_SIZE = 128

N_HEADS = 16
HEAD_DIM = D_MODEL // N_HEADS
KV_HEADS = 4
HEADS_PER_KV = N_HEADS // KV_HEADS
KV_WIDTH = KV_HEADS * HEAD_DIM
ROT_DIM = HEAD_DIM // 4
ROPE_THETA = 500000.0
CMP_BLOCK = 32
SEL_BLOCK = 64
CMP_PER_SEL = SEL_BLOCK // CMP_BLOCK
TOP_N = 8
WINDOW = 512
Q_BLOCK = 64
N_BRANCH = 3
FORCE_BONUS = float(HEADS_PER_KV + 1)
NSA_IN_WIDTH = N_HEADS * HEAD_DIM + 6 * KV_WIDTH + N_BRANCH * N_HEADS
CONV_WIDTH = 3
CONV_DIM = D_MODEL
D_FF = (7 * D_MODEL) // 2
N_EXPERTS = 8
TOP_K = 2
N_ATTN_LAYERS = (DEPTH + 1) // 2
N_CONV_LAYERS = DEPTH // 2
N_DENSE_FFN = (DEPTH + 1) // 2
N_MOE_FFN = DEPTH // 2
EPS = 1e-6

kernel_name = 'nsa_shortconv_moe_hybrid_step'

def _rmsnorm(x, g):
    x32 = x.astype(jnp.float32)
    y = x32 * lax.rsqrt(jnp.mean(x32 * x32, axis=-1, keepdims=True) + EPS)
    return y.astype(x.dtype) * g

def _rope(x, pos):
    half = ROT_DIM // 2
    inv = 1.0 / (ROPE_THETA ** (jnp.arange(half, dtype=jnp.float32) * (2.0 / ROT_DIM)))
    ang = pos.astype(jnp.float32)[:, None] * inv[None, :]
    cos = jnp.cos(ang)[:, None, :].astype(x.dtype)
    sin = jnp.sin(ang)[:, None, :].astype(x.dtype)
    x1 = x[..., :half]
    x2 = x[..., half:ROT_DIM]
    return jnp.concatenate([x1 * cos - x2 * sin, x2 * cos + x1 * sin, x[..., ROT_DIM:]], axis=-1)

def _masked_softmax(s, mask):
    s = jnp.where(mask, s, -jnp.inf)
    m = jnp.max(s, axis=-1, keepdims=True)
    m = jnp.where(jnp.isfinite(m), m, 0.0)
    e = jnp.where(mask, jnp.exp(s - m), 0.0)
    return e / jnp.maximum(jnp.sum(e, axis=-1, keepdims=True), 1e-30)

def _compress(rows, w, pe):
    b, tk = rows.shape[0], rows.shape[1]
    nc = tk // CMP_BLOCK
    blocks = rows[:, :nc * CMP_BLOCK].reshape(b, nc, CMP_BLOCK, KV_HEADS, HEAD_DIM) + pe[None, None, :, None, :]
    return jnp.einsum('bnlgd,lde->bnge', blocks, w)

def _nsa_attend(q, gates, q_pos0, k_cmp, v_cmp, k_sel, v_sel, k_win, v_win, win_pos0, w_ck, pe_ck, w_cv, pe_cv):
    b, tq = q.shape[0], q.shape[1]
    tk = k_cmp.shape[1]
    scale = HEAD_DIM ** -0.5
    ck = _compress(k_cmp, w_ck, pe_ck)
    cv = _compress(v_cmp, w_cv, pe_cv)
    nc = ck.shape[1]
    c_end = jnp.arange(nc) * CMP_BLOCK + (CMP_BLOCK - 1)
    ck = _rope(ck, c_end)
    ns = -(-tk // SEL_BLOCK)
    pad = ns * SEL_BLOCK - tk
    kb = jnp.pad(k_sel, ((0, 0), (0, pad), (0, 0), (0, 0))).reshape(b, ns, SEL_BLOCK, KV_HEADS, HEAD_DIM).transpose(0, 3, 1, 2, 4)
    vb = jnp.pad(v_sel, ((0, 0), (0, pad), (0, 0), (0, 0))).reshape(b, ns, SEL_BLOCK, KV_HEADS, HEAD_DIM).transpose(0, 3, 1, 2, 4)
    n_sel = min(TOP_N, ns)
    bi = jnp.arange(b)[:, None, None]
    gi = jnp.arange(KV_HEADS)[None, :, None]
    kwp = jnp.pad(k_win, ((0, 0), (WINDOW, 0), (0, 0), (0, 0)))
    vwp = jnp.pad(v_win, ((0, 0), (WINDOW, 0), (0, 0), (0, 0)))
    qb_len = Q_BLOCK if (tq > Q_BLOCK and tq % Q_BLOCK == 0) else tq
    nb = tq // qb_len

    def block(args):
        qb, gb, i = args
        p0 = q_pos0 + i * qb_len
        t = p0 + jnp.arange(qb_len)
        qg = qb.reshape(b, qb_len, KV_HEADS, HEADS_PER_KV, HEAD_DIM)
        s = jnp.einsum('bqgrd,bngd->bqgrn', qg, ck, preferred_element_type=jnp.float32) * scale
        vis = (c_end[None, :] <= t[:, None])[None, :, None, None, :]
        p_c = _masked_softmax(s, vis)
        o_c = jnp.einsum('bqgrn,bngd->bqgrd', p_c.astype(cv.dtype), cv)
        imp = jnp.sum(p_c, axis=3)
        imp = jnp.pad(imp, ((0, 0), (0, 0), (0, 0), (0, ns * CMP_PER_SEL - nc)))
        imp = imp.reshape(b, qb_len, KV_HEADS, ns, CMP_PER_SEL).sum(-1)
        blk = jnp.arange(ns)
        cur = t // SEL_BLOCK
        forced = (blk[None, :] == 0) | (blk[None, :] == cur[:, None])
        valid = blk[None, :] <= cur[:, None]
        score = jnp.where(valid[None, :, None, :], imp + FORCE_BONUS * forced[None, :, None, :], -jnp.inf)
        _, idx = lax.top_k(score, n_sel)
        idx_t = idx.transpose(0, 2, 1, 3).reshape(b, KV_HEADS, qb_len * n_sel)
        ks = kb[bi, gi, idx_t].reshape(b, KV_HEADS, qb_len, n_sel * SEL_BLOCK, HEAD_DIM)
        vs = vb[bi, gi, idx_t].reshape(b, KV_HEADS, qb_len, n_sel * SEL_BLOCK, HEAD_DIM)
        kpos = (idx[..., None] * SEL_BLOCK + jnp.arange(SEL_BLOCK)).reshape(b, qb_len, KV_HEADS, n_sel * SEL_BLOCK)
        smask = (kpos <= t[None, :, None, None])[:, :, :, None, :]
        s = jnp.einsum('bqgrd,bgqkd->bqgrk', qg, ks, preferred_element_type=jnp.float32) * scale
        p_s = _masked_softmax(s, smask)
        o_s = jnp.einsum('bqgrk,bgqkd->bqgrd', p_s.astype(vs.dtype), vs)
        start = p0 - win_pos0
        kw = lax.dynamic_slice_in_dim(kwp, start, WINDOW + qb_len, axis=1)
        vw = lax.dynamic_slice_in_dim(vwp, start, WINDOW + qb_len, axis=1)
        wpos = p0 - WINDOW + jnp.arange(WINDOW + qb_len)
        wmask = (wpos[None, :] <= t[:, None]) & (wpos[None, :] >= t[:, None] - WINDOW) & (wpos[None, :] >= win_pos0)
        s = jnp.einsum('bqgrd,bkgd->bqgrk', qg, kw, preferred_element_type=jnp.float32) * scale
        p_w = _masked_softmax(s, wmask[None, :, None, None, :])
        o_w = jnp.einsum('bqgrk,bkgd->bqgrd', p_w.astype(vw.dtype), vw)
        g = gb.reshape(b, qb_len, KV_HEADS, HEADS_PER_KV, N_BRANCH)
        o = g[..., 0:1] * o_c + g[..., 1:2] * o_s + g[..., 2:3] * o_w
        return o.reshape(b, qb_len, N_HEADS, HEAD_DIM)

    if nb == 1:
        return block((q, gates, 0))
    qs = q.reshape(b, nb, qb_len, N_HEADS, HEAD_DIM).transpose(1, 0, 2, 3, 4)
    gs = gates.reshape(b, nb, qb_len, N_HEADS * N_BRANCH).transpose(1, 0, 2, 3)
    out = lax.map(block, (qs, gs, jnp.arange(nb)))
    return out.transpose(1, 0, 2, 3, 4).reshape(b, tq, N_HEADS, HEAD_DIM)

def _nsa_mixer(h, q_pos0, past_cmp, past_sel, win_buf, w_in, w_out, w_ck, pe_ck, w_cv, pe_cv):
    b, t, _ = h.shape
    hq = N_HEADS * HEAD_DIM
    proj = h @ w_in
    q = proj[..., :hq].reshape(b, t, N_HEADS, HEAD_DIM)
    kv = proj[..., hq:hq + 6 * KV_WIDTH].reshape(b, t, 6, KV_HEADS, HEAD_DIM)
    gates = jax.nn.sigmoid(proj[..., hq + 6 * KV_WIDTH:].astype(jnp.float32)).astype(h.dtype).reshape(b, t, N_HEADS, N_BRANCH)
    pos = q_pos0 + jnp.arange(t)
    q = _rope(q, pos)
    new_cmp = jnp.stack([kv[:, :, 0], kv[:, :, 1]], axis=2)
    new_sel = jnp.stack([_rope(kv[:, :, 2], pos), kv[:, :, 3]], axis=2)
    new_win = jnp.stack([_rope(kv[:, :, 4], pos), kv[:, :, 5]], axis=2)
    if past_cmp is None:
        cmp_rows, sel_rows, win_rows, win_pos0 = new_cmp, new_sel, new_win, 0
        win_state = new_win[:, -min(WINDOW, t):]
    else:
        wb = win_buf.shape[1]
        cmp_rows = jnp.concatenate([past_cmp, new_cmp], axis=1)
        sel_rows = jnp.concatenate([past_sel, new_sel], axis=1)
        win_rows = jnp.concatenate([win_buf, new_win], axis=1)
        win_pos0 = q_pos0 - wb
        win_state = win_rows[:, -wb:]
    o = _nsa_attend(q, gates, q_pos0, cmp_rows[:, :, 0], cmp_rows[:, :, 1], sel_rows[:, :, 0], sel_rows[:, :, 1],
                    win_rows[:, :, 0], win_rows[:, :, 1], win_pos0, w_ck, pe_ck, w_cv, pe_cv)
    return o.reshape(b, t, hq) @ w_out, new_cmp, new_sel, win_state

def _conv_mixer(h, state, w_in, w_conv, w_out):
    b, t, _ = h.shape
    bg, cg, v = jnp.split(h @ w_in, 3, axis=-1)
    u = cg * v
    prev = jnp.zeros((b, CONV_WIDTH - 1, CONV_DIM), u.dtype) if state is None else state
    ue = jnp.concatenate([prev, u], axis=1)
    conv = w_conv[0] * ue[:, 0:t]
    for j in range(1, CONV_WIDTH):
        conv = conv + w_conv[j] * ue[:, j:j + t]
    return (bg * conv) @ w_out, ue[:, -(CONV_WIDTH - 1):]

def _swiglu(h, w_gu, w_down):
    g, u = jnp.split(h @ w_gu, 2, axis=-1)
    return (jax.nn.silu(g) * u) @ w_down

def _moe(h, w_router, b_router, w_gu, w_down):
    logits = (h @ w_router).astype(jnp.float32) + b_router.astype(jnp.float32)
    top_v, top_i = lax.top_k(logits, TOP_K)
    top_w = jax.nn.softmax(top_v, axis=-1)
    combine = jnp.sum(jax.nn.one_hot(top_i, N_EXPERTS, dtype=jnp.float32) * top_w[..., None], axis=-2).astype(h.dtype)
    out = jnp.zeros_like(h)
    for e in range(N_EXPERTS):
        out = out + combine[..., e:e + 1] * _swiglu(h, w_gu[e], w_down[e])
    return out

def _trunk(x, c, q_pos0, caches, p):
    new_cmp, new_sel, new_win, new_conv = [], [], [], []
    cs = jax.nn.silu(c)
    for i in range(DEPTH):
        mod = (cs @ p['w_ada'][i] + p['b_ada'][i])[:, None, :]
        sh1, sc1, g1, sh2, sc2, g2 = jnp.split(mod, 6, axis=-1)
        h = _rmsnorm(x, p['g_norm_mix'][i]) * (1 + sc1) + sh1
        j = i // 2
        if i % 2 == 0:
            if caches is None:
                past_cmp = past_sel = win_buf = None
            else:
                pt = caches['page_table']
                nrows = pt.shape[1] * PAGE_SIZE
                past_cmp = caches['cmp'][j][pt].reshape(pt.shape[0], nrows, 2, KV_HEADS, HEAD_DIM)
                past_sel = caches['sel'][j][pt].reshape(pt.shape[0], nrows, 2, KV_HEADS, HEAD_DIM)
                win_buf = caches['win'][j]
            y, nc_, ns_, nw_ = _nsa_mixer(h, q_pos0, past_cmp, past_sel, win_buf, p['w_nsa_in'][j], p['w_nsa_out'][j],
                                          p['w_cmp_k'][j], p['pe_cmp_k'][j], p['w_cmp_v'][j], p['pe_cmp_v'][j])
            new_cmp.append(nc_)
            new_sel.append(ns_)
            new_win.append(nw_)
        else:
            state = None if caches is None else caches['conv'][j]
            y, st = _conv_mixer(h, state, p['w_conv_in'][j], p['w_conv'][j], p['w_conv_out'][j])
            new_conv.append(st)
        x = x + g1 * y
        h = _rmsnorm(x, p['g_norm_ffn'][i]) * (1 + sc2) + sh2
        if i % 2 == 0:
            f = _swiglu(h, p['w_ff_gu'][j], p['w_ff_down'][j])
        else:
            f = _moe(h, p['w_router'][j], p['b_router'][j], p['w_moe_gu'][j], p['w_moe_down'][j])
        x = x + g2 * f
    y = _rmsnorm(x, p['g_norm_final'])
    return y, jnp.stack(new_cmp), jnp.stack(new_sel), jnp.stack(new_win), jnp.stack(new_conv)

def setup_inputs(seed: int = 0) -> dict:
    key = jax.random.key(seed)
    ks = jax.random.split(key, 32)
    f32 = jnp.float32

    def nrm(k, shape, scale):
        return jax.random.normal(k, shape, f32) * scale

    n_pages = PAST_LEN // PAGE_SIZE
    n_used = DEC_BATCH * n_pages
    n_phys = n_used + max(1, n_used // 4)
    win_buf = min(WINDOW, PAST_LEN)
    page_table = jax.random.permutation(ks[0], n_phys)[:n_used].reshape(DEC_BATCH, n_pages).astype(jnp.int32)
    return {
        'x_prompt': nrm(ks[1], (BATCH, SEQ, D_MODEL), 1.0),
        'x_sample': nrm(ks[2], (DEC_BATCH, DEC_SEQ, D_MODEL), 1.0),
        'cache_cmp_kv': nrm(ks[3], (N_ATTN_LAYERS, n_phys, PAGE_SIZE, 2, KV_HEADS, HEAD_DIM), 1.0),
        'cache_sel_kv': nrm(ks[4], (N_ATTN_LAYERS, n_phys, PAGE_SIZE, 2, KV_HEADS, HEAD_DIM), 1.0),
        'cache_win_kv': nrm(ks[5], (N_ATTN_LAYERS, DEC_BATCH, win_buf, 2, KV_HEADS, HEAD_DIM), 1.0),
        'state_conv': nrm(ks[6], (N_CONV_LAYERS, DEC_BATCH, CONV_WIDTH - 1, CONV_DIM), 1.0),
        'page_table': page_table,
        'c_prompt': nrm(ks[7], (BATCH, D_MODEL), 1.0),
        'c_sample': nrm(ks[8], (DEC_BATCH, D_MODEL), 1.0),
        'w_ada': nrm(ks[9], (DEPTH, D_MODEL, 6 * D_MODEL), 0.5 * D_MODEL ** -0.5),
        'b_ada': nrm(ks[10], (DEPTH, 6 * D_MODEL), 0.01),
        'g_norm_mix': 1.0 + nrm(ks[11], (DEPTH, D_MODEL), 0.05),
        'g_norm_ffn': 1.0 + nrm(ks[12], (DEPTH, D_MODEL), 0.05),
        'g_norm_final': 1.0 + nrm(ks[13], (D_MODEL,), 0.05),
        'w_nsa_in': nrm(ks[14], (N_ATTN_LAYERS, D_MODEL, NSA_IN_WIDTH), D_MODEL ** -0.5),
        'w_nsa_out': nrm(ks[15], (N_ATTN_LAYERS, N_HEADS * HEAD_DIM, D_MODEL), (N_HEADS * HEAD_DIM) ** -0.5),
        'w_cmp_k': nrm(ks[16], (N_ATTN_LAYERS, CMP_BLOCK, HEAD_DIM, HEAD_DIM), (CMP_BLOCK * HEAD_DIM) ** -0.5),
        'pe_cmp_k': nrm(ks[17], (N_ATTN_LAYERS, CMP_BLOCK, HEAD_DIM), 0.1),
        'w_cmp_v': nrm(ks[18], (N_ATTN_LAYERS, CMP_BLOCK, HEAD_DIM, HEAD_DIM), (CMP_BLOCK * HEAD_DIM) ** -0.5),
        'pe_cmp_v': nrm(ks[19], (N_ATTN_LAYERS, CMP_BLOCK, HEAD_DIM), 0.1),
        'w_conv_in': nrm(ks[20], (N_CONV_LAYERS, D_MODEL, 3 * CONV_DIM), D_MODEL ** -0.5),
        'w_conv': nrm(ks[21], (N_CONV_LAYERS, CONV_WIDTH, CONV_DIM), CONV_WIDTH ** -0.5),
        'w_conv_out': nrm(ks[22], (N_CONV_LAYERS, CONV_DIM, D_MODEL), CONV_DIM ** -0.5),
        'w_ff_gu': nrm(ks[23], (N_DENSE_FFN, D_MODEL, 2 * D_FF), D_MODEL ** -0.5),
        'w_ff_down': nrm(ks[24], (N_DENSE_FFN, D_FF, D_MODEL), D_FF ** -0.5),
        'w_router': nrm(ks[25], (N_MOE_FFN, D_MODEL, N_EXPERTS), D_MODEL ** -0.5),
        'b_router': nrm(ks[26], (N_MOE_FFN, N_EXPERTS), 0.01),
        'w_moe_gu': nrm(ks[27], (N_MOE_FFN, N_EXPERTS, D_MODEL, 2 * D_FF), D_MODEL ** -0.5),
        'w_moe_down': nrm(ks[28], (N_MOE_FFN, N_EXPERTS, D_FF, D_MODEL), D_FF ** -0.5),
    }

def reference(x_prompt, x_sample, cache_cmp_kv, cache_sel_kv, cache_win_kv, state_conv, page_table, c_prompt, c_sample,
              w_ada, b_ada, g_norm_mix, g_norm_ffn, g_norm_final, w_nsa_in, w_nsa_out, w_cmp_k, pe_cmp_k, w_cmp_v, pe_cmp_v,
              w_conv_in, w_conv, w_conv_out, w_ff_gu, w_ff_down, w_router, b_router, w_moe_gu, w_moe_down):
    p = {'w_ada': w_ada, 'b_ada': b_ada, 'g_norm_mix': g_norm_mix, 'g_norm_ffn': g_norm_ffn, 'g_norm_final': g_norm_final,
         'w_nsa_in': w_nsa_in, 'w_nsa_out': w_nsa_out, 'w_cmp_k': w_cmp_k, 'pe_cmp_k': pe_cmp_k, 'w_cmp_v': w_cmp_v,
         'pe_cmp_v': pe_cmp_v, 'w_conv_in': w_conv_in, 'w_conv': w_conv, 'w_conv_out': w_conv_out, 'w_ff_gu': w_ff_gu,
         'w_ff_down': w_ff_down, 'w_router': w_router, 'b_router': b_router, 'w_moe_gu': w_moe_gu, 'w_moe_down': w_moe_down}
    y_prompt, cmp_p, sel_p, win_p, conv_p = _trunk(x_prompt, c_prompt, 0, None, p)
    past_len = page_table.shape[1] * PAGE_SIZE
    caches = {'cmp': cache_cmp_kv, 'sel': cache_sel_kv, 'win': cache_win_kv, 'conv': state_conv, 'page_table': page_table}
    y_sample, cmp_s, sel_s, win_s, conv_s = _trunk(x_sample, c_sample, past_len, caches, p)
    return (y_prompt, y_sample, cmp_p, cmp_s, sel_p, sel_s, win_p, win_s, conv_p, conv_s)


_drawn_inputs = setup_inputs


def setup_inputs(seed=0):
    import zlib

    import numpy as np

    out = dict(_drawn_inputs(seed))
    spreads = {}
    factors = {'cache_sel_kv': 3.13, 'pe_cmp_k': 8.0, 'b_router': 18.668}
    for name, (base, spread) in spreads.items():
        noise = np.random.default_rng([zlib.crc32(name.encode()), seed]).standard_normal(out[name].shape)
        drawn = base * np.exp(spread * noise) if base else spread * noise
        out[name] = __import__('jax').numpy.asarray(drawn.astype(out[name].dtype))
    for name, factor in factors.items():
        out[name] = (out[name] * factor).astype(out[name].dtype)
    return out
```

```python
from contextlib import ExitStack

import concourse.bass as bass
from concourse import mybir

F32 = mybir.dt.float32
I32 = mybir.dt.int32
ALU = mybir.AluOpType
ACT = mybir.ActivationFunctionType
AX = mybir.AxisListType.X

D = 1024
DC = D // 128
SEQ = 256
NB, NT = 8, 4
NTOK = SEQ + NB * NT
HD = 64
FF = 3584
NE = 8
KVW = 256
PROJ = 2608
SCALE = HD ** -0.5
BIG = 1.0e30
EPS = 1e-6
RING = 7
SLOT = 2048
SLOTS_E = 128
TILES_E = 42
TOK = [(0, 128), (128, 128), (256, 32)]

CONSTS = [("ident", 128), ("causal", 256), ("rot", 128), ("ckcos", 32), ("cksin", 32), ("tcos", 24), ("tsin", 24),
          ("cmpadd", 16), ("cmpmul", 16), ("headsum", 128), ("bonus", 17), ("winmask", 512), ("newmask", 128),
          ("rowtok", 512), ("rowhead", 16), ("before", 289), ("repn", 128), ("vbdmask", 16), ("earlier", 128),
          ("ones", 128), ("iota", 128), ("valid", 3), ("eps", 1)]
AT = {}
_o = 0
for _n, _w in CONSTS:
    AT[_n] = (_o, _w)
    _o += _w
NCONST = _o


class Count:

    def __init__(self, sem):
        self.sem, self.n = sem, 0

    def inc(self, ins):
        ins.then_inc(self.sem, 1)
        self.n += 1

    def wait(self, eng):
        eng.wait_ge(self.sem, self.n)


def trunk(nc, A, O):
    with ExitStack() as ctx:
        def sb(name, shape, dt=F32):
            return ctx.enter_context(nc.sbuf_tensor(name, shape, dt))

        def sem(name):
            return ctx.enter_context(nc.semaphore(name))

        ps = ctx.enter_context(nc.psum_tensor("ps", [128, 8, 512], F32))
        ring = sb("ring", [128, RING, SLOT])
        work = sb("work", [128, 16384])
        con = sb("con", [128, NCONST])
        xT = sb("xT", [128, DC, NTOK])
        hT = sb("hT", [128, DC, NTOK])
        oT = hT
        nT = sb("nT", [128, DC, NTOK])
        std = sb("std", [128, NTOK])
        rstd = sb("rstd", [128, NTOK])
        modT = sb("modT", [128, 2, 6, DC, 9])
        rowsT = sb("rowsT", [128, 296])
        qT = sb("qT", [128, 8, SEQ])
        kTp = sb("kTp", [128, 2, 2, SEQ])
        cTp = sb("cTp", [128, 2, 2, SEQ])
        qbd = sb("qbd", [128, NB, 64])
        kTn = sb("kTn", [128, 2, 2, 32])
        vnew = sb("vnew", [32, 2, KVW])
        gnew = sb("gnew", [32, 48])
        attn = sb("attn", [128, 1632 + 15 * 128])
        small = sb("small", [128, 128])
        pgt = sb("pgt", [1, 64], I32)
        cnti = sb("cnti", [1, 1], I32)
        wr = sb("wr", [128, DC, 8])
        br = sb("br", [128, 8])

        def C(name, p=128):
            o, w = AT[name]
            return con[0:p, o:o + w]

        b_adaT = rowsT[:, 0:96].rearrange("p (l c) -> p l c", l=2)
        g_mixT = rowsT[:, 96:112].rearrange("p (l c) -> p l c", l=2)
        g_ffnT = rowsT[:, 112:128].rearrange("p (l c) -> p l c", l=2)
        g_finT = rowsT[:, 128:136]
        w_convT = rowsT[:, 136:160].rearrange("p (j c) -> p j c", j=3)
        csT = rowsT[:, 160:232].rearrange("p (s c) -> p s c", s=9)
        peT = rowsT[:, 232:296].rearrange("p (k l) -> p k l", k=2)

        xrow = work[:, 0:3072].rearrange("p (t d) -> p t d", t=3)
        rowsA = work[0:96, 3072:3200]
        rowsB = work[0:64, 3200:3328]
        rowsC = work[0:72, 3328:3456]
        rowsCe = work[0:72, 3456:3584]
        rowsP = work[0:32, 3584:3840]
        proj = work[:, 0:3 * PROJ].rearrange("p (t n) -> p t n", t=3)
        wbd = work[:, 8192:16384].rearrange("p (k l e) -> p k l e", k=2, l=32)
        TKV = work[:, 0:4096].rearrange("p (k g n) -> p k g n", k=2, g=2)
        TS = work[:, 4096:6144].rearrange("p (g n) -> p g n", g=2)
        TW = work[:, 6144:7168].rearrange("p (g n) -> p g n", g=2)
        actF = work[:, 0:28 * NTOK].rearrange("p (c t) -> p c t", c=28)
        sgF = work[:, 8192:8192 + 2 * 2 * NTOK].rearrange("p (i k t) -> p i k t", i=2, k=2)
        bgT = work[:, 0:2304].rearrange("p (c t) -> p c t", c=8)
        cgT = work[:, 2304:4608].rearrange("p (c t) -> p c t", c=8)
        uP = work[:, 4608:4608 + 8 * 258].rearrange("p (c t) -> p c t", c=8)
        uS = work[:, 6672:6672 + 8 * 48].rearrange("p (c b t) -> p c b t", c=8, b=8)
        zT = work[:, 7056:7056 + 2304].rearrange("p (c t) -> p c t", c=8)
        ctmp = work[:, 9360:9360 + 2 * 288].rearrange("p (i t) -> p i t", i=2)
        tail = work[:, 9936:9936 + 8 * 18].rearrange("p (c j) -> p c j", c=8)
        strow = attn[0:16, 0:1024]
        tailrow = attn[0:18, 1024:2048]
        hN = work[:, 0:3072].rearrange("p (t d) -> p t d", t=3)
        yacc = work[:, 3072:3072 + 2304].rearrange("p (c t) -> p c t", c=8)
        XT = work[:, 5376:6400].rearrange("p (c s) -> p c s", c=8)
        actM = work[:, 6400:7424].rearrange("p (i n) -> p i n", i=2)
        actT = work[:, 7424:7424 + 3584].rearrange("p (k s) -> p k s", k=28)
        eM = work[:, 11008:11520]
        rM = work[:, 11520:12032]
        ysb = work[:, 12032:13056]
        Dm = work[:, 13056:13440].rearrange("p (t s) -> p t s", t=3)
        Dw = work[:, 13440:13824].rearrange("p (t s) -> p t s", t=3)
        DT = work[:, 13824:14112]
        outN = work[:, 0:3072].rearrange("p (t d) -> p t d", t=3)
        lg = work[:, 14112:14136].rearrange("p (t e) -> p t e", t=3)
        selE = work[:, 14136:14160].rearrange("p (t e) -> p t e", t=3)
        cw = work[:, 14160:14184].rearrange("p (t e) -> p t e", t=3)
        pos = work[:, 14184:14208].rearrange("p (t e) -> p t e", t=3)
        rkA = work[:, 14208:14400].rearrange("p (t j i) -> p t j i", t=3, j=8)
        rkB = work[:, 14400:14592].rearrange("p (t j i) -> p t j i", t=3, j=8)
        mE = work[:, 14592:14608]
        cnt8 = work[:, 14608:14616]
        cur = work[:, 14616:14632].rearrange("p (a t) -> p a t", a=4)
        Ssb = attn[:, 0:1536].rearrange("p (i n) -> p i n", i=3)
        PTs = attn[:, 1536:2560].rearrange("p (i n) -> p i n", i=2)
        ScP = attn[:, 2560:2816].rearrange("p (t n) -> p t n", t=2)
        PTc = attn[:, 2816:3072].rearrange("p (t n) -> p t n", t=2)
        SS = attn[:, 0:1632]
        PT = attn[:, 1632:1632 + 1920].rearrange("p (k n) -> p k n", k=15)
        ropet = attn[:, 0:512].rearrange("p (k n) -> p k n", k=4)
        Vbd = sb("Vbd", [128, 8, 128])
        cmpv = sb("cmpv", [128, 2, 64])
        ckr = sb("ckr", [128, 64])
        ckt = sb("ckt", [128, 64])
        cvn = sb("cvn", [32, 2, KVW])
        peb = sb("peb", [128, 2])
        rank = Vbd[:].rearrange("p c n -> p (c n)")[:, 0:578].rearrange("p (i n) -> p i n", i=2)

        s3 = Vbd[:].rearrange("p c n -> p (c n)")[:, 600:696]
        s_slot = [sem(f"s_slot{i}") for i in range(RING)]
        s_used = sem("s_used")
        s_consts_in = sem("s_consts_in")
        s_rows_in = sem("s_rows_in")
        s_c_in = sem("s_c_in")
        s_x_in = sem("s_x_in")
        s_router_in = sem("s_router_in")
        s_pages_in = sem("s_pages_in")
        s_wbd_clear = sem("s_wbd_clear")
        s_wbd_in = sem("s_wbd_in")
        s_cexp = sem("s_cexp")
        s_csilu = sem("s_csilu")
        s_rows_turned = sem("s_rows_turned")
        s_rowsT_ready = sem("s_rowsT_ready")
        s_x_turned = sem("s_x_turned")
        s_x_ready = sem("s_x_ready")
        s_ada_done = sem("s_ada_done")
        s_mod_ready = sem("s_mod_ready")
        s_sq_ready = sem("s_sq_ready")
        s_ss_done = sem("s_ss_done")
        s_std_ready = sem("s_std_ready")
        s_rstd_ready = sem("s_rstd_ready")
        s_xhat_ready = sem("s_xhat_ready")
        s_h_prompt = sem("s_h_prompt")
        s_h_sample = sem("s_h_sample")
        s_proj_done = sem("s_proj_done")
        s_proj_dve = sem("s_proj_dve")
        s_proj_act = sem("s_proj_act")
        s_gate_exp = sem("s_gate_exp")
        s_rope_done = sem("s_rope_done")
        s_qk_turned = sem("s_qk_turned")
        s_qk_prompt = sem("s_qk_prompt")
        s_qk_sample = sem("s_qk_sample")
        s_vnew_ready = sem("s_vnew_ready")
        s_pe_ready = sem("s_pe_ready")
        s_cmp_prompt = sem("s_cmp_prompt")
        s_cmp_copied = sem("s_cmp_copied")
        s_rot_prompt = sem("s_rot_prompt")
        s_ck_prompt = sem("s_ck_prompt")
        s_cv_prompt = sem("s_cv_prompt")
        s_cv_spread = sem("s_cv_spread")
        s_vbd_ready = sem("s_vbd_ready")
        s_cscore_done = sem("s_cscore_done")
        s_cscore_shift = sem("s_cscore_shift")
        s_cscore_exp = sem("s_cscore_exp")
        s_cprob_ready = sem("s_cprob_ready")
        s_cprob_turned = sem("s_cprob_turned")
        s_cprobT_ready = sem("s_cprobT_ready")
        s_scores_done = sem("s_scores_done")
        s_scores_taken = sem("s_scores_taken")
        s_dve_chain = sem("s_dve_chain")
        s_negmax_ready = sem("s_negmax_ready")
        s_exp_ready = sem("s_exp_ready")
        s_probs_ready = sem("s_probs_ready")
        s_probs_turned = sem("s_probs_turned")
        s_probsT_ready = sem("s_probsT_ready")
        s_pv_done = sem("s_pv_done")
        s_o_taken = sem("s_o_taken")
        s_bank_turned = sem("s_bank_turned")
        s_bank_act = sem("s_bank_act")
        s_bank_dve = sem("s_bank_dve")
        s_cmp_done = sem("s_cmp_done")
        s_craw_ready = sem("s_craw_ready")
        s_rot_done = sem("s_rot_done")
        s_ck_ready = sem("s_ck_ready")
        s_seq_scores = sem("s_seq_scores")
        s_gate_rows = sem("s_gate_rows")
        s_group_scores = sem("s_group_scores")
        s_cnegmax = sem("s_cnegmax")
        s_cexp_ready = sem("s_cexp_ready")
        s_cprobs = sem("s_cprobs")
        s_importance = sem("s_importance")
        s_snegmax = sem("s_snegmax")
        s_sexp_ready = sem("s_sexp_ready")
        s_group_probs = sem("s_group_probs")
        s_group_pv = sem("s_group_pv")
        s_group_o = sem("s_group_o")
        s_wo_done = sem("s_wo_done")
        s_gu_done = sem("s_gu_done")
        s_gexp_ready = sem("s_gexp_ready")
        s_act_ready = sem("s_act_ready")
        s_down_done = sem("s_down_done")
        s_conv_done = sem("s_conv_done")
        s_conv_copied = sem("s_conv_copied")
        s_u_ready = sem("s_u_ready")
        s_tail_ready = sem("s_tail_ready")
        s_z_ready = sem("s_z_ready")
        s_state_in = sem("s_state_in")
        s_state_turned = sem("s_state_turned")
        s_tail_turned = sem("s_tail_turned")
        s_tail_rows = sem("s_tail_rows")
        s_kv_stored = sem("s_kv_stored")
        s_logits_done = sem("s_logits_done")
        s_logits_shift = sem("s_logits_shift")
        s_logits_exp = sem("s_logits_exp")
        s_sel_ready = sem("s_sel_ready")
        s_pos_done = sem("s_pos_done")
        s_count_ready = sem("s_count_ready")
        s_rows_done = sem("s_rows_done")
        s_rows_taken = sem("s_rows_taken")
        s_gathered = sem("s_gathered")
        s_xt_act = sem("s_xt_act")
        s_xt_dve = sem("s_xt_dve")
        s_scatter_ready = sem("s_scatter_ready")
        s_up_done = sem("s_up_done")
        s_eexp_ready = sem("s_eexp_ready")
        s_moe_chain = sem("s_moe_chain")
        s_eact_ready = sem("s_eact_ready")
        s_eact_turned = sem("s_eact_turned")
        s_eactT_ready = sem("s_eactT_ready")
        s_y_done = sem("s_y_done")
        s_y_act = sem("s_y_act")
        s_y_dve = sem("s_y_dve")
        s_share_done = sem("s_share_done")
        s_share_added = sem("s_share_added")
        s_gather_ready = sem("s_gather_ready")
        s_final_ready = sem("s_final_ready")
        s_final_rows = sem("s_final_rows")
        s_stored = sem("s_stored")

        def quarter(w, r0, c0, kcs, width):
            return w[r0:r0 + 128 * kcs, c0:c0 + width].rearrange("(k p) n -> p k n", p=128)

        stream = []

        def pair(w, c0, width=512):
            for h in range(2):
                stream.append([(0, 128, quarter(w, 512 * h, c0, 4, width), 4)])

        for k in range(24):
            pair(A["w_ada"][k // 12], (k % 12) * 512)
        T_NSA = len(stream)
        for ct in range(5):
            pair(A["w_nsa_in"][0], ct * 512)
        stream.append([(0, 128, quarter(A["w_nsa_in"][0], 0, 2560, 8, 48), 8)])
        T_CACHE = len(stream)
        for tau in range(4):
            for b in (2 * tau, 2 * tau + 1):
                for h in range(2):
                    stream.append(("page", "cmp", b, h))
            for b in (2 * tau, 2 * tau + 1):
                for h in range(2):
                    stream.append(("page", "sel", b, h))
                stream.append([(0, 128, A["cache_win_kv"][0, b].rearrange("(j p) k g d -> p j (k g d)", p=128), 4)])
        T_WO = len(stream)
        for ch in range(2):
            for gp in range(2):
                w = A["w_nsa_out"][0].rearrange("(g r d) n -> g d r n", g=4, r=4)
                stream.append([(64 * g2, 64, w[2 * gp + g2][:, :, ch * 512:ch * 512 + 512], 4) for g2 in range(2)])
        T_FU = len(stream)
        for j in range(7):
            pair(A["w_ff_gu"][0], j * 512)
            pair(A["w_ff_gu"][0], FF + j * 512)
        T_FD = len(stream)
        for ch in range(2):
            for i in range(7):
                stream.append([(0, 128, quarter(A["w_ff_down"][0], 512 * i, ch * 512, 4, 512), 4)])
        T_CI = len(stream)
        for jt in range(2):
            for wh in range(3):
                pair(A["w_conv_in"][0], wh * 1024 + jt * 512)
        T_CO = len(stream)
        for ch in range(2):
            pair(A["w_conv_out"][0], ch * 512)
        T_MOE = len(stream)
        total = [0] * RING
        need = []
        for n, ent in enumerate(stream):
            q = n % RING
            total[q] += 16 * (4 if ent[0] == "page" else len(ent))
            need.append(total[q])

        def wait_tile(pe, n):
            pe.wait_ge(s_slot[n % RING], need[n])

        def slot(n, kc=4):
            w = {4: 512, 8: 48}[kc]
            return ring[:, n % RING, 0:kc * w].rearrange("p (k n) -> p k n", k=kc)

        def dst_n(ap):
            n = 1
            for d_ in ap.shape[1:]:
                n *= d_
            return n

        def turned(j, dst):
            np_, n = dst.shape[0], dst_n(dst)
            src = ps[0:np_, 4 + j % 2, 0:n]
            return src if len(dst.shape) == 2 else src.rearrange("p (k n) -> p k n", n=128)

        block = ctx.enter_context(nc.Block())

        @block.sync
        def _(sp):
            sp.dma_start(pgt[:], A["page_table"].rearrange("(o b) p -> o (b p)", o=1)).then_inc(s_pages_in, 16)
            for n, ent in enumerate(stream):
                if n == T_CACHE:
                    sp.wait_ge(s_pages_in, 16)
                if ent[0] == "page":
                    _, kind, b, h = ent
                    src = A["cache_cmp_kv"] if kind == "cmp" else A["cache_sel_kv"]
                    for j in range(4):
                        i = b * 8 + h * 4 + j
                        pg = sp.value_load(pgt[0:1, i:i + 1], min_val=0, max_val=src.shape[1] - 1)
                        if n >= RING and j == 0:
                            sp.wait_ge(s_used, n - RING + 1)
                        sp.dma_start(slot(n)[:, j, :], src[0, bass.ds(pg, 1)].rearrange("o r k g d -> (o r) (k g d)")
                                     ).then_inc(s_slot[n % RING], 16)
                    continue
                if n >= RING:
                    sp.wait_ge(s_used, n - RING + 1)
                for p0, pn, src, kc in ent:
                    sp.dma_start(slot(n, kc)[p0:p0 + pn], src).then_inc(s_slot[n % RING], 16)

            def experts(rnd):
                with sp.Fori(0, NE) as e:
                    for i in range(TILES_E):
                        sp.wait_ge(s_used, (e + NE * rnd) * TILES_E + (T_MOE + i - RING + 1))
                        if i < 28:
                            j, u, h = i // 4, (i // 2) % 2, i % 2
                            src = A["w_moe_gu"][0, bass.ds(e, 1), 512 * h:512 * h + 512,
                                                u * FF + j * 512:u * FF + j * 512 + 512
                                                ].rearrange("o (k p) n -> p (o k) n", p=128)
                            dst = slot(T_MOE + i)
                        else:
                            src = A["w_moe_down"][0, bass.ds(e, 1), 256 * (i - 28):256 * (i - 27), :
                                                  ].rearrange("o (k p) n -> p (o k) n", p=128)
                            dst = ring[:, (T_MOE + i) % RING, :].rearrange("p (k n) -> p k n", k=2)
                        sp.dma_start(dst, src).then_inc(s_slot[(T_MOE + i) % RING], 16)

            experts(0)
            sp.wait_ge(s_count_ready, 1)
            c = sp.value_load(cnti[0:1, 0:1], min_val=0, max_val=NTOK)
            for rnd in (1, 2):
                with sp.If(c > SLOTS_E * rnd):
                    experts(rnd)

        @block.gpsimd
        def _(g):
            g.wait_ge(s_wbd_clear, 1)
            for kv, nm_ in enumerate(("w_cmp_k", "w_cmp_v")):
                for g2 in range(2):
                    g.dma_start(wbd[64 * g2:64 * g2 + 64, kv, :, 64 * g2:64 * g2 + 64],
                                A[nm_][0].rearrange("l d e -> d l e")).then_inc(s_wbd_in, 16)
            g.dma_start(O[7][0, :, 0:508].rearrange("b r k g d -> b (r k g d)"),
                        A["cache_win_kv"][0, :, 4:512].rearrange("b r k g d -> b (r k g d)")).then_inc(s_stored, 16)
            n = 1
            g.wait_ge(s_rope_done, 6)
            for o_p, o_s, c0 in ((2, 3, 1024), (4, 5, 1536), (6, None, 2048)):
                g.dma_start(O[o_p][0, 0].rearrange("(t p) k g d -> p t (k g d)", p=128),
                            proj[:, 0:2, c0:c0 + 512]).then_inc(s_stored, 16)
                n += 1
                if o_s is not None:
                    g.dma_start(O[o_s][0].rearrange("b t k g d -> (b t) (k g d)"),
                                proj[0:32, 2, c0:c0 + 512]).then_inc(s_stored, 16)
                    n += 1
                else:
                    for b in range(NB):
                        g.dma_start(O[7][0, b, 508:512].rearrange("t k g d -> t (k g d)"),
                                    proj[4 * b:4 * b + 4, 2, c0:c0 + 512]).then_inc(s_stored, 16)
                        n += 1
            g.wait_ge(s_stored, 16 * n)
            g.sem_inc(s_kv_stored, 1)
            g.wait_ge(s_tail_rows, 2)
            g.dma_start(O[8][0, 0], tailrow[0:2, :]).then_inc(s_stored, 16)
            g.dma_start(O[9][0].rearrange("b j d -> (b j) d"), tailrow[2:18, :]).then_inc(s_stored, 16)
            n += 2
            g.wait_ge(s_stored, 16 * n)
            g.wait_ge(s_final_rows, 6)
            g.dma_start(O[0][0].rearrange("(t p) d -> p t d", p=128), outN[:, 0:2, :]).then_inc(s_stored, 16)
            g.dma_start(O[1].rearrange("b t d -> (b t) d"), outN[0:32, 2, :]).then_inc(s_stored, 16)
            n += 2
            g.wait_ge(s_stored, 16 * n)

        @block.scalar
        def _(a):
            a.dma_start(rowsC[0:8, :], A["c_prompt"].rearrange("s (c p) -> (s c) p", p=128)).then_inc(s_c_in, 16)
            a.dma_start(rowsC[8:72, :], A["c_sample"].rearrange("s (c p) -> (s c) p", p=128)).then_inc(s_c_in, 16)
            a.dma_start(con[:], A["consts"]).then_inc(s_consts_in, 16)
            a.dma_start(rowsA, A["b_ada"].rearrange("l (c p) -> (l c) p", p=128)).then_inc(s_rows_in, 16)
            a.dma_start(rowsB[0:16, :], A["g_norm_mix"].rearrange("l (c p) -> (l c) p", p=128)).then_inc(s_rows_in, 16)
            a.dma_start(rowsB[16:32, :], A["g_norm_ffn"].rearrange("l (c p) -> (l c) p", p=128)).then_inc(s_rows_in, 16)
            a.dma_start(rowsB[32:40, :], A["g_norm_final"].rearrange("(c p) -> c p", p=128)).then_inc(s_rows_in, 16)
            a.dma_start(rowsB[40:64, :], A["w_conv"][0].rearrange("j (c p) -> (j c) p", p=128)).then_inc(s_rows_in, 16)
            for kv, nm_ in enumerate(("pe_cmp_k", "pe_cmp_v")):
                for g2 in range(2):
                    a.dma_start(rowsP[:, kv * 128 + g2 * 64:kv * 128 + g2 * 64 + 64], A[nm_][0]).then_inc(s_rows_in, 16)
            a.dma_start(xrow[:, 0:2, :], A["x_prompt"][0].rearrange("(t p) d -> p t d", p=128)).then_inc(s_x_in, 16)
            a.dma_start(xrow[0:32, 2, :], A["x_sample"].rearrange("b t d -> (b t) d")).then_inc(s_x_in, 16)
            a.dma_start(wr[:], A["w_router"][0].rearrange("(c p) e -> p c e", p=128)).then_inc(s_router_in, 16)
            a.dma_start(br[:], A["b_router"].to_broadcast([128, 8])).then_inc(s_router_in, 16)

            a.wait_ge(s_c_in, 32)
            a.activation(rowsCe, rowsC, ACT.Exp, scale=-1.0).then_inc(s_cexp, 1)

            def norm(n):
                for c in range(DC):
                    a.wait_ge(s_x_ready, 8 * n + c + 1)
                    if n and c == 0:
                        a.wait_ge(s_h_sample, n)
                    a.activation(nT[:, c, :], xT[:, c, :], ACT.Square).then_inc(s_sq_ready, 1)
                a.wait_ge(s_ss_done, n + 1)
                if n:
                    a.wait_ge(s_rstd_ready, n)
                a.activation(std[:], ps[:, 6, 0:NTOK], ACT.Sqrt, bias=C("eps"), scale=1.0 / D).then_inc(s_std_ready, 1)
                if n < 4:
                    lay, v = n // 2, 3 * (n % 2)
                    a.wait_ge(s_xhat_ready, n + 1)
                    a.wait_ge(s_mod_ready, lay + 1)
                    for c in range(DC):
                        a.activation(hT[:, c, 0:SEQ], nT[:, c, 0:SEQ], ACT.Identity, bias=modT[:, lay, v, c, 0:1],
                                     scale=modT[:, lay, v + 1, c, 0:1]).then_inc(s_h_prompt, 1)

            norm(0)
            for ct in range(5):
                a.wait_ge(s_proj_done, ct + 1)
                src, dst = ps[:, 3 * (ct % 2) + 1, :], proj[:, 1, ct * 512:ct * 512 + 512]
                for g2 in range(2 if ct < 2 else 1):
                    if ct < 2:
                        ins = a.activation(dst.rearrange("p (r g d) -> p g r d", r=4, g=2)[:, g2],
                                           src.rearrange("p (g r d) -> p g r d", g=2, r=4)[:, g2], ACT.Copy)
                    else:
                        ins = a.activation(dst, src, ACT.Copy)
                ins.then_inc(s_proj_act, 1)
            a.wait_ge(s_proj_done, 6)
            for t, (_, m) in enumerate(TOK):
                a.activation(proj[0:m, t, 2560:PROJ], ps[0:m, 3 + t, 0:48], ACT.Exp, scale=-1.0).then_inc(s_gate_exp, 1)
            for i in range(16):
                a.wait_ge(s_qk_turned, i + 1)
                src = ps[:, i % 6, 0:SEQ]
                if i < 8:
                    dst = qT[:, i, :]
                elif i < 12:
                    dst = kTp[:, (i - 8) % 2, (i - 8) // 2, :]
                else:
                    dst = cTp[:, (i - 12) // 2, (i - 12) % 2, :]
                a.activation(dst, src, ACT.Copy).then_inc(s_qk_prompt, 1)
            for t in range(2):
                a.wait_ge(s_cscore_shift, t + 1)
                a.activation(ScP[:, t, :], ScP[:, t, :], ACT.Exp, scale=SCALE).then_inc(s_cscore_exp, 1)
            for i in range(34):
                if i < 32:
                    w = 128 * (i // 16 + 1)
                    a.wait_ge(s_negmax_ready, i + 1)
                    for k in range(2):
                        a.activation(Ssb[:, i % 3, k * w:k * w + w], Ssb[:, i % 3, k * w:k * w + w], ACT.Exp,
                                     bias=small[:, 8 * (i % 3) + 2 + k:8 * (i % 3) + 3 + k], scale=SCALE,
                                     accum_out=small[:, 8 * (i % 3) + 4 + k:8 * (i % 3) + 5 + k]).then_inc(s_exp_ready, 1)
                if i >= 2:
                    u = i - 2
                    w = 128 * (u // 16 + 1)
                    a.wait_ge(s_probs_turned, u + 1)
                    if u >= 2:
                        a.wait_ge(s_pv_done, u - 1)
                    a.activation(PTs[:, u % 2, 0:2 * w], ps[:, 3 + u % 2, 0:2 * w], ACT.Copy).then_inc(s_probsT_ready, 1)
            a.wait_ge(s_pv_done, 32)
            a.wait_ge(s_kv_stored, 1)
            def take(j, dst):
                a.wait_ge(s_bank_turned, j + 1)
                a.activation(dst, turned(j, dst), ACT.Copy).then_inc(s_bank_act, 1)

            for tau in range(4):
                j = 32 * tau
                for b2 in range(2):
                    b = 2 * tau + b2
                    for h in range(2):
                        for kv in range(2):
                            if b:
                                a.wait_ge(s_cmp_done, b)
                            take(j, TKV[:, kv, 0, 512 * h:512 * h + 512])
                            j += 2
                for b2 in range(2):
                    b = 2 * tau + b2
                    for h in range(2):
                        if b:
                            a.wait_ge(s_seq_scores, b)
                        take(j, TS[:, 0, 512 * h:512 * h + 512])
                        j += 2
                    if b:
                        a.wait_ge(s_seq_scores, b)
                    take(j, TW[:, 0, :])
                    j += 2
                a.wait_ge(s_cnegmax, tau + 1)
                a.activation(SS[:, 1600:1632], s3[:, 64:96], ACT.Exp, bias=small[:, 33:34], scale=SCALE,
                             accum_out=small[:, 34:35]).then_inc(s_cexp_ready, 1)
                a.wait_ge(s_snegmax, tau + 1)
                for k, (lo, hi) in enumerate(((0, 1056), (1056, 1600))):
                    a.activation(SS[:, lo:hi], SS[:, lo:hi], ACT.Exp, bias=small[:, 38 + k:39 + k], scale=SCALE,
                                 accum_out=small[:, 40 + k:41 + k]).then_inc(s_sexp_ready, 1)
                if tau:
                    a.wait_ge(s_group_pv, tau)
                take(j, PT[:, 0:4, :])
                take(j + 2, PT[:, 8:12, :])
            norm(1)
            for m in range(28):
                a.wait_ge(s_gu_done, m + 1)
                if m >= 2:
                    a.wait_ge(s_act_ready, m - 1)
                a.activation(sgF[:, m % 2, 0, :], ps[:, 2 * (m % 3), 0:NTOK], ACT.Exp, scale=-1.0).then_inc(s_gexp_ready, 1)
            norm(2)
            a.dma_start(strow, A["state_conv"][0].rearrange("b j d -> (b j) d")).then_inc(s_state_in, 16)
            k = 0
            for B in range(24):
                wh, c = (B // 4) % 3, 4 * (B // 12) + B % 4
                if wh < 2:
                    a.wait_ge(s_conv_done, B + 1)
                    a.activation((bgT, cgT)[wh][:, c, :], ps[:, B % 6, 0:NTOK], ACT.Copy).then_inc(s_conv_copied, 1)
            norm(3)
            a.wait_ge(s_logits_shift, 1)
            a.activation(lg[:], lg[:], ACT.Exp).then_inc(s_logits_exp, 1)

            def experts(rnd):
                with a.Fori(0, NE) as e0:
                    e = e0 + NE * rnd
                    a.wait_ge(s_gathered, e * 3 + 1)
                    a.activation(XT[:, 0:4, :], ps[:, 4, :].rearrange("p (c s) -> p c s", c=4), ACT.Copy
                                 ).then_inc(s_xt_act, 1)
                    for j in range(7):
                        a.wait_ge(s_up_done, e * 7 + (j + 1))
                        if j:
                            a.wait_ge(s_eact_ready, e * 7 + j)
                        a.activation(eM, ps[:, 2 * (j % 2), :], ACT.Exp, scale=-1.0).then_inc(s_eexp_ready, 1)
                        if j >= 1:
                            a.wait_ge(s_eact_turned, e * 7 + j)
                            a.activation(actT[:, 4 * j - 4:4 * j, :],
                                         ps[:, 4 + (j - 1) % 2, :].rearrange("p (k s) -> p k s", k=4), ACT.Copy
                                         ).then_inc(s_eactT_ready, 1)
                    a.wait_ge(s_eact_turned, e * 7 + 7)
                    a.activation(actT[:, 24:28, :], ps[:, 4, :].rearrange("p (k s) -> p k s", k=4), ACT.Copy
                                 ).then_inc(s_eactT_ready, 1)
                    a.wait_ge(s_y_done, e + 1)
                    a.activation(ysb[:, 0:512], ps[:, 6, :], ACT.Copy).then_inc(s_y_act, 1)

            experts(0)
            a.wait_ge(s_count_ready, 1)
            c = a.value_load(cnti[0:1, 0:1], min_val=0, max_val=NTOK)
            for rnd in (1, 2):
                with a.If(c > SLOTS_E * rnd):
                    experts(rnd)
            norm(4)

        @block.vector
        def _(v):
            ch = Count(s_dve_chain)

            def link(ins):
                ch.inc(ins)
                ch.wait(v)

            link(v.memset(wbd[:], 0.0))
            v.memset(qbd[:], 0.0).then_inc(s_wbd_clear, 1)
            v.wait_ge(s_cexp, 1)
            link(v.tensor_scalar_add(rowsCe, rowsCe, 1.0))
            link(v.reciprocal(rowsCe, rowsCe))
            v.tensor_tensor(rowsC, rowsC, rowsCe, ALU.mult).then_inc(s_csilu, 1)
            v.wait_ge(s_rows_turned, 1)
            v.tensor_copy(rowsT[:], ps[:, 7, 0:296]).then_inc(s_rowsT_ready, 1)
            for c in range(DC):
                v.wait_ge(s_x_turned, c + 1)
                v.tensor_copy(xT[:, c, :], ps[:, 2 + c % 4, 0:NTOK]).then_inc(s_x_ready, 1)

            def modulation(lay):
                v.wait_ge(s_ada_done, lay + 1)
                v.wait_ge(s_rowsT_ready, 1)
                m = modT[:, lay].rearrange("p v c s -> p (v c) s")
                link(v.tensor_tensor(m, ps[:, lay, 0:432].rearrange("p (c s) -> p c s", s=9),
                                     b_adaT[:, lay].unsqueeze(2).to_broadcast([128, 48, 9]), ALU.add))
                for k, g_ in ((1, g_mixT), (4, g_ffnT)):
                    ins = v.scalar_tensor_tensor(out=modT[:, lay, k], in0=modT[:, lay, k], scalar=1.0,
                                                 in1=g_[:, lay].unsqueeze(2).to_broadcast([128, 8, 9]),
                                                 op0=ALU.add, op1=ALU.mult)
                    if k == 1:
                        link(ins)
                ins.then_inc(s_mod_ready, 1)
                v.wait_ge(s_mod_ready, lay + 1)

            def norm(n):
                v.wait_ge(s_std_ready, n + 1)
                v.reciprocal(rstd[:], std[:]).then_inc(s_rstd_ready, 1)
                v.wait_ge(s_rstd_ready, n + 1)
                v.tensor_tensor(nT[:], xT[:], rstd[:].unsqueeze(1).to_broadcast([128, DC, NTOK]),
                                ALU.mult).then_inc(s_xhat_ready, 1)
                v.wait_ge(s_xhat_ready, n + 1)
                if n < 4:
                    lay, k = n // 2, 3 * (n % 2)
                    nS = nT[:, :, SEQ:].rearrange("p c (b t) -> p c b t", t=NT)
                    hS = hT[:, :, SEQ:].rearrange("p c (b t) -> p c b t", t=NT)
                    for t in range(NT):
                        ins = v.tensor_tensor(nS[:, :, :, t], nS[:, :, :, t], modT[:, lay, k + 1, :, 1:9], ALU.mult)
                    link(ins)
                    for t in range(NT):
                        ins = v.tensor_tensor(hS[:, :, :, t], nS[:, :, :, t], modT[:, lay, k, :, 1:9], ALU.add)
                    ins.then_inc(s_h_sample, 1)

            def residual(lay, k, src):
                for c in range(DC):
                    y = src(c)
                    ys = small[:, 64 + 32 * (c % 2):96 + 32 * (c % 2)]
                    v.scalar_tensor_tensor(out=xT[:, c, 0:SEQ], in0=y[:, 0:SEQ], scalar=modT[:, lay, k, c, 0:1],
                                           in1=xT[:, c, 0:SEQ], op0=ALU.mult, op1=ALU.add)
                    link(v.tensor_tensor(ys.rearrange("p (b t) -> p b t", t=NT),
                                         y[:, SEQ:NTOK].rearrange("p (b t) -> p b t", t=NT),
                                         modT[:, lay, k, c, 1:9].unsqueeze(2).to_broadcast([128, NB, NT]), ALU.mult))
                    v.tensor_tensor(xT[:, c, SEQ:], xT[:, c, SEQ:], ys, ALU.add).then_inc(s_x_ready, 1)

            modulation(0)
            modulation(1)
            norm(0)
            for ct in range(5):
                v.wait_ge(s_proj_done, ct + 1)
                for t in (0, 2):
                    m = TOK[t][1]
                    src, dst = ps[0:m, 3 * (ct % 2) + t, :], proj[0:m, t, ct * 512:ct * 512 + 512]
                    if ct < 2:
                        for g2 in range(2):
                            ins = v.tensor_copy(dst.rearrange("p (r g d) -> p g r d", r=4, g=2)[:, g2],
                                                src.rearrange("p (g r d) -> p g r d", g=2, r=4)[:, g2])
                    else:
                        ins = v.tensor_copy(dst, src)
                ins.then_inc(s_proj_dve, 1)
            v.wait_ge(s_proj_act, 5)
            v.wait_ge(s_proj_dve, 5)
            tc, ts_ = (C(x).rearrange("p (t n) -> p t n", t=3) for x in ("tcos", "tsin"))
            for grp in range(2):
                for t, (_, m) in enumerate(TOK):
                    if grp == 0:
                        xv = proj[0:m, t, 0:1024].rearrange("p (h d) -> p h d", h=16)
                        x1, x2 = xv[:, :, 0:8], xv[:, :, 8:16]
                        tv = [ropet[0:m, i, 0:128].rearrange("p (h n) -> p h n", n=8) for i in range(4)]
                        co = tc[0:m, t].unsqueeze(1).to_broadcast([m, 16, 8])
                        si = ts_[0:m, t].unsqueeze(1).to_broadcast([m, 16, 8])
                        parts = [(x1, x2, tv, co, si)]
                    else:
                        parts = []
                        for q_, c0 in enumerate((1536, 2048)):
                            xv = proj[0:m, t, c0:c0 + 256].rearrange("p (h d) -> p h d", h=4)
                            tv = [ropet[0:m, i, 32 * q_:32 * q_ + 32].rearrange("p (h n) -> p h n", n=8) for i in range(4)]
                            parts.append((xv[:, :, 0:8], xv[:, :, 8:16], tv,
                                          tc[0:m, t].unsqueeze(1).to_broadcast([m, 4, 8]),
                                          ts_[0:m, t].unsqueeze(1).to_broadcast([m, 4, 8])))
                    for x1, x2, tv, co, si in parts:
                        v.tensor_tensor(tv[0], x1, co, ALU.mult)
                        v.tensor_tensor(tv[1], x2, si, ALU.mult)
                        v.tensor_tensor(tv[2], x2, co, ALU.mult)
                        ins = v.tensor_tensor(tv[3], x1, si, ALU.mult)
                    link(ins)
                    for x1, x2, tv, co, si in parts:
                        v.tensor_tensor(x1, tv[0], tv[1], ALU.subtract)
                        ins = v.tensor_tensor(x2, tv[2], tv[3], ALU.add)
                    ins.then_inc(s_rope_done, 1)
                    v.wait_ge(s_rope_done, 3 * grp + t + 1)
            v.wait_ge(s_gate_exp, 3)
            for t, (_, m) in enumerate(TOK):
                gv = proj[0:m, t, 2560:PROJ]
                link(v.tensor_scalar_add(gv, gv, 1.0))
                link(v.reciprocal(gv, gv))
            v.tensor_copy(gnew[:], proj[0:32, 2, 2560:PROJ])
            v.tensor_copy(vnew[:, 0, :], proj[0:32, 2, 1792:2048])
            v.tensor_copy(vnew[:, 1, :], proj[0:32, 2, 2304:2560]).then_inc(s_vnew_ready, 1)
            for i in range(12):
                v.wait_ge(s_qk_prompt, i + 1)
                if i < 8:
                    gp, r = i // 4, i % 4
                    for g2 in range(2):
                        dst = qbd[64 * g2:64 * g2 + 64].rearrange("p b (g k r t) -> p b g k r t", g=2, k=2, r=4)
                        ins = v.tensor_copy(dst[:, :, gp, g2, r, :],
                                            ps[64 * g2:64 * g2 + 64, i % 6, SEQ:NTOK].rearrange("p (b t) -> p b t", t=NT))
                else:
                    ins = v.tensor_copy(kTn[:, (i - 8) % 2, (i - 8) // 2, :], ps[:, i % 6, SEQ:NTOK])
                ins.then_inc(s_qk_sample, 1)
            v.wait_ge(s_cmp_prompt, 1)
            v.tensor_copy(peb[:], ps[:, 7, 0:2]).then_inc(s_pe_ready, 1)
            v.wait_ge(s_pe_ready, 1)
            for kv in range(2):
                ins = v.tensor_scalar(cmpv[:, kv, 0:16], ps[:, 7, 16 + 16 * kv:32 + 16 * kv], peb[:, kv:kv + 1], None, ALU.add)
            ins.then_inc(s_cmp_copied, 1)
            v.wait_ge(s_cmp_copied, 1)
            v.wait_ge(s_rot_prompt, 1)

            def rope_cmp(n, rot):
                co = C("ckcos")[:, 0:n].unsqueeze(1).to_broadcast([128, 2, n])
                si = C("cksin")[:, 0:n].unsqueeze(1).to_broadcast([128, 2, n])
                v2 = lambda x: x[:, 0:2 * n].rearrange("p (g n) -> p g n", g=2)
                v.tensor_tensor(v2(ckr), v2(cmpv[:, 0]), co, ALU.mult)
                link(v.tensor_tensor(v2(ckt), rot.rearrange("p (g n) -> p g n", g=2), si, ALU.mult))
                return v.tensor_tensor(v2(ckr), v2(ckr), v2(ckt), ALU.add)

            rope_cmp(8, ps[:, 7, 64:80]).then_inc(s_ck_prompt, 1)
            v.tensor_copy(cvn[0:8, 0, :], ps[0:8, 7, 96:352]).then_inc(s_cv_prompt, 1)
            v.wait_ge(s_cv_spread, 1)
            vm = C("vbdmask").rearrange("p (c g) -> p c g", c=8)
            for gp in range(2):
                for g2 in range(2):
                    ins = v.tensor_tensor(Vbd[:, 4 * gp:4 * gp + 4, 64 * g2:64 * g2 + 64],
                                          ps[:, 6, gp * 128 + g2 * 64:gp * 128 + g2 * 64 + 64].unsqueeze(1).to_broadcast([128, 4, 64]),
                                          vm[:, 4 * gp:4 * gp + 4, g2].unsqueeze(2).to_broadcast([128, 4, 64]), ALU.mult)
            ins.then_inc(s_vbd_ready, 1)
            ca, cm = (C(x).rearrange("p (t n) -> p t n", t=2) for x in ("cmpadd", "cmpmul"))
            mxc, smc = small[:, 96:112], small[:, 112:128]
            v.wait_ge(s_cscore_done, 1)
            for t in range(2):
                sc = ScP[:, t, :].rearrange("p (c g n) -> p c g n", c=8, g=2)
                s16 = ScP[:, t, :].rearrange("p (h n) -> p h n", h=16)
                for g2 in range(2):
                    ins = v.tensor_tensor(sc[:, :, g2, :], ps[:, 6 + g2, 256 + 64 * t:320 + 64 * t].rearrange("p (c n) -> p c n", c=8),
                                          ca[:, t].unsqueeze(1).to_broadcast([128, 8, 8]), ALU.add)
                link(ins)
                link(v.tensor_reduce(mxc, s16, AX, ALU.max))
                v.tensor_tensor(s16, s16, mxc.unsqueeze(2).to_broadcast([128, 16, 8]), ALU.subtract).then_inc(s_cscore_shift, 1)
                v.wait_ge(s_cscore_exp, t + 1)
                link(v.tensor_tensor(s16, s16, cm[:, t].unsqueeze(1).to_broadcast([128, 16, 8]), ALU.mult))
                link(v.tensor_reduce(smc, s16, AX, ALU.add))
                link(v.tensor_scalar_max(smc, smc, 1e-30))
                link(v.reciprocal(smc, smc))
                gv = proj[:, t, 2560:PROJ].rearrange("p (g k r b) -> p g k r b", g=2, k=2, r=4)
                for gp in range(2):
                    for k in range(2):
                        mv = smc.rearrange("p (g r k) -> p g r k", g=2, k=2)[:, gp, :, k]
                        ins = v.tensor_tensor(mv, mv, gv[:, gp, k, :, 0], ALU.mult)
                link(ins)
                v.tensor_tensor(s16, s16, smc.unsqueeze(2).to_broadcast([128, 16, 8]), ALU.mult).then_inc(s_cprob_ready, 1)
            v.wait_ge(s_cprob_turned, 1)
            v.tensor_copy(PTc[:], ps[:, 5, 0:256].rearrange("p (t n) -> p t n", t=2)).then_inc(s_cprobT_ready, 1)
            for i in range(35):
                if i < 32:
                    t = i // 16
                    w = 128 * (t + 1)
                    Sv = Ssb[:, i % 3, 0:2 * w].rearrange("p (k n) -> p k n", k=2)
                    mx, nm = small[:, 8 * (i % 3):8 * (i % 3) + 2], small[:, 8 * (i % 3) + 2:8 * (i % 3) + 4]
                    v.wait_ge(s_scores_done, i + 1)
                    if i >= 3:
                        v.wait_ge(s_probs_turned, i - 2)
                    v.tensor_tensor(Sv, ps[:, i % 3, 0:2 * w].rearrange("p (k n) -> p k n", k=2),
                                    C("causal")[:, 256 - w:256].unsqueeze(1).to_broadcast([128, 2, w]), ALU.add
                                    ).then_inc(s_scores_taken, 1)
                    v.wait_ge(s_scores_taken, i + 1)
                    link(v.tensor_reduce(mx, Sv, AX, ALU.max))
                    v.tensor_scalar_mul(nm, mx, -SCALE).then_inc(s_negmax_ready, 1)
                if 1 <= i < 33:
                    u = i - 1
                    t, hh = u // 16, u % 16
                    gp, r, g2 = hh // 8, (hh // 2) % 4, hh % 2
                    w = 128 * (t + 1)
                    Sv = Ssb[:, u % 3, 0:2 * w].rearrange("p (k n) -> p k n", k=2)
                    sm, rg = small[:, 8 * (u % 3) + 4:8 * (u % 3) + 6], small[:, 8 * (u % 3) + 6:8 * (u % 3) + 8]
                    v.wait_ge(s_exp_ready, 2 * (u + 1))
                    link(v.reciprocal(rg, sm))
                    h = gp * 8 + g2 * 4 + r
                    link(v.tensor_tensor(rg, rg, proj[:, t, 2560 + 3 * h + 1:2560 + 3 * h + 3], ALU.mult))
                    v.tensor_tensor(Sv, Sv, rg.unsqueeze(2).to_broadcast([128, 2, w]), ALU.mult).then_inc(s_probs_ready, 1)
                if i >= 3 and (i - 3) % 2 == 1:
                    u = i - 3
                    t, c = u // 16, (u % 16) // 2
                    v.wait_ge(s_pv_done, u + 1)
                    v.tensor_copy(oT[:, c, 128 * t:128 * t + 128], ps[:, 5 + (u // 2) % 2, 0:128]).then_inc(s_o_taken, 1)
            v.wait_ge(s_kv_stored, 1)

            def take(j, dst):
                v.wait_ge(s_bank_turned, j + 1)
                v.tensor_copy(dst, turned(j, dst)).then_inc(s_bank_dve, 1)

            for tau in range(4):
                j = 32 * tau + 1
                for b2 in range(2):
                    b = 2 * tau + b2
                    for h in range(2):
                        for kv in range(2):
                            if b:
                                v.wait_ge(s_cmp_done, b)
                            take(j, TKV[:, kv, 1, 512 * h:512 * h + 512])
                            j += 2
                    v.wait_ge(s_cmp_done, b + 1)
                    for kv in range(2):
                        ins = v.tensor_scalar(cmpv[:, kv, :], ps[:, 6, 64 * kv:64 * kv + 64], peb[:, kv:kv + 1],
                                              None, ALU.add)
                    ins.then_inc(s_craw_ready, 1)
                    v.wait_ge(s_craw_ready, b + 1)
                    v.wait_ge(s_rot_done, b + 1)
                    if b2 == 0 and tau:
                        v.wait_ge(s_group_pv, tau)
                    v.tensor_copy(cvn[:, b2, :], ps[0:32, 6, 256:512])
                    rope_cmp(32, ps[:, 6, 128:192]).then_inc(s_ck_ready, 1)
                for b2 in range(2):
                    b = 2 * tau + b2
                    for h in range(2):
                        if b:
                            v.wait_ge(s_seq_scores, b)
                        take(j, TS[:, 1, 512 * h:512 * h + 512])
                        j += 2
                    if b:
                        v.wait_ge(s_seq_scores, b)
                    take(j, TW[:, 1, :])
                    j += 2
                v.wait_ge(s_gate_rows, tau + 1)
                gt = rank[:, 0, 0:48].rearrange("p (h b) -> p h b", b=3)
                link(v.tensor_tensor(gt, ps[:, 7, 384:432].rearrange("p (h b) -> p h b", b=3),
                                     C("rowhead").unsqueeze(2).to_broadcast([128, 16, 3]), ALU.mult))
                grow = small[:, 44:47]
                link(v.tensor_reduce(grow, gt.rearrange("p h b -> p b h"), AX, ALU.add))
                v.wait_ge(s_group_scores, tau + 1)
                link(v.tensor_copy(s3, ps[:, 3, 0:96]))
                link(v.tensor_reduce(small[:, 32:33], s3[:, 64:96], AX, ALU.max))
                v.tensor_scalar_mul(small[:, 33:34], small[:, 32:33], -SCALE).then_inc(s_cnegmax, 1)
                v.wait_ge(s_cexp_ready, tau + 1)
                link(v.reciprocal(small[:, 35:36], small[:, 34:35]))
                v.tensor_scalar(SS[:, 1600:1632], SS[:, 1600:1632], small[:, 35:36], None, ALU.mult).then_inc(s_cprobs, 1)
                nm_ = C("newmask").rearrange("p (t n) -> p t n", t=4)[:, tau]
                v.tensor_tensor(SS[:, 1056:1568], ps[:, 2, :], C("winmask"), ALU.add)
                link(v.tensor_tensor(SS[:, 1568:1600], s3[:, 32:64], nm_, ALU.add))
                link(v.tensor_reduce(small[:, 37:38], SS[:, 1056:1600], AX, ALU.max))
                v.wait_ge(s_importance, tau + 1)
                sc17 = small[:, 47:64]
                link(v.memset(sc17[:, 16:17], 0.0))
                link(v.tensor_reduce(sc17[:, 0:16], ps[:, 3, 96:128].rearrange("p (n c) -> p n c", c=2), AX, ALU.add))
                link(v.tensor_tensor(sc17, sc17, C("bonus"), ALU.add))
                rk = [rank[:, i, :].rearrange("p (j i) -> p j i", j=17) for i in range(2)]
                si_, sj_ = sc17.unsqueeze(1).to_broadcast([128, 17, 17]), sc17.unsqueeze(2).to_broadcast([128, 17, 17])
                v.tensor_tensor(rk[0], si_, sj_, ALU.is_gt)
                link(v.tensor_tensor(rk[1], si_, sj_, ALU.is_equal))
                link(v.tensor_tensor(rk[1], rk[1], C("before").rearrange("p (j i) -> p j i", j=17), ALU.mult))
                link(v.tensor_tensor(rk[0], rk[0], rk[1], ALU.add))
                out17 = small[:, 96:113]
                link(v.tensor_reduce(out17, rk[0], AX, ALU.add))
                link(v.tensor_scalar(out17, out17, 7.5, -BIG, ALU.is_gt, ALU.mult))
                v.tensor_tensor(SS[:, 0:1024].rearrange("p (j n) -> p j n", j=16),
                                ps[:, 0:2, :].rearrange("p a (j n) -> p (a j) n", n=64),
                                out17[:, 0:16].unsqueeze(2).to_broadcast([128, 16, 64]), ALU.add)
                link(v.scalar_tensor_tensor(out=SS[:, 1024:1056], in0=s3[:, 0:32], scalar=out17[:, 16:17], in1=nm_,
                                            op0=ALU.add, op1=ALU.add))
                link(v.tensor_reduce(small[:, 36:37], SS[:, 0:1056], AX, ALU.max))
                v.tensor_scalar_mul(small[:, 38:40], small[:, 36:38], -SCALE).then_inc(s_snegmax, 1)
                v.tensor_scalar(SS[:, 1600:1632], SS[:, 1600:1632], grow[:, 0:1], None, ALU.mult)
                v.wait_ge(s_sexp_ready, 2 * (tau + 1))
                link(v.reciprocal(small[:, 42:44], small[:, 40:42]))
                link(v.tensor_tensor(small[:, 42:44], small[:, 42:44], grow[:, 1:3], ALU.mult))
                v.tensor_scalar(SS[:, 0:1056], SS[:, 0:1056], small[:, 42:43], None, ALU.mult)
                v.tensor_scalar(SS[:, 1056:1600], SS[:, 1056:1600], small[:, 43:44], None, ALU.mult).then_inc(s_group_probs, 1)
                if tau:
                    v.wait_ge(s_group_pv, tau)
                take(j, PT[:, 4:8, :])
                take(j + 2, PT[0:32, 12:15, :])
                v.wait_ge(s_group_pv, tau + 1)
                for g2 in range(2):
                    for gp in range(2):
                        for b2 in range(2):
                            p_ = slice(64 * g2, 64 * g2 + 64)
                            c0 = b2 * 64 + gp * 32 + g2 * 16
                            t0 = SEQ + (2 * tau + b2) * NT
                            ins = v.tensor_copy(oT[p_, 4 * gp:4 * gp + 4, t0:t0 + NT],
                                                ps[p_, 7, c0:c0 + 16].rearrange("p (r t) -> p r t", t=NT))
                ins.then_inc(s_group_o, 1)

            def from_wo(c):
                v.wait_ge(s_wo_done, c + 1)
                return ps[:, c % 6, :]
            v.wait_ge(s_group_o, 4)
            residual(0, 2, from_wo)
            norm(1)
            for m in range(28):
                v.wait_ge(s_gexp_ready, m + 1)
                t_, g_ = sgF[:, m % 2, 0, :], sgF[:, m % 2, 1, :]
                link(v.tensor_scalar_add(t_, t_, 1.0))
                link(v.reciprocal(t_, t_))
                link(v.tensor_tensor(g_, t_, ps[:, 2 * (m % 3), 0:NTOK], ALU.mult))
                v.tensor_tensor(actF[:, m, :], g_, ps[:, 2 * (m % 3) + 1, 0:NTOK], ALU.mult).then_inc(s_act_ready, 1)

            def from_dn(c):
                v.wait_ge(s_down_done, c // 4 + 1)
                return ps[:, c, :]
            residual(0, 5, from_dn)
            norm(2)
            v.wait_ge(s_down_done, 2)
            link(v.memset(uP[:, :, 0:2], 0.0))
            v.wait_ge(s_state_turned, 1)
            link(v.tensor_copy(uS[:, :, :, 0:2], ps[:, 7, 0:128].rearrange("p (c b j) -> p c b j", c=8, b=8)))
            for c in range(DC):
                B = 12 * (c // 4) + 8 + c % 4
                v.wait_ge(s_conv_done, B + 1)
                v.wait_ge(s_conv_copied, 8 * (c // 4) + 4 + c % 4 + 1)
                v.tensor_tensor(uP[:, c, 2:258], ps[:, B % 6, 0:SEQ], cgT[:, c, 0:SEQ], ALU.mult)
                ins = v.tensor_tensor(uS[:, c, :, 2:6], ps[:, B % 6, SEQ:NTOK].rearrange("p (b t) -> p b t", t=NT),
                                      cgT[:, c, SEQ:].rearrange("p (b t) -> p b t", t=NT), ALU.mult)
                ins.then_inc(s_u_ready, 1)
                v.wait_ge(s_u_ready, c + 1)
                ct_ = ctmp[:, c % 2]
                cS = ct_[:, SEQ:].rearrange("p (b t) -> p b t", t=NT)
                v.tensor_scalar(ct_[:, 0:SEQ], uP[:, c, 0:SEQ], w_convT[:, 0, c:c + 1], None, ALU.mult)
                link(v.tensor_scalar(cS, uS[:, c, :, 0:NT], w_convT[:, 0, c:c + 1], None, ALU.mult))
                for j in (1, 2):
                    v.scalar_tensor_tensor(out=ct_[:, 0:SEQ], in0=uP[:, c, j:j + SEQ], scalar=w_convT[:, j, c:c + 1],
                                           in1=ct_[:, 0:SEQ], op0=ALU.mult, op1=ALU.add)
                    link(v.scalar_tensor_tensor(out=cS, in0=uS[:, c, :, j:j + NT], scalar=w_convT[:, j, c:c + 1],
                                                in1=cS, op0=ALU.mult, op1=ALU.add))
                v.tensor_tensor(zT[:, c, :], ct_, bgT[:, c, :], ALU.mult).then_inc(s_z_ready, 1)
            v.tensor_copy(tail[:, :, 0:2], uP[:, :, 256:258])
            for j in range(2):
                ins = v.tensor_copy(tail[:, :, 2:18].rearrange("p c (b j) -> p c b j", j=2)[:, :, :, j], uS[:, :, :, 4 + j])
            ins.then_inc(s_tail_ready, 1)
            for i in range(2):
                v.wait_ge(s_tail_turned, i + 1)
                v.tensor_copy(tailrow[:, 512 * i:512 * i + 512], ps[0:18, 6 + i, :]).then_inc(s_tail_rows, 1)

            def from_co(c):
                v.wait_ge(s_conv_done, 24 + c + 1)
                return ps[:, (24 + c) % 6, :]
            residual(1, 2, from_co)
            norm(3)
            v.wait_ge(s_logits_done, 1)
            v.wait_ge(s_tail_rows, 2)
            v.wait_ge(s_router_in, 32)
            link(v.memset(lg[:], 0.0))
            v.tensor_tensor(lg[:, 0:2, :], ps[:, 7, 0:16].rearrange("p (t e) -> p t e", t=2),
                            br[:].unsqueeze(1).to_broadcast([128, 2, 8]), ALU.add)
            link(v.tensor_tensor(lg[0:32, 2, :], ps[0:32, 7, 16:24], br[0:32, :], ALU.add))
            bef = C("before").rearrange("p (j i) -> p j i", j=17)[:, 0:8, 0:8]
            for t in range(3):
                li, lj = lg[:, t].unsqueeze(1).to_broadcast([128, 8, 8]), lg[:, t].unsqueeze(2).to_broadcast([128, 8, 8])
                v.tensor_tensor(rkA[:, t], li, lj, ALU.is_gt)
                link(v.tensor_tensor(rkB[:, t], li, lj, ALU.is_equal))
                ins = v.tensor_tensor(rkB[:, t], rkB[:, t], bef, ALU.mult)
            link(ins)
            link(v.tensor_tensor(rkA[:], rkA[:], rkB[:], ALU.add))
            link(v.tensor_reduce(selE, rkA[:], AX, ALU.add))
            link(v.tensor_scalar(selE, selE, 1.5, None, ALU.is_lt))
            v.tensor_tensor(selE, selE, C("valid").unsqueeze(2).to_broadcast([128, 3, 8]), ALU.mult).then_inc(s_sel_ready, 1)
            v.wait_ge(s_sel_ready, 1)
            link(v.tensor_reduce(mE[:, 0:3], lg[:], AX, ALU.max))
            v.tensor_tensor(lg[:], lg[:], mE[:, 0:3].unsqueeze(2).to_broadcast([128, 3, 8]), ALU.subtract).then_inc(s_logits_shift, 1)
            v.wait_ge(s_logits_exp, 1)
            link(v.tensor_tensor(cw, lg[:], selE, ALU.mult))
            link(v.tensor_reduce(mE[:, 4:7], cw, AX, ALU.add))
            link(v.tensor_scalar_max(mE[:, 4:7], mE[:, 4:7], 1e-30))
            link(v.reciprocal(mE[:, 8:11], mE[:, 4:7]))
            link(v.tensor_tensor(cw, cw, mE[:, 8:11].unsqueeze(2).to_broadcast([128, 3, 8]), ALU.mult))
            v.wait_ge(s_pos_done, 1)
            v.tensor_copy(pos, ps[:, 7, 32:56].rearrange("p (t e) -> p t e", t=3))
            link(v.tensor_reduce(mE[:, 12:13], ps[:, 7, 56:64], AX, ALU.max))
            v.tensor_copy(cnti[:], mE[0:1, 12:13]).then_inc(s_count_ready, 1)
            for i in range(6):
                v.wait_ge(s_rows_done, i + 1)
                t, h = i // 2, i % 2
                m = TOK[t][1]
                v.tensor_copy(hN[0:m, t, 512 * h:512 * h + 512], ps[0:m, i, :]).then_inc(s_rows_taken, 1)
            link(v.memset(yacc[:], 0.0))

            LN = [0]

            def experts(rnd):
                with v.Fori(0, NE) as e0:
                    e = e0 + NE * rnd
                    K = 3 + 7 * 3
                    n = [0]

                    def mlink(ins):
                        ins.then_inc(s_moe_chain, 1)
                        n[0] += 1
                        v.wait_ge(s_moe_chain, e * K + n[0])
                    for i, src in enumerate((pos, selE, cw)):
                        ins = v.tensor_copy(cur[:, i, 0:3], src[:, :, bass.ds(e0, 1)].rearrange("p t o -> p (t o)"))
                    mlink(ins)
                    if rnd:
                        mlink(v.tensor_scalar_add(cur[:, 0, 0:3], cur[:, 0, 0:3], -float(SLOTS_E * rnd)))
                    else:
                        mlink(v.tensor_scalar_add(cur[:, 0, 0:3], cur[:, 0, 0:3], 0.0))
                    for t in range(3):
                        ins = v.tensor_scalar(Dm[:, t, :], C("iota"), cur[:, 0, t:t + 1], cur[:, 1, t:t + 1],
                                              ALU.is_equal, ALU.mult)
                    mlink(ins)
                    for t in range(3):
                        ins = v.tensor_scalar(Dw[:, t, :], Dm[:, t, :], cur[:, 2, t:t + 1], None, ALU.mult)
                    ins.then_inc(s_gather_ready, 1)
                    v.wait_ge(s_gathered, e * 3 + 2)
                    v.tensor_copy(XT[:, 4:8, :], ps[:, 5, :].rearrange("p (c s) -> p c s", c=4)).then_inc(s_xt_dve, 1)
                    v.wait_ge(s_gathered, e * 3 + 3)
                    v.tensor_copy(DT, ps[:, 6, 0:NTOK]).then_inc(s_scatter_ready, 1)
                    for j in range(7):
                        v.wait_ge(s_eexp_ready, e * 7 + (j + 1))
                        mlink(v.tensor_scalar_add(rM, eM, 1.0))
                        mlink(v.reciprocal(rM, rM))
                        mlink(v.tensor_tensor(rM, rM, ps[:, 2 * (j % 2), :], ALU.mult))
                        if j >= 2:
                            v.wait_ge(s_eact_turned, e * 7 + (j - 1))
                        v.tensor_tensor(actM[:, j % 2, :], rM, ps[:, 2 * (j % 2) + 1, :], ALU.mult).then_inc(s_eact_ready, 1)
                    assert n[0] == K
                    v.wait_ge(s_y_done, e + 1)
                    v.tensor_copy(ysb[:, 512:1024], ps[:, 7, :]).then_inc(s_y_dve, 1)
                    for c in range(DC):
                        v.wait_ge(s_share_done, e * 8 + (c + 1))
                        v.tensor_tensor(yacc[:, c, :], yacc[:, c, :], ps[:, c % 4, 0:NTOK], ALU.add).then_inc(s_share_added, 1)
                    v.wait_ge(s_share_added, e * 8 + 8)

            experts(0)
            c_ = v.value_load(cnti[0:1, 0:1], min_val=0, max_val=NTOK)
            for rnd in (1, 2):
                with v.If(c_ > SLOTS_E * rnd):
                    experts(rnd)
            residual(1, 5, lambda c: yacc[:, c, :])
            norm(4)
            for c in range(DC):
                ins = v.tensor_scalar(nT[:, c, :], nT[:, c, :], g_finT[:, c:c + 1], None, ALU.mult)
            ins.then_inc(s_final_ready, 1)
            for i in range(6):
                v.wait_ge(s_rows_done, 6 + i + 1)
                t, h = i // 2, i % 2
                m = TOK[t][1]
                v.tensor_copy(outN[0:m, t, 512 * h:512 * h + 512], ps[0:m, i, :]).then_inc(s_final_rows, 1)

        @block.tensor
        def _(pe):
            ident = C("ident")

            def mm(out, l, r, k, n, **kw):
                return pe.matmul(out, l, r, start=(k == 0), stop=(k == n - 1), **kw)

            used = Count(s_used)

            pe.wait_ge(s_consts_in, 16)
            pe.wait_ge(s_rows_in, 16 * 9)
            pe.wait_ge(s_csilu, 1)
            pe.transpose(ps[:, 7, 0:96], rowsA, ident[0:96, 0:96])
            pe.transpose(ps[:, 7, 96:160], rowsB, ident[0:64, 0:64])
            pe.transpose(ps[:, 7, 160:232], rowsC, ident[0:72, 0:72])
            pe.transpose(ps[:, 7, 232:264], rowsP[:, 0:128], ident[0:32, 0:32])
            pe.transpose(ps[:, 7, 264:296], rowsP[:, 128:256], ident[0:32, 0:32]).then_inc(s_rows_turned, 1)
            pe.wait_ge(s_x_in, 32)
            for c in range(DC):
                if c >= 4:
                    pe.wait_ge(s_x_ready, c - 3)
                for t, (t0, m) in enumerate(TOK):
                    ins = pe.transpose(ps[:, 2 + c % 4, t0:t0 + m], xrow[0:m, t, 128 * c:128 * c + 128], ident[0:m, 0:m])
                ins.then_inc(s_x_turned, 1)
            pe.wait_ge(s_rowsT_ready, 1)
            for k in range(24):
                n = 2 * k
                wait_tile(pe, n)
                wait_tile(pe, n + 1)
                for b in range(4):
                    o = ((k % 12) * 4 + b) * 9
                    for kc in range(8):
                        ins = mm(ps[:, k // 12, o:o + 9], slot(n + kc // 4)[:, kc % 4, 128 * b:128 * b + 128],
                                 csT[:, :, kc], kc, 8)
                        if b == 3 and kc % 4 == 3:
                            ins.then_inc(s_used, 1)
                if k % 12 == 11:
                    pe.wait_ge(s_used, n + 2)
                    pe.sem_inc(s_ada_done, 1)

            def norm(n):
                for c in range(DC):
                    if n and c == 0:
                        pe.wait_ge(s_std_ready, n)
                    pe.wait_ge(s_sq_ready, 8 * n + c + 1)
                    ins = mm(ps[:, 6, 0:NTOK], C("ones"), nT[:, c, :], c, DC)
                ins.then_inc(s_ss_done, 1)

            def h_ready(n):
                pe.wait_ge(s_h_prompt, 8 * (n + 1))
                pe.wait_ge(s_h_sample, n + 1)

            norm(0)
            h_ready(0)
            pe.wait_ge(s_mod_ready, 2)
            for ct in range(6):
                n = T_NSA + 2 * ct
                last = ct == 5
                wait_tile(pe, n)
                if not last:
                    wait_tile(pe, n + 1)
                if ct >= 2:
                    pe.wait_ge(s_proj_dve, ct - 1)
                    pe.wait_ge(s_proj_act, ct - 1)
                for t, (t0, m) in enumerate(TOK):
                    for kc in range(8):
                        if last:
                            rhs, out = slot(n, 8)[:, kc, :], ps[0:m, 3 + t, 0:48]
                        else:
                            rhs, out = slot(n + kc // 4)[:, kc % 4, :], ps[0:m, 3 * (ct % 2) + t, :]
                        ins = mm(out, hT[:, kc, t0:t0 + m], rhs, kc, 8)
                        if t == 2 and kc == 3 and not last:
                            ins.then_inc(s_used, 1)
                ins.then_inc(s_proj_done, 1)
                pe.wait_ge(s_proj_done, ct + 1)
                pe.sem_inc(s_used, 1)
            cols = [128 * i for i in range(8)] + [1536, 1664, 2048, 2176, 1024, 1152, 1280, 1408]
            pe.wait_ge(s_rope_done, 6)
            pe.wait_ge(s_gate_exp, 3)
            for i, c0 in enumerate(cols):
                if i >= 6:
                    pe.wait_ge(s_qk_prompt, i - 5)
                    pe.wait_ge(s_qk_sample, min(i - 5, 12))
                for t, (t0, m) in enumerate(TOK if i < 12 else TOK[:2]):
                    ins = pe.transpose(ps[:, i % 6, t0:t0 + m], proj[0:m, t, c0:c0 + 128], ident[0:m, 0:m])
                ins.then_inc(s_qk_turned, 1)
            pe.wait_ge(s_wbd_in, 64)
            for kv in range(2):
                for l in range(32):
                    ins = mm(ps[:, 7, kv:kv + 1], wbd[:, kv, l, :], peT[:, kv, l:l + 1], l, 32)
            pe.wait_ge(s_qk_prompt, 16)
            for kv in range(2):
                src = cTp[:, kv].rearrange("p g (n l) -> p g n l", l=32)
                for l in range(32):
                    ins = mm(ps[:, 7, 16 + 16 * kv:32 + 16 * kv], wbd[:, kv, l, :], src[:, :, :, l], l, 32)
            ins.then_inc(s_cmp_prompt, 1)
            pe.wait_ge(s_cmp_copied, 1)
            for gp in range(2):
                pe.transpose(ps[0:8, 7, 96 + 128 * gp:224 + 128 * gp], cmpv[:, 1, 8 * gp:8 * gp + 8], ident)
            mm(ps[:, 7, 64:80], C("rot"), cmpv[:, 0, 0:16], 0, 1).then_inc(s_rot_prompt, 1)
            pe.wait_ge(s_cv_prompt, 1)
            mm(ps[:, 6, 0:256], C("repn", 8), cvn[0:8, 0, :], 0, 1).then_inc(s_cv_spread, 1)
            pe.wait_ge(s_ck_prompt, 1)
            pe.wait_ge(s_vbd_ready, 1)
            for t in range(2):
                for hh in range(16):
                    c, g2 = hh // 2, hh % 2
                    p_ = slice(64 * g2, 64 * g2 + 64)
                    o = 256 + 64 * t + 8 * c
                    ins = mm(ps[:, 6 + g2, o:o + 8], qT[p_, c, 128 * t:128 * t + 128],
                             ckr[p_, 8 * (c // 4):8 * (c // 4) + 8], 0, 1)
            ins.then_inc(s_cscore_done, 1)
            for t in range(2):
                pe.wait_ge(s_cprob_ready, t + 1)
                ins = pe.transpose(ps[:, 5, 128 * t:128 * t + 128], ScP[:, t, :], ident)
            ins.then_inc(s_cprob_turned, 1)
            pe.wait_ge(s_cprobT_ready, 1)
            for i in range(35):
                if i < 32:
                    t, hh = i // 16, i % 16
                    c, g2 = hh // 2, hh % 2
                    p_ = slice(64 * g2, 64 * g2 + 64)
                    w = 128 * (t + 1)
                    if i >= 3:
                        pe.wait_ge(s_scores_taken, i - 2)
                    mm(ps[:, i % 3, 0:2 * w], qT[p_, c, 128 * t:128 * t + 128], kTp[p_, c // 4, :, 0:w], 0, 1
                       ).then_inc(s_scores_done, 1)
                if 2 <= i < 34:
                    u = i - 2
                    w = 128 * (u // 16 + 1)
                    pe.wait_ge(s_probs_ready, u + 1)
                    if u >= 2:
                        pe.wait_ge(s_probsT_ready, u - 1)
                    for k in range(2 * w // 128):
                        ins = pe.transpose(ps[:, 3 + u % 2, 128 * k:128 * k + 128],
                                           Ssb[:, u % 3, 128 * k:128 * k + 128], ident)
                    ins.then_inc(s_probs_turned, 1)
                if i >= 3:
                    u = i - 3
                    t, hh = u // 16, u % 16
                    c, g2 = hh // 2, hh % 2
                    bank = 5 + (u // 2) % 2
                    pe.wait_ge(s_probsT_ready, u + 1)
                    if g2 == 0:
                        if u >= 4:
                            pe.wait_ge(s_o_taken, u // 2 - 1)
                        pe.matmul(ps[:, bank, 0:128], Vbd[:, c, :], PTc[:, t, :], start=True, stop=False,
                                  skip_group_check=True)
                    g_ = 2 * (c // 4) + g2
                    for k in range(2):
                        for kt in range(t + 1):
                            c0 = (1792, 2304)[k] + 64 * g_
                            ins = pe.matmul(ps[64 * g2:64 * g2 + 64, bank, 0:128], proj[:, kt, c0:c0 + 64],
                                            PTs[:, u % 2, (k * (t + 1) + kt) * 128:(k * (t + 1) + kt) * 128 + 128],
                                            start=False, stop=(k == 1 and kt == t), skip_group_check=True)
                    ins.then_inc(s_pv_done, 1)
            pe.wait_ge(s_o_taken, 16)
            pe.wait_ge(s_vnew_ready, 1)
            jb = [0]

            def bank_free():
                j = jb[0]
                if j >= 2:
                    pe.wait_ge(s_bank_act if j % 2 == 0 else s_bank_dve, j // 2)
                jb[0] += 1
                return 4 + j % 2

            def copied(j):
                pe.wait_ge(s_bank_act, (j + 1) // 2)
                pe.wait_ge(s_bank_dve, j // 2)

            for tau in range(4):
                T0 = T_CACHE + 10 * tau
                for b2 in range(2):
                    b = 2 * tau + b2
                    for h in range(2):
                        n = T0 + 2 * b2 + h
                        wait_tile(pe, n)
                        for kv in range(2):
                            for gp in range(2):
                                bk = bank_free()
                                for j in range(4):
                                    c0 = kv * 256 + gp * 128
                                    ins = pe.transpose(ps[:, bk, 128 * j:128 * j + 128], slot(n)[:, j, c0:c0 + 128], ident)
                                ins.then_inc(s_bank_turned, 1)
                        pe.wait_ge(s_bank_turned, jb[0])
                        pe.sem_inc(s_used, 1)
                    copied(jb[0])
                    if b:
                        pe.wait_ge(s_ck_ready, b)
                    for kv in range(2):
                        src = TKV[:, kv].rearrange("p g (n l) -> p g n l", l=32)
                        for l in range(32):
                            ins = mm(ps[:, 6, 64 * kv:64 * kv + 64], wbd[:, kv, l, :], src[:, :, :, l], l, 32)
                    ins.then_inc(s_cmp_done, 1)
                    pe.wait_ge(s_craw_ready, b + 1)
                    for gp in range(2):
                        pe.transpose(ps[0:32, 6, 256 + 128 * gp:384 + 128 * gp], cmpv[:, 1, 32 * gp:32 * gp + 32], ident)
                    mm(ps[:, 6, 128:192], C("rot"), cmpv[:, 0, :], 0, 1).then_inc(s_rot_done, 1)
                    pe.wait_ge(s_ck_ready, b + 1)
                    if tau and b2 == 0:
                        pe.wait_ge(s_group_probs, tau)
                        pe.wait_ge(s_group_o, tau)
                    for gp in range(2):
                        st = 2 * b2 + gp
                        o_ = slice(32 * st, 32 * st + 32)
                        q_ = qbd[:, b, 32 * gp:32 * gp + 32]
                        mm(ps[o_, 3, 64:96], q_, ckr[:, 32 * gp:32 * gp + 32], 0, 1)
                        mm(ps[o_, 3, 0:32], q_, kTn[:, gp, 0, :], 0, 1)
                        ins = mm(ps[o_, 3, 32:64], q_, kTn[:, gp, 1, :], 0, 1)
                mm(ps[:, 7, 384:432], C("rowtok", 32)[:, 128 * tau:128 * tau + 128], gnew[:], 0, 1).then_inc(s_gate_rows, 1)
                for b2 in range(2):
                    b = 2 * tau + b2
                    n = T0 + 4 + 3 * b2
                    for h in range(3):
                        wait_tile(pe, n + h)
                        for gp in range(2):
                            bk = bank_free()
                            for j in range(4):
                                ins = pe.transpose(ps[:, bk, 128 * j:128 * j + 128],
                                                   slot(n + h)[:, j, 128 * gp:128 * gp + 128], ident)
                            ins.then_inc(s_bank_turned, 1)
                    copied(jb[0])
                    for gp in range(2):
                        st = 2 * b2 + gp
                        o_ = slice(32 * st, 32 * st + 32)
                        q_ = qbd[:, b, 32 * gp:32 * gp + 32]
                        mm(ps[o_, 0, :], q_, TS[:, gp, 0:512], 0, 1)
                        mm(ps[o_, 1, :], q_, TS[:, gp, 512:1024], 0, 1)
                        ins = mm(ps[o_, 2, :], q_, TW[:, gp, :], 0, 1)
                    ins.then_inc(s_seq_scores, 1)
                pe.wait_ge(s_seq_scores, 2 * tau + 2)
                pe.sem_inc(s_group_scores, 1)
                pe.wait_ge(s_cprobs, tau + 1)
                mm(ps[:, 3, 96:128], C("headsum"), SS[:, 1600:1632], 0, 1).then_inc(s_importance, 1)
                pe.wait_ge(s_group_probs, tau + 1)
                for i, (k0, nk) in enumerate(((0, 4), (4, 4), (8, 4))):
                    bk = bank_free()
                    for k in range(nk):
                        c0 = (0, 512, 1056)[i] + 128 * k
                        ins = pe.transpose(ps[:, bk, 128 * k:128 * k + 128], SS[:, c0:c0 + 128], ident)
                    ins.then_inc(s_bank_turned, 1)
                bk = bank_free()
                for k, c0 in enumerate((1024, 1568, 1600)):
                    ins = pe.transpose(ps[0:32, bk, 128 * k:128 * k + 128], SS[:, c0:c0 + 32], ident)
                ins.then_inc(s_bank_turned, 1)
                copied(jb[0])
                if tau:
                    pe.wait_ge(s_group_o, tau)
                for st in range(4):
                    b2, gp = st // 2, st % 2
                    o = ps[:, 7, 32 * st:32 * st + 32]
                    m_ = slice(32 * st, 32 * st + 32)
                    n = T0 + 4 + 3 * b2
                    c0 = 256 + 128 * gp
                    for k in range(12):
                        mm(o, slot(n + k // 4)[:, k % 4, c0:c0 + 128], PT[:, k, m_], k, 15)
                    mm(o, vnew[:, 0, 128 * gp:128 * gp + 128], PT[0:32, 12, m_], 12, 15)
                    mm(o, vnew[:, 1, 128 * gp:128 * gp + 128], PT[0:32, 13, m_], 13, 15)
                    ins = mm(o, cvn[:, b2, 128 * gp:128 * gp + 128], PT[0:32, 14, m_], 14, 15)
                ins.then_inc(s_group_pv, 1)
                pe.wait_ge(s_group_pv, tau + 1)
                pe.sem_inc(s_used, 6)
            pe.wait_ge(s_group_o, 4)

            def dense(n, mov, out, done, ntile=2):
                wait_tile(pe, n)
                wait_tile(pe, n + 1)
                for b in range(4):
                    o = out(b)
                    for kc in range(8):
                        ins = mm(o, slot(n + kc // 4)[:, kc % 4, 128 * b:128 * b + 128], mov(kc), kc, 8)
                        if b == 3 and kc == 3:
                            ins.then_inc(s_used, 1)
                    ins.then_inc(done, 1)
                    nd[done] = nd.get(done, 0) + 1
                pe.wait_ge(done, nd[done])
                pe.sem_inc(s_used, 1)

            nd = {}

            def wo_bank(ch):
                def f(b):
                    c = 4 * ch + b
                    if c >= 6:
                        pe.wait_ge(s_x_ready, 8 + c - 5)
                    return ps[:, c % 6, 0:NTOK]
                return f
            for ch in range(2):
                dense(T_WO + 2 * ch, lambda kc: oT[:, kc, :], wo_bank(ch), s_wo_done)
            norm(1)
            h_ready(1)
            for j in range(7):
                n = T_FU + 4 * j
                for i in range(4):
                    wait_tile(pe, n + i)
                for b in range(4):
                    m = 4 * j + b
                    if m >= 3:
                        pe.wait_ge(s_act_ready, m - 2)
                    for u in range(2):
                        for kc in range(8):
                            ins = mm(ps[:, 2 * (m % 3) + u, 0:NTOK],
                                     slot(n + 2 * u + kc // 4)[:, kc % 4, 128 * b:128 * b + 128], hT[:, kc, :], kc, 8)
                            if b == 3 and kc % 4 == 3 and (u, kc) != (1, 7):
                                ins.then_inc(s_used, 1)
                    ins.then_inc(s_gu_done, 1)
                pe.wait_ge(s_gu_done, 4 * j + 4)
                pe.sem_inc(s_used, 1)
            pe.wait_ge(s_act_ready, 28)
            for ch in range(2):
                for i in range(7):
                    n = T_FD + 7 * ch + i
                    wait_tile(pe, n)
                    for kc in range(4):
                        m = 4 * i + kc
                        for b in range(4):
                            ins = mm(ps[:, 4 * ch + b, 0:NTOK], slot(n)[:, kc, 128 * b:128 * b + 128], actF[:, m, :], m, 28)
                    if i < 6:
                        ins.then_inc(s_used, 1)
                    else:
                        ins.then_inc(s_down_done, 1)
                        pe.wait_ge(s_down_done, ch + 1)
                        pe.sem_inc(s_used, 1)
            pe.wait_ge(s_x_ready, 24)
            norm(2)
            h_ready(2)
            pe.wait_ge(s_state_in, 16)
            for c in range(DC):
                ins = pe.transpose(ps[:, 7, 16 * c:16 * c + 16], strow[:, 128 * c:128 * c + 128], ident[0:16, 0:16])
            ins.then_inc(s_state_turned, 1)

            def ci_bank(B0):
                def f(b):
                    B = B0 + b
                    if B >= 6:
                        q = B - 6
                        if q >= 24:
                            pe.wait_ge(s_x_ready, 24 + q - 24 + 1)
                        elif (q // 4) % 3 < 2:
                            pe.wait_ge(s_conv_copied, 8 * (q // 12) + 4 * ((q // 4) % 3) + q % 4 + 1)
                        else:
                            pe.wait_ge(s_u_ready, 4 * (q // 12) + q % 4 + 1)
                    return ps[:, B % 6, 0:NTOK]
                return f
            for k in range(6):
                dense(T_CI + 2 * k, lambda kc: hT[:, kc, :], ci_bank(4 * k), s_conv_done)
            pe.wait_ge(s_z_ready, 8)
            dense(T_CO, lambda kc: zT[:, kc, :], ci_bank(24), s_conv_done)
            pe.wait_ge(s_tail_ready, 1)
            for c in range(DC):
                ins = pe.transpose(ps[0:18, 6 + c // 4, 128 * (c % 4):128 * (c % 4) + 128], tail[:, c, :], ident)
                if c % 4 == 3:
                    ins.then_inc(s_tail_turned, 1)
            dense(T_CO + 2, lambda kc: zT[:, kc, :], ci_bank(28), s_conv_done)
            pe.wait_ge(s_tail_rows, 2)
            norm(3)
            h_ready(3)
            pe.wait_ge(s_router_in, 32)
            for t, (t0, m) in enumerate(TOK):
                for kc in range(DC):
                    ins = mm(ps[0:m, 7, 8 * t:8 * t + 8], hT[:, kc, t0:t0 + m], wr[:, kc, :], kc, DC)
            ins.then_inc(s_logits_done, 1)

            def to_tokens(src, base):
                for i in range(6):
                    t, h = i // 2, i % 2
                    t0, m = TOK[t]
                    for q in range(4):
                        ins = pe.transpose(ps[0:m, i, 128 * q:128 * q + 128], src[:, 4 * h + q, t0:t0 + m], ident)
                    ins.then_inc(s_rows_done, 1)
            pe.wait_ge(s_x_ready, 32)
            to_tokens(hT, 0)
            pe.wait_ge(s_sel_ready, 1)
            for t in range(3):
                for k in range(t):
                    mm(ps[:, 7, 32 + 8 * t:40 + 8 * t], C("ones"), selE[:, k, :], k, t + 1)
                mm(ps[:, 7, 32 + 8 * t:40 + 8 * t], C("earlier"), selE[:, t, :], t, t + 1)
            for t in range(3):
                ins = mm(ps[:, 7, 56:64], C("ones"), selE[:, t, :], t, 3)
            ins.then_inc(s_pos_done, 1)
            pe.wait_ge(s_rows_taken, 6)
            pe.wait_ge(s_count_ready, 1)

            def experts(rnd):
                with pe.Fori(0, NE) as e0:
                    e = e0 + NE * rnd

                    def tile_wait(i):
                        q = (T_MOE + i) % RING
                        pe.wait_ge(s_slot[q], e * (16 * TILES_E // RING) + (total[q] + 16 * (i // RING + 1)))
                    pe.wait_ge(s_gather_ready, e + 1)
                    for h in range(2):
                        for c in range(4 * h, 4 * h + 4):
                            for t, (_, m) in enumerate(TOK):
                                ins = mm(ps[:, 4 + h, 128 * (c % 4):128 * (c % 4) + 128],
                                         hN[0:m, t, 128 * c:128 * c + 128], Dm[0:m, t, :], t, 3)
                        ins.then_inc(s_gathered, 1)
                    for t, (t0, m) in enumerate(TOK):
                        ins = pe.transpose(ps[:, 6, t0:t0 + m], Dw[0:m, t, :], ident[0:m, 0:m])
                    ins.then_inc(s_gathered, 1)
                    pe.wait_ge(s_xt_act, e + 1)
                    pe.wait_ge(s_xt_dve, e + 1)

                    def turn(j):
                        pe.wait_ge(s_eact_ready, e * 7 + (j + 1))
                        if j >= 2:
                            pe.wait_ge(s_eactT_ready, e * 7 + (j - 1))
                        for q in range(4):
                            ins = pe.transpose(ps[:, 4 + j % 2, 128 * q:128 * q + 128],
                                               actM[:, j % 2, 128 * q:128 * q + 128], ident)
                        ins.then_inc(s_eact_turned, 1)
                    for j in range(7):
                        if j >= 2:
                            pe.wait_ge(s_eact_ready, e * 7 + (j - 1))
                        for u in range(2):
                            for kc in range(8):
                                i = 4 * j + 2 * u + kc // 4
                                if kc % 4 == 0:
                                    tile_wait(i)
                                ins = mm(ps[:, 2 * (j % 2) + u, :], XT[:, kc, :], slot(T_MOE + i)[:, kc % 4, :], kc, 8)
                                if kc % 4 == 3 and (u, kc) != (1, 7):
                                    ins.then_inc(s_used, 1)
                        ins.then_inc(s_up_done, 1)
                        pe.wait_ge(s_up_done, e * 7 + (j + 1))
                        pe.sem_inc(s_used, 1)
                        if j:
                            turn(j - 1)
                    pe.wait_ge(s_scatter_ready, e + 1)
                    for i in range(14):
                        if i == 4:
                            turn(6)
                        tile_wait(28 + i)
                        w = ring[:, (T_MOE + 28 + i) % RING, :].rearrange("p (k n) -> p k n", k=2)
                        for kk in range(2):
                            k = 2 * i + kk
                            if k % 4 == 0:
                                pe.wait_ge(s_eactT_ready, e * 7 + (k // 4 + 1))
                            for h in range(2):
                                ins = mm(ps[:, 6 + h, :], actT[:, k, :], w[:, kk, 512 * h:512 * h + 512], k, 28)
                        if i < 13:
                            ins.then_inc(s_used, 1)
                    ins.then_inc(s_y_done, 1)
                    pe.wait_ge(s_y_done, e + 1)
                    pe.sem_inc(s_used, 1)
                    pe.wait_ge(s_y_act, e + 1)
                    pe.wait_ge(s_y_dve, e + 1)
                    for c in range(DC):
                        if c >= 4:
                            pe.wait_ge(s_share_added, e * 8 + (c - 3))
                        mm(ps[:, c % 4, 0:NTOK], ysb[:, 128 * c:128 * c + 128], DT, 0, 1).then_inc(s_share_done, 1)
                    pe.wait_ge(s_share_added, e * 8 + 8)

            experts(0)
            c_ = pe.value_load(cnti[0:1, 0:1], min_val=0, max_val=NTOK)
            for rnd in (1, 2):
                with pe.If(c_ > SLOTS_E * rnd):
                    experts(rnd)
            norm(4)
            pe.wait_ge(s_final_ready, 1)
            to_tokens(nT, 6)


def constants():
    import numpy as np
    t = {n: np.zeros((128, w), np.float32) for n, w in CONSTS}
    p = np.arange(128)
    t["ident"][:] = np.eye(128)
    t["causal"][:, 128:] = np.where(p[None, :] <= p[:, None], 0.0, -BIG)
    d = p % 64
    for q in range(128):
        if d[q] < 8:
            t["rot"][q + 8, q] = -1.0
        elif d[q] < 16:
            t["rot"][q - 8, q] = 1.0
    inv = (1.0 / (np.float32(500000.0) ** (np.arange(8, dtype=np.float32) * np.float32(2.0 / 16)))).astype(np.float32)
    cend = (np.arange(32) * 32 + 31).astype(np.float32)
    ang = (cend[:, None] * inv[None, :]).astype(np.float32)
    for q in range(128):
        if d[q] < 16:
            t["ckcos"][q] = np.cos(ang[:, d[q] % 8])
            t["cksin"][q] = np.sin(ang[:, d[q] % 8])
        else:
            t["ckcos"][q] = 1.0
    posn = np.stack([p, 128 + p, 1024 + p % 4], 1).astype(np.float32)
    ang = (posn[:, :, None] * inv).astype(np.float32)
    t["tcos"][:] = np.cos(ang).reshape(128, 24)
    t["tsin"][:] = np.sin(ang).reshape(128, 24)
    ce = np.arange(8) * 32 + 31
    for k in range(2):
        vis = ce[None, :] <= (128 * k + p)[:, None]
        t["cmpadd"][:, 8 * k:8 * k + 8] = np.where(vis, 0.0, -BIG)
        t["cmpmul"][:, 8 * k:8 * k + 8] = vis
    b2, gp, g2, r, tt = p // 64, (p // 32) % 2, (p // 16) % 2, (p // 4) % 4, p % 4
    key = (b2 * 2 + gp) * 8 + g2 * 4 + tt
    t["headsum"][:] = key[:, None] == key[None, :]
    t["bonus"][:, 0] = 5.0
    t["bonus"][:, 16] = 5.0
    t["winmask"][:] = np.where(np.arange(512)[None, :] >= tt[:, None], 0.0, -BIG)
    n = np.arange(32)
    for tau in range(4):
        ok = (n[None, :] // 4 == (2 * tau + b2)[:, None]) & (n[None, :] % 4 <= tt[:, None])
        t["newmask"][:, 32 * tau:32 * tau + 32] = np.where(ok, 0.0, -BIG)
        t["rowtok"][0:32, 128 * tau:128 * tau + 128] = n[:, None] == ((2 * tau + b2) * 4 + tt)[None, :]
    t["rowhead"][:] = np.arange(16)[None, :] == (gp * 8 + g2 * 4 + r)[:, None]
    j = np.arange(17)
    t["before"][:] = (j[None, :] < j[:, None]).reshape(1, 289)
    t["repn"][0:8, :] = np.arange(8)[:, None] == (p % 8)[None, :]
    for c in range(8):
        for g in range(2):
            t["vbdmask"][:, 2 * c + g] = (p // 8) == (2 * c + g)
    t["earlier"][:] = p[:, None] < p[None, :]
    t["ones"][:] = 1.0
    t["iota"][:] = p[None, :]
    t["valid"][:, 0:2] = 1.0
    t["valid"][0:32, 2] = 1.0
    t["eps"][:] = EPS
    return np.concatenate([t[n] for n, _ in CONSTS], 1)


_INS = ["x_prompt", "x_sample", "cache_cmp_kv", "cache_sel_kv", "cache_win_kv", "state_conv", "page_table", "c_prompt",
        "c_sample", "w_ada", "b_ada", "g_norm_mix", "g_norm_ffn", "g_norm_final", "w_nsa_in", "w_nsa_out", "w_cmp_k",
        "pe_cmp_k", "w_cmp_v", "pe_cmp_v", "w_conv_in", "w_conv", "w_conv_out", "w_ff_gu", "w_ff_down", "w_router",
        "b_router", "w_moe_gu", "w_moe_down"]
_OUTS = [(1, 256, 1024), (8, 4, 1024), (1, 1, 256, 2, 4, 64), (1, 8, 4, 2, 4, 64), (1, 1, 256, 2, 4, 64),
         (1, 8, 4, 2, 4, 64), (1, 1, 256, 2, 4, 64), (1, 8, 512, 2, 4, 64), (1, 1, 2, 1024), (1, 8, 2, 1024)]


def kernel(**inputs):
    import numpy as _np
    import concourse.bacc as _bacc
    from concourse.bass_utils import run_bass_kernel_spmd as _run

    nc = _bacc.Bacc("TRN2", target_bir_lowering=False, num_devices=1)
    arrays, A = {}, {}
    for name in _INS + ["consts"]:
        a = constants() if name == "consts" else _np.ascontiguousarray(inputs[name])
        arrays[f"in_{name}"] = a
        A[name] = nc.dram_tensor(f"in_{name}", a.shape, mybir.dt.from_np(a.dtype), kind="ExternalInput").ap()
    O = [nc.dram_tensor(f"out_{i}", sh, F32, kind="ExternalOutput").ap() for i, sh in enumerate(_OUTS)]
    trunk(nc, A, O)
    r = _run(nc, [arrays], core_ids=[0])
    return tuple(r.results[0][f"out_{i}"] for i in range(len(_OUTS)))
```

```python
from contextlib import ExitStack

import concourse.bass as bass
from concourse import mybir

F32 = mybir.dt.float32
F32R = mybir.dt.float32r
I32 = mybir.dt.int32
ALU = mybir.AluOpType
ACT = mybir.ActivationFunctionType
AX = mybir.AxisListType.X

D = 1024
DC = D // 128
SEQ = 256
NB, NT = 8, 4
NTOK = SEQ + NB * NT
HD = 64
FF = 3584
NE = 8
KVW = 256
PROJ = 2560
TAIL = 544
SCALE = HD ** -0.5
BIG = 1.0e30
EPS = 1e-6
RING = 7
SLOT = 2048
SLOTS_E = 128
TILES_E = 42
SPLIT = 3
TOK = [(0, 128), (128, 128), (256, 32)]

CONSTS = [("ident", 128), ("causal", 256), ("rot", 128), ("ckcos", 32), ("cksin", 32), ("tcos", 24), ("tsin", 24),
          ("cmpadd", 16), ("cmpmul", 16), ("headsum", 128), ("bonus", 17), ("winmask", 4), ("newmask", 128),
          ("rowtok", 512), ("rowhead", 16), ("before", 289), ("repn", 128), ("vbdmask", 16), ("earlier", 128),
          ("ones", 128), ("iota", 128), ("valid", 3), ("eps", 1)]
AT = {}
_o = 0
for _n, _w in CONSTS:
    AT[_n] = (_o, _w)
    _o += _w
NCONST = _o


class Count:

    def __init__(self, sem):
        self.sem, self.n = sem, 0

    def inc(self, ins):
        ins.then_inc(self.sem, 1)
        self.n += 1

    def wait(self, eng):
        eng.wait_ge(self.sem, self.n)


def trunk(nc, A, O):
    with ExitStack() as ctx:
        def sb(name, shape, dt=F32):
            return ctx.enter_context(nc.sbuf_tensor(name, shape, dt))

        def sem(name):
            return ctx.enter_context(nc.semaphore(name))

        ps = ctx.enter_context(nc.psum_tensor("ps", [128, 8, 512], F32))
        ring = sb("ring", [128, RING, SLOT])
        con = sb("con", [128, NCONST])
        xT = sb("xT", [128, DC, NTOK])
        hT = sb("hT", [128, DC, NTOK])
        oT = hT
        nT = sb("nT", [128, DC, NTOK])
        std = sb("std", [128, NTOK])
        rstd = std
        modT = sb("modT", [128, 2, 6, DC, 9])
        rowsT = sb("rowsT", [128, 296])
        small = sb("small", [128, 128])
        pgt = sb("pgt", [1, 64], I32)
        cnti = sb("cnti", [1, 1], I32)
        wr = sb("wr", [128, DC, 8])
        br = sb("br", [128, 8])

        early = ExitStack()

        def early_sb(name, shape):
            return early.enter_context(nc.sbuf_tensor(name, shape, F32))

        work = early_sb("work", [128, 17472])
        qT = early_sb("qT", [128, 8, SEQ])
        kTp = early_sb("kTp", [128, 2, 2, SEQ])
        qbd = early_sb("qbd", [128, NB, 64])
        kTn = early_sb("kTn", [128, 2, 2, 32])
        vP = early_sb("vP", [128, 3, 560])
        ckS = early_sb("ckS", [128, 512])
        smp = early_sb("smp", [128, 320])
        attn = early_sb("attn", [128, 1632 + 15 * 128])
        early.close()

        hN = sb("hN", [128, 3, D])
        XTh = sb("XTh", [128, DC, 128], F32R)
        XTl = sb("XTl", [128, DC, 128], F32R)
        actM = sb("actM", [128, 2, 512])
        siluM = sb("siluM", [128, 512])
        actTh = sb("actTh", [128, 28, 128], F32R)
        actTl = sb("actTl", [128, 28, 128], F32R)
        whi = sb("whi", [128, SPLIT, SLOT], F32R)
        wlo = sb("wlo", [128, SPLIT, SLOT], F32R)
        route = sb("route", [128, 552])

        def C(name, p=128):
            o, w = AT[name]
            return con[0:p, o:o + w]

        b_adaT = rowsT[:, 0:96].rearrange("p (l c) -> p l c", l=2)
        g_mixT = rowsT[:, 96:112].rearrange("p (l c) -> p l c", l=2)
        g_ffnT = rowsT[:, 112:128].rearrange("p (l c) -> p l c", l=2)
        g_finT = rowsT[:, 128:136]
        w_convT = rowsT[:, 136:160].rearrange("p (j c) -> p j c", j=3)
        csT = rowsT[:, 160:232].rearrange("p (s c) -> p s c", s=9)
        peT = rowsT[:, 232:296].rearrange("p (k l) -> p k l", k=2)

        xrow = work[:, 0:3072].rearrange("p (t d) -> p t d", t=3)
        rowsA = work[0:96, 3072:3200]
        rowsB = work[0:64, 3200:3328]
        rowsC = work[0:72, 3328:3456]
        rowsCe = work[0:72, 3456:3584]
        rowsP = work[0:32, 3584:3840]
        modrow = work[0:9, 4096:5120].rearrange("s (i n) -> s i n", i=2)
        Tmain = work[:, TAIL:TAIL + 8192].rearrange("p (g b n) -> p g b n", g=2, b=4)
        Ttail = [work[:, 0:TAIL], work[:, TAIL + 8192:2 * TAIL + 8192]]
        proj = work[:, TAIL:TAIL + 3 * PROJ].rearrange("p (t n) -> p t n", t=3)
        wbd = work[:, 9280:17472].rearrange("p (k l e) -> p k l e", k=2, l=32)
        Vbd = work[:, 0:1024].rearrange("p (c n) -> p c n", c=8)
        TS = work[:, 0:8192].rearrange("p (i b g n) -> p i b g n", i=2, b=2, g=2)
        TW = work[:, 8192:12288].rearrange("p (i b g n) -> p i b g n", i=2, b=2, g=2)
        cvS = nT[0:32].rearrange("p c t -> p (c t)")[:, 0:2048].rearrange("p (b n) -> p b n", b=8)
        cvn = nT[0:8].rearrange("p c t -> p (c t)")[:, 2048:2304]
        actF = work[:, 0:28 * NTOK].rearrange("p (c t) -> p c t", c=28)
        sgF = work[:, 8192:8192 + 2 * 2 * NTOK].rearrange("p (i k t) -> p i k t", i=2, k=2)
        bgT = work[:, 0:2304].rearrange("p (c t) -> p c t", c=8)
        cgT = work[:, 2304:4608].rearrange("p (c t) -> p c t", c=8)
        uP = work[:, 4608:4608 + 8 * 258].rearrange("p (c t) -> p c t", c=8)
        uS = work[:, 6672:6672 + 8 * 48].rearrange("p (c b t) -> p c b t", c=8, b=8)
        zT = work[:, 7056:7056 + 2304].rearrange("p (c t) -> p c t", c=8)
        ctmp = work[:, 9360:9360 + 2 * 288].rearrange("p (i t) -> p i t", i=2)
        tail = work[:, 9936:9936 + 8 * 18].rearrange("p (c j) -> p c j", c=8)
        strow = attn[0:16, 0:1024]
        tailrow = attn[0:18, 1024:2048]
        yacc = hT
        outN = hN
        spare = nT.rearrange("p c t -> p (c t)")
        ysb = spare[:, 0:1024]
        Dm = spare[:, 1024:1408].rearrange("p (t s) -> p t s", t=3)
        Dw = spare[:, 1408:1792].rearrange("p (t s) -> p t s", t=3)
        DT = spare[:, 1792:2080]
        nine = route[:, 0:81]
        selP, cwP, posP = [nine[:, 27 * i:27 * i + 27].rearrange("p (t e) -> p t e", t=3) for i in range(3)]
        selE, cw, pos = [x[:, :, 0:8] for x in (selP, cwP, posP)]
        lg = route[:, 84:108].rearrange("p (t e) -> p t e", t=3)
        mE = route[:, 108:124]
        cur = route[:, 124:140].rearrange("p (a t) -> p a t", a=4)
        rkA = route[:, 140:332].rearrange("p (t j i) -> p t j i", t=3, j=8)
        rkB = route[:, 332:524].rearrange("p (t j i) -> p t j i", t=3, j=8)
        Ssb = attn[:, 0:1536].rearrange("p (i n) -> p i n", i=3)
        PTs = attn[:, 1536:2560].rearrange("p (i n) -> p i n", i=2)
        ScP = attn[:, 2560:2816].rearrange("p (t n) -> p t n", t=2)
        PTc = attn[:, 2816:3072].rearrange("p (t n) -> p t n", t=2)
        SS = attn[:, 0:1632]
        PT = attn[:, 1632:1632 + 1920].rearrange("p (k n) -> p k n", k=15)
        ropet = attn[:, 0:512].rearrange("p (k n) -> p k n", k=4)
        kraw = attn[:, 0:512].rearrange("p (h n) -> p h n", h=2)
        vraw = attn[:, 512:1024].rearrange("p (h n) -> p h n", h=2)
        praw = attn[:, 1024:1056].rearrange("p (k n) -> p k n", k=2)
        ckt = attn[:, 1056:1584]
        rank = attn[:, 0:2312].rearrange("p (k t j i) -> p k t j i", k=2, t=4, j=17)
        gtmp = attn[:, 2312:2504].rearrange("p (t h b) -> p t h b", t=4, b=3)
        osb = qT[:, 0, 0:128]
        selneg = smp[:, 0:68].rearrange("p (t j) -> p t j", t=4)
        score = smp[:, 68:136].rearrange("p (t j) -> p t j", t=4)
        PcG = smp[:, 136:264].rearrange("p (t n) -> p t n", t=4)
        grow = smp[:, 264:276].rearrange("p (t b) -> p t b", t=4)
        ckP = smp[:, 276:292]
        peb = smp[:, 292:294]
        mx4, sm4 = smp[:, 296:300], smp[:, 300:304]
        s_slot = [sem(f"s_slot{i}") for i in range(RING)]
        s_used = sem("s_used")
        s_consts_in = sem("s_consts_in")
        s_rows_in = sem("s_rows_in")
        s_c_in = sem("s_c_in")
        s_x_in = sem("s_x_in")
        s_router_in = sem("s_router_in")
        s_pages_in = sem("s_pages_in")
        s_wbd_clear = sem("s_wbd_clear")
        s_wbd_in = sem("s_wbd_in")
        s_cexp = sem("s_cexp")
        s_csilu = sem("s_csilu")
        s_rows_turned = sem("s_rows_turned")
        s_rowsT_ready = sem("s_rowsT_ready")
        s_x_turned = sem("s_x_turned")
        s_x_ready = sem("s_x_ready")
        s_mod_ready = sem("s_mod_ready")
        s_sq_ready = sem("s_sq_ready")
        s_ss_done = sem("s_ss_done")
        s_std_ready = sem("s_std_ready")
        s_rstd_ready = sem("s_rstd_ready")
        s_xhat_ready = sem("s_xhat_ready")
        s_h_prompt = sem("s_h_prompt")
        s_h_sample = sem("s_h_sample")
        s_proj_done = sem("s_proj_done")
        s_proj_dve = sem("s_proj_dve")
        s_proj_act = sem("s_proj_act")
        s_gate_exp = sem("s_gate_exp")
        s_rope_done = sem("s_rope_done")
        s_qk_turned = sem("s_qk_turned")
        s_qk_prompt = sem("s_qk_prompt")
        s_qk_sample = sem("s_qk_sample")
        s_cv_spread = sem("s_cv_spread")
        s_vbd_ready = sem("s_vbd_ready")
        s_cscore_done = sem("s_cscore_done")
        s_cscore_shift = sem("s_cscore_shift")
        s_cscore_exp = sem("s_cscore_exp")
        s_cprob_ready = sem("s_cprob_ready")
        s_cprob_turned = sem("s_cprob_turned")
        s_cprobT_ready = sem("s_cprobT_ready")
        s_scores_done = sem("s_scores_done")
        s_scores_taken = sem("s_scores_taken")
        s_dve_chain = sem("s_dve_chain")
        s_negmax_ready = sem("s_negmax_ready")
        s_exp_ready = sem("s_exp_ready")
        s_probs_ready = sem("s_probs_ready")
        s_probs_turned = sem("s_probs_turned")
        s_probsT_ready = sem("s_probsT_ready")
        s_pv_done = sem("s_pv_done")
        s_o_taken = sem("s_o_taken")
        s_bank_turned = sem("s_bank_turned")
        s_bank_act = sem("s_bank_act")
        s_bank_dve = sem("s_bank_dve")
        s_cmp_done = sem("s_cmp_done")
        s_craw_ready = sem("s_craw_ready")
        s_rot_done = sem("s_rot_done")
        s_ck_ready = sem("s_ck_ready")
        s_seq_scores = sem("s_seq_scores")
        s_group_scores = sem("s_group_scores")
        s_cprobs = sem("s_cprobs")
        s_importance = sem("s_importance")
        s_snegmax = sem("s_snegmax")
        s_sexp_ready = sem("s_sexp_ready")
        s_group_probs = sem("s_group_probs")
        s_group_pv = sem("s_group_pv")
        s_group_o = sem("s_group_o")
        s_wo_done = sem("s_wo_done")
        s_gu_done = sem("s_gu_done")
        s_gexp_ready = sem("s_gexp_ready")
        s_act_ready = sem("s_act_ready")
        s_down_done = sem("s_down_done")
        s_conv_done = sem("s_conv_done")
        s_conv_copied = sem("s_conv_copied")
        s_u_ready = sem("s_u_ready")
        s_tail_ready = sem("s_tail_ready")
        s_z_ready = sem("s_z_ready")
        s_state_in = sem("s_state_in")
        s_state_turned = sem("s_state_turned")
        s_tail_turned = sem("s_tail_turned")
        s_tail_rows = sem("s_tail_rows")
        s_kv_stored = sem("s_kv_stored")
        s_logits_done = sem("s_logits_done")
        s_logits_shift = sem("s_logits_shift")
        s_logits_exp = sem("s_logits_exp")
        s_sel_ready = sem("s_sel_ready")
        s_pos_done = sem("s_pos_done")
        s_count_ready = sem("s_count_ready")
        s_rows_done = sem("s_rows_done")
        s_rows_taken = sem("s_rows_taken")
        s_gathered = sem("s_gathered")
        s_split_hi = sem("s_split_hi")
        s_tile_done = sem("s_tile_done")
        s_xt_hi = sem("s_xt_hi")
        s_xt_lo = sem("s_xt_lo")
        s_tail_stored = sem("s_tail_stored")
        s_scatter_ready = sem("s_scatter_ready")
        s_silu_ready = sem("s_silu_ready")
        s_moe_chain = sem("s_moe_chain")
        s_eact_ready = sem("s_eact_ready")
        s_eact_turned = sem("s_eact_turned")
        s_eactT_hi = sem("s_eactT_hi")
        s_eactT_lo = sem("s_eactT_lo")
        s_y_act = sem("s_y_act")
        s_y_dve = sem("s_y_dve")
        s_share_done = sem("s_share_done")
        s_share_added = sem("s_share_added")
        s_gather_ready = sem("s_gather_ready")
        s_final_ready = sem("s_final_ready")
        s_final_rows = sem("s_final_rows")
        s_stored = sem("s_stored")
        s_vp_ready = sem("s_vp_ready")
        s_tail_pe = sem("s_tail_pe")
        s_sc_done = sem("s_sc_done")
        s_sc_shift = sem("s_sc_shift")
        s_sc_exp = sem("s_sc_exp")
        s_cv_ready = sem("s_cv_ready")
        s_modrow = sem("s_modrow")
        s_mod_turned = sem("s_mod_turned")
        s_osb_ready = sem("s_osb_ready")
        s_osb_turned = sem("s_osb_turned")

        def quarter(w, r0, c0, kcs, width):
            return w[r0:r0 + 128 * kcs, c0:c0 + width].rearrange("(k p) n -> p k n", p=128)

        stream = []

        def pair(w, c0, width=512):
            for h in range(2):
                stream.append([(0, 128, quarter(w, 512 * h, c0, 4, width), 4)])

        for k in range(24):
            pair(A["w_ada"][k // 12], (k % 12) * 512)
        T_NSA = len(stream)
        for ct in range(5):
            pair(A["w_nsa_in"][0], ct * 512)
        stream.append([(0, 128, quarter(A["w_nsa_in"][0], 0, 2560, 8, 48), 8)])
        T_CACHE = len(stream)
        for kv in range(2):
            for b in range(NB):
                stream.append(("page", "cmp", b, kv))
        T_SEL = len(stream)
        tile_k, tile_v = {}, {}
        for kv, tau in ((0, 0), (0, 1), (1, 0), (0, 2), (1, 1), (0, 3), (1, 2), (1, 3)):
            (tile_k, tile_v)[kv][tau] = len(stream)
            for b in (2 * tau, 2 * tau + 1):
                stream.append(("page", "sel", b, kv))
            stream.append(("win", tau, kv))
        T_WO = len(stream)
        for ch in range(2):
            for gp in range(2):
                w = A["w_nsa_out"][0].rearrange("(g r d) n -> g d r n", g=4, r=4)
                stream.append([(64 * g2, 64, w[2 * gp + g2][:, :, ch * 512:ch * 512 + 512], 4) for g2 in range(2)])
        T_FU = len(stream)
        for j in range(7):
            pair(A["w_ff_gu"][0], j * 512)
            pair(A["w_ff_gu"][0], FF + j * 512)
        T_FD = len(stream)
        for ch in range(2):
            for i in range(7):
                stream.append([(0, 128, quarter(A["w_ff_down"][0], 512 * i, ch * 512, 4, 512), 4)])
        T_CI = len(stream)
        for jt in range(2):
            for wh in range(3):
                pair(A["w_conv_in"][0], wh * 1024 + jt * 512)
        T_CO = len(stream)
        for ch in range(2):
            pair(A["w_conv_out"][0], ch * 512)
        T_MOE = len(stream)
        total = [0] * RING
        need = []
        for n, ent in enumerate(stream):
            q = n % RING
            total[q] += 16 * ({"page": 8, "win": 2}[ent[0]] if isinstance(ent, tuple) else len(ent))
            need.append(total[q])

        def wait_tile(pe, n):
            pe.wait_ge(s_slot[n % RING], need[n])

        def wait_expert_tile(eng, e, i):
            q = (T_MOE + i) % RING
            eng.wait_ge(s_slot[q], e * (16 * TILES_E // RING) + (total[q] + 16 * (i // RING + 1)))

        def slot(n, kc=4):
            w = {4: 512, 8: 48}[kc]
            return ring[:, n % RING, 0:kc * w].rearrange("p (k n) -> p k n", k=kc)

        def dst_n(ap):
            n = 1
            for d_ in ap.shape[1:]:
                n *= d_
            return n

        def turned(j, dst):
            np_, n = dst.shape[0], dst_n(dst)
            src = ps[0:np_, j % 4 if j < 64 else 4 + (j - 64) % 3, 0:n]
            return src if len(dst.shape) == 2 else src.rearrange("p (k n) -> p k n", n=128)

        J_SEL = 64

        def j_keys(tau):
            return J_SEL + 12 * tau + 4 * max(tau - 1, 0)

        def j_probs(tau):
            return J_SEL + 12 * min(tau + 2, 4) + 4 * tau

        def pages(n):
            return ring[:, n % RING, :].rearrange("p (k n) -> p k n", k=8)

        block = ctx.enter_context(nc.Block())

        @block.sync
        def _(sp):
            sp.dma_start(pgt[:], A["page_table"].rearrange("(o b) p -> o (b p)", o=1)).then_inc(s_pages_in, 16)
            for n, ent in enumerate(stream):
                if n == T_CACHE:
                    sp.wait_ge(s_pages_in, 16)
                if isinstance(ent, tuple) and ent[0] == "page":
                    _, kind, b, kv = ent
                    src = A["cache_cmp_kv"] if kind == "cmp" else A["cache_sel_kv"]
                    for j in range(8):
                        pg = sp.value_load(pgt[0:1, b * 8 + j:b * 8 + j + 1], min_val=0, max_val=src.shape[1] - 1)
                        if j == 0:
                            sp.wait_ge(s_used, n - RING + 1)
                        sp.dma_start(pages(n)[:, j, :], src[0, bass.ds(pg, 1), :, kv].rearrange("o r g d -> (o r) (g d)")
                                     ).then_inc(s_slot[n % RING], 16)
                    continue
                if n >= RING:
                    sp.wait_ge(s_used, n - RING + 1)
                if isinstance(ent, tuple):
                    _, tau, kv = ent
                    for b2 in range(2):
                        sp.dma_start(pages(n)[:, 4 * b2:4 * b2 + 4, :],
                                     A["cache_win_kv"][0, 2 * tau + b2, :, kv].rearrange("(j p) g d -> p j (g d)", p=128)
                                     ).then_inc(s_slot[n % RING], 16)
                    continue
                for p0, pn, src, kc in ent:
                    sp.dma_start(slot(n, kc)[p0:p0 + pn], src).then_inc(s_slot[n % RING], 16)

            def experts(rnd):
                with sp.Fori(0, NE) as e:
                    for i in range(TILES_E):
                        sp.wait_ge(s_used, (e + NE * rnd) * TILES_E + (T_MOE + i - RING + 1))
                        if i < 28:
                            j, u, h = i // 4, (i // 2) % 2, i % 2
                            src = A["w_moe_gu"][0, bass.ds(e, 1), 512 * h:512 * h + 512,
                                                u * FF + j * 512:u * FF + j * 512 + 512
                                                ].rearrange("o (k p) n -> p (o k) n", p=128)
                            dst = slot(T_MOE + i)
                        else:
                            src = A["w_moe_down"][0, bass.ds(e, 1), 256 * (i - 28):256 * (i - 27), :
                                                  ].rearrange("o (k p) n -> p (o k) n", p=128)
                            dst = ring[:, (T_MOE + i) % RING, :].rearrange("p (k n) -> p k n", k=2)
                        sp.dma_start(dst, src).then_inc(s_slot[(T_MOE + i) % RING], 16)

            experts(0)
            sp.wait_ge(s_count_ready, 1)
            c = sp.value_load(cnti[0:1, 0:1], min_val=0, max_val=NTOK)
            for rnd in (1, 2):
                with sp.If(c > SLOTS_E * rnd):
                    experts(rnd)

        @block.gpsimd
        def _(g):
            g.wait_ge(s_wbd_clear, 1)
            for kv, nm_ in enumerate(("w_cmp_k", "w_cmp_v")):
                for g2 in range(2):
                    g.dma_start(wbd[64 * g2:64 * g2 + 64, kv, :, 64 * g2:64 * g2 + 64],
                                A[nm_][0].rearrange("l d e -> d l e")).then_inc(s_wbd_in, 16)
            g.dma_start(O[7][0, :, 0:508].rearrange("b r k g d -> b (r k g d)"),
                        A["cache_win_kv"][0, :, 4:512].rearrange("b r k g d -> b (r k g d)")).then_inc(s_stored, 16)
            n = 1
            g.wait_ge(s_rope_done, 6)
            for o_p, o_s, c0 in ((2, 3, 1024), (4, 5, 1536), (6, None, 2048)):
                g.dma_start(O[o_p][0, 0].rearrange("(t p) k g d -> p t (k g d)", p=128),
                            proj[:, 0:2, c0:c0 + 512]).then_inc(s_stored, 16)
                n += 1
                if o_s is not None:
                    g.dma_start(O[o_s][0].rearrange("b t k g d -> (b t) (k g d)"),
                                proj[0:32, 2, c0:c0 + 512]).then_inc(s_stored, 16)
                    n += 1
                else:
                    for b in range(NB):
                        g.dma_start(O[7][0, b, 508:512].rearrange("t k g d -> t (k g d)"),
                                    proj[4 * b:4 * b + 4, 2, c0:c0 + 512]).then_inc(s_stored, 16)
                        n += 1
            g.wait_ge(s_stored, 16 * n)
            g.sem_inc(s_kv_stored, 1)
            g.wait_ge(s_tail_rows, 2)
            g.dma_start(O[8][0, 0], tailrow[0:2, :]).then_inc(s_stored, 16)
            g.dma_start(O[9][0].rearrange("b j d -> (b j) d"), tailrow[2:18, :]).then_inc(s_stored, 16)
            n += 2
            g.wait_ge(s_stored, 16 * n)
            g.sem_inc(s_tail_stored, 1)
            g.wait_ge(s_final_rows, 6)
            g.dma_start(O[0][0].rearrange("(t p) d -> p t d", p=128), outN[:, 0:2, :]).then_inc(s_stored, 16)
            g.dma_start(O[1].rearrange("b t d -> (b t) d"), outN[0:32, 2, :]).then_inc(s_stored, 16)
            n += 2
            g.wait_ge(s_stored, 16 * n)

        @block.scalar
        def _(a):
            a.dma_start(rowsC[0:8, :], A["c_prompt"].rearrange("s (c p) -> (s c) p", p=128)).then_inc(s_c_in, 16)
            a.dma_start(rowsC[8:72, :], A["c_sample"].rearrange("s (c p) -> (s c) p", p=128)).then_inc(s_c_in, 16)
            a.dma_start(con[:], A["consts"]).then_inc(s_consts_in, 16)
            a.dma_start(rowsA, A["b_ada"].rearrange("l (c p) -> (l c) p", p=128)).then_inc(s_rows_in, 16)
            a.dma_start(rowsB[0:16, :], A["g_norm_mix"].rearrange("l (c p) -> (l c) p", p=128)).then_inc(s_rows_in, 16)
            a.dma_start(rowsB[16:32, :], A["g_norm_ffn"].rearrange("l (c p) -> (l c) p", p=128)).then_inc(s_rows_in, 16)
            a.dma_start(rowsB[32:40, :], A["g_norm_final"].rearrange("(c p) -> c p", p=128)).then_inc(s_rows_in, 16)
            a.dma_start(rowsB[40:64, :], A["w_conv"][0].rearrange("j (c p) -> (j c) p", p=128)).then_inc(s_rows_in, 16)
            for kv, nm_ in enumerate(("pe_cmp_k", "pe_cmp_v")):
                for g2 in range(2):
                    a.dma_start(rowsP[:, kv * 128 + g2 * 64:kv * 128 + g2 * 64 + 64], A[nm_][0]).then_inc(s_rows_in, 16)
            a.dma_start(xrow[:, 0:2, :], A["x_prompt"][0].rearrange("(t p) d -> p t d", p=128)).then_inc(s_x_in, 16)
            a.dma_start(xrow[0:32, 2, :], A["x_sample"].rearrange("b t d -> (b t) d")).then_inc(s_x_in, 16)
            a.dma_start(wr[:], A["w_router"][0].rearrange("(c p) e -> p c e", p=128)).then_inc(s_router_in, 16)
            a.dma_start(br[:], A["b_router"].to_broadcast([128, 8])).then_inc(s_router_in, 16)

            a.wait_ge(s_c_in, 32)
            a.activation(rowsCe, rowsC, ACT.Exp, scale=-1.0).then_inc(s_cexp, 1)

            def norm(n):
                for c in range(DC):
                    a.wait_ge(s_x_ready, 8 * n + c + 1)
                    if n and c == 0:
                        a.wait_ge(s_h_sample, n)
                    a.activation(nT[:, c, :], xT[:, c, :], ACT.Square).then_inc(s_sq_ready, 1)
                a.wait_ge(s_ss_done, n + 1)
                if n:
                    a.wait_ge(s_xhat_ready, n)
                a.activation(std[:], ps[:, 6, 0:NTOK], ACT.Sqrt, bias=C("eps"), scale=1.0 / D).then_inc(s_std_ready, 1)
                if n < 4:
                    lay, v = n // 2, 3 * (n % 2)
                    a.wait_ge(s_xhat_ready, n + 1)
                    a.wait_ge(s_mod_ready, lay + 1)
                    for c in range(DC):
                        a.activation(hT[:, c, 0:SEQ], nT[:, c, 0:SEQ], ACT.Identity, bias=modT[:, lay, v, c, 0:1],
                                     scale=modT[:, lay, v + 1, c, 0:1]).then_inc(s_h_prompt, 1)

            norm(0)
            for ct in range(5):
                a.wait_ge(s_proj_done, ct + 1)
                src, dst = ps[:, 3 * (ct % 2) + 1, :], proj[:, 1, ct * 512:ct * 512 + 512]
                for g2 in range(2 if ct < 2 else 1):
                    if ct < 2:
                        ins = a.activation(dst.rearrange("p (r g d) -> p g r d", r=4, g=2)[:, g2],
                                           src.rearrange("p (g r d) -> p g r d", g=2, r=4)[:, g2], ACT.Copy)
                    else:
                        ins = a.activation(dst, src, ACT.Copy)
                ins.then_inc(s_proj_act, 1)
            a.wait_ge(s_proj_done, 6)
            for t, (_, m) in enumerate(TOK):
                a.activation(vP[0:m, t, 512:560], ps[0:m, 3 + t, 0:48], ACT.Exp, scale=-1.0).then_inc(s_gate_exp, 1)
            for i in range(16):
                a.wait_ge(s_qk_turned, i + 1)
                src = ps[:, i % 6, 0:SEQ]
                if i < 8:
                    dst = qT[:, i, :]
                elif i < 12:
                    dst = kTp[:, (i - 8) % 2, (i - 8) // 2, :]
                else:
                    dst = Ttail[(i - 12) // 2][:, SEQ * ((i - 12) % 2):SEQ * ((i - 12) % 2) + SEQ]
                a.activation(dst, src, ACT.Copy).then_inc(s_qk_prompt, 1)
            def take(j, dst):
                a.wait_ge(s_bank_turned, j + 1)
                a.activation(dst, turned(j, dst), ACT.Copy).then_inc(s_bank_act, 1)

            a.wait_ge(s_kv_stored, 1)
            a.wait_ge(s_qk_turned, 16)
            a.wait_ge(s_vp_ready, 1)
            for kv in range(2):
                for b in range(NB):
                    if b % 4 == 0 and (kv or b):
                        a.wait_ge(s_cmp_done, 2 * kv + b // 4)
                    for h in range(2):
                        take(32 * kv + 4 * b + 2 * h, Tmain[:, 0, b % 4, 512 * h:512 * h + 512])
            a.wait_ge(s_sc_shift, 1)
            a.activation(PcG, PcG, ACT.Exp, scale=SCALE).then_inc(s_sc_exp, 1)
            for t in range(2):
                a.wait_ge(s_cscore_shift, t + 1)
                a.activation(ScP[:, t, :], ScP[:, t, :], ACT.Exp, scale=SCALE).then_inc(s_cscore_exp, 1)
            for i in range(34):
                if i < 32:
                    w = 128 * (i // 16 + 1)
                    a.wait_ge(s_negmax_ready, i + 1)
                    for k in range(2):
                        a.activation(Ssb[:, i % 3, k * w:k * w + w], Ssb[:, i % 3, k * w:k * w + w], ACT.Exp,
                                     bias=small[:, 8 * (i % 3) + 2 + k:8 * (i % 3) + 3 + k], scale=SCALE,
                                     accum_out=small[:, 8 * (i % 3) + 4 + k:8 * (i % 3) + 5 + k]).then_inc(s_exp_ready, 1)
                if i >= 2:
                    u = i - 2
                    w = 128 * (u // 16 + 1)
                    a.wait_ge(s_probs_turned, u + 1)
                    if u >= 2:
                        a.wait_ge(s_pv_done, u - 1)
                    a.activation(PTs[:, u % 2, 0:2 * w], ps[:, 3 + u % 2, 0:2 * w], ACT.Copy).then_inc(s_probsT_ready, 1)
            a.wait_ge(s_pv_done, 32)

            def take_keys(tau):
                j = j_keys(tau)
                for b2 in range(2):
                    if tau >= 2:
                        a.wait_ge(s_seq_scores, 2 * (tau - 2) + b2 + 1)
                    for q in range(4):
                        if (j + 4 * b2 + q) % 2 == 0:
                            take(j + 4 * b2 + q, TS[:, tau % 2, b2, q // 2, 512 * (q % 2):512 * (q % 2) + 512])
                for q in range(4):
                    if (j + 8 + q) % 2 == 0:
                        take(j + 8 + q, TW[:, tau % 2, q // 2, q % 2, :])

            take_keys(0)
            for tau in range(4):
                if tau < 3:
                    take_keys(tau + 1)
                a.wait_ge(s_snegmax, tau + 1)
                for k, (lo, hi) in enumerate(((0, 1056), (1056, 1600))):
                    a.activation(SS[:, lo:hi], SS[:, lo:hi], ACT.Exp, bias=small[:, 38 + k:39 + k], scale=SCALE,
                                 accum_out=small[:, 40 + k:41 + k]).then_inc(s_sexp_ready, 1)
                if tau:
                    a.wait_ge(s_group_pv, tau)
                take(j_probs(tau), PT[:, 0:4, :])
                take(j_probs(tau) + 2, PT[:, 8:12, :])
            norm(1)
            for m in range(28):
                a.wait_ge(s_gu_done, m + 1)
                if m >= 2:
                    a.wait_ge(s_act_ready, m - 1)
                a.activation(sgF[:, m % 2, 0, :], ps[:, 2 * (m % 3), 0:NTOK], ACT.Exp, scale=-1.0).then_inc(s_gexp_ready, 1)
            norm(2)
            a.dma_start(strow, A["state_conv"][0].rearrange("b j d -> (b j) d")).then_inc(s_state_in, 16)
            k = 0
            for B in range(24):
                wh, c = (B // 4) % 3, 4 * (B // 12) + B % 4
                if wh < 2:
                    a.wait_ge(s_conv_done, B + 1)
                    a.activation((bgT, cgT)[wh][:, c, :], ps[:, B % 6, 0:NTOK], ACT.Copy).then_inc(s_conv_copied, 1)
            norm(3)
            a.wait_ge(s_logits_shift, 1)
            a.activation(lg[:], lg[:], ACT.Exp).then_inc(s_logits_exp, 1)

            def experts(rnd):
                with a.Fori(0, NE) as e0:
                    e = e0 + NE * rnd
                    for i in range(TILES_E):
                        wait_expert_tile(a, e, i)
                        a.wait_ge(s_tile_done, e * TILES_E + (i + 1))
                        a.activation(whi[:, i % SPLIT, :], ring[:, (T_MOE + i) % RING, :], ACT.Copy).then_inc(s_split_hi, 1)
                        if i == 2:
                            for h in range(2):
                                a.wait_ge(s_gathered, e * 3 + (h + 1))
                                a.activation(XTh[:, 4 * h:4 * h + 4, :], ps[:, 4 + h, :].rearrange("p (c s) -> p c s", c=4),
                                             ACT.Copy).then_inc(s_xt_hi, 1)
                        if i % 4 == 2 and 6 <= i <= 30:
                            j = (i - 6) // 4
                            a.wait_ge(s_tile_done, e * TILES_E + (4 * j + 4 + SPLIT))
                            if j:
                                a.wait_ge(s_eact_ready, e * 7 + j)
                            a.activation(siluM[:], ps[:, 2 * (j % 2), :], ACT.Silu).then_inc(s_silu_ready, 1)
                        if i % 4 == 2 and 10 <= i <= 34:
                            j = (i - 10) // 4
                            a.wait_ge(s_eact_turned, e * 7 + (j + 1))
                            a.activation(actTh[:, 4 * j:4 * j + 4, :], ps[:, 4 + j % 2, :].rearrange("p (k s) -> p k s", k=4),
                                         ACT.Copy).then_inc(s_eactT_hi, 1)
                    a.wait_ge(s_tile_done, e * TILES_E + (TILES_E + SPLIT))
                    a.activation(ysb[:, 0:512], ps[:, 6, :], ACT.Copy).then_inc(s_y_act, 1)

            experts(0)
            a.wait_ge(s_count_ready, 1)
            c = a.value_load(cnti[0:1, 0:1], min_val=0, max_val=NTOK)
            for rnd in (1, 2):
                with a.If(c > SLOTS_E * rnd):
                    experts(rnd)
            norm(4)

        @block.vector
        def _(v):
            ch = Count(s_dve_chain)

            def link(ins):
                ch.inc(ins)
                ch.wait(v)

            link(v.memset(wbd[:], 0.0))
            v.memset(qbd[:], 0.0).then_inc(s_wbd_clear, 1)
            v.wait_ge(s_cexp, 1)
            link(v.tensor_scalar_add(rowsCe, rowsCe, 1.0))
            link(v.reciprocal(rowsCe, rowsCe))
            v.tensor_tensor(rowsC, rowsC, rowsCe, ALU.mult).then_inc(s_csilu, 1)
            v.wait_ge(s_rows_turned, 1)
            v.tensor_copy(rowsT[:], ps[:, 7, 0:296]).then_inc(s_rowsT_ready, 1)
            for c in range(DC):
                v.wait_ge(s_x_turned, c + 1)
                v.tensor_copy(xT[:, c, :], ps[:, 2 + c % 4, 0:NTOK]).then_inc(s_x_ready, 1)

            for k in range(24):
                v.wait_ge(s_used, 2 * k + 2)
                if k >= 2:
                    v.wait_ge(s_mod_turned, k - 1)
                v.tensor_copy(modrow[:, k % 2, :], ps[0:9, k % 2, :]).then_inc(s_modrow, 1)

            def modulation(lay):
                v.wait_ge(s_mod_turned, 12 * lay + 12)
                m = modT[:, lay].rearrange("p v c s -> p (v c) s")
                link(v.tensor_tensor(m, ps[:, 2 + lay, 0:432].rearrange("p (c s) -> p c s", s=9),
                                     b_adaT[:, lay].unsqueeze(2).to_broadcast([128, 48, 9]), ALU.add))
                for k, g_ in ((1, g_mixT), (4, g_ffnT)):
                    ins = v.scalar_tensor_tensor(out=modT[:, lay, k], in0=modT[:, lay, k], scalar=1.0,
                                                 in1=g_[:, lay].unsqueeze(2).to_broadcast([128, 8, 9]),
                                                 op0=ALU.add, op1=ALU.mult)
                    if k == 1:
                        link(ins)
                ins.then_inc(s_mod_ready, 1)
                v.wait_ge(s_mod_ready, lay + 1)

            def norm(n):
                v.wait_ge(s_std_ready, n + 1)
                v.reciprocal(rstd[:], std[:]).then_inc(s_rstd_ready, 1)
                v.wait_ge(s_rstd_ready, n + 1)
                v.tensor_tensor(nT[:], xT[:], rstd[:].unsqueeze(1).to_broadcast([128, DC, NTOK]),
                                ALU.mult).then_inc(s_xhat_ready, 1)
                v.wait_ge(s_xhat_ready, n + 1)
                if n < 4:
                    lay, k = n // 2, 3 * (n % 2)
                    nS = nT[:, :, SEQ:].rearrange("p c (b t) -> p c b t", t=NT)
                    hS = hT[:, :, SEQ:].rearrange("p c (b t) -> p c b t", t=NT)
                    for t in range(NT):
                        ins = v.tensor_tensor(nS[:, :, :, t], nS[:, :, :, t], modT[:, lay, k + 1, :, 1:9], ALU.mult)
                    link(ins)
                    for t in range(NT):
                        ins = v.tensor_tensor(hS[:, :, :, t], nS[:, :, :, t], modT[:, lay, k, :, 1:9], ALU.add)
                    ins.then_inc(s_h_sample, 1)

            def residual(lay, k, src):
                for c in range(DC):
                    y = src(c)
                    ys = small[:, 64 + 32 * (c % 2):96 + 32 * (c % 2)]
                    v.scalar_tensor_tensor(out=xT[:, c, 0:SEQ], in0=y[:, 0:SEQ], scalar=modT[:, lay, k, c, 0:1],
                                           in1=xT[:, c, 0:SEQ], op0=ALU.mult, op1=ALU.add)
                    link(v.tensor_tensor(ys.rearrange("p (b t) -> p b t", t=NT),
                                         y[:, SEQ:NTOK].rearrange("p (b t) -> p b t", t=NT),
                                         modT[:, lay, k, c, 1:9].unsqueeze(2).to_broadcast([128, NB, NT]), ALU.mult))
                    v.tensor_tensor(xT[:, c, SEQ:], xT[:, c, SEQ:], ys, ALU.add).then_inc(s_x_ready, 1)

            modulation(0)
            modulation(1)
            norm(0)
            for ct in range(5):
                v.wait_ge(s_proj_done, ct + 1)
                for t in (0, 2):
                    m = TOK[t][1]
                    src, dst = ps[0:m, 3 * (ct % 2) + t, :], proj[0:m, t, ct * 512:ct * 512 + 512]
                    if ct < 2:
                        for g2 in range(2):
                            ins = v.tensor_copy(dst.rearrange("p (r g d) -> p g r d", r=4, g=2)[:, g2],
                                                src.rearrange("p (g r d) -> p g r d", g=2, r=4)[:, g2])
                    else:
                        ins = v.tensor_copy(dst, src)
                ins.then_inc(s_proj_dve, 1)
            v.wait_ge(s_proj_act, 5)
            v.wait_ge(s_proj_dve, 5)
            tc, ts_ = (C(x).rearrange("p (t n) -> p t n", t=3) for x in ("tcos", "tsin"))
            for grp in range(2):
                for t, (_, m) in enumerate(TOK):
                    if grp == 0:
                        xv = proj[0:m, t, 0:1024].rearrange("p (h d) -> p h d", h=16)
                        x1, x2 = xv[:, :, 0:8], xv[:, :, 8:16]
                        tv = [ropet[0:m, i, 0:128].rearrange("p (h n) -> p h n", n=8) for i in range(4)]
                        co = tc[0:m, t].unsqueeze(1).to_broadcast([m, 16, 8])
                        si = ts_[0:m, t].unsqueeze(1).to_broadcast([m, 16, 8])
                        parts = [(x1, x2, tv, co, si)]
                    else:
                        parts = []
                        for q_, c0 in enumerate((1536, 2048)):
                            xv = proj[0:m, t, c0:c0 + 256].rearrange("p (h d) -> p h d", h=4)
                            tv = [ropet[0:m, i, 32 * q_:32 * q_ + 32].rearrange("p (h n) -> p h n", n=8) for i in range(4)]
                            parts.append((xv[:, :, 0:8], xv[:, :, 8:16], tv,
                                          tc[0:m, t].unsqueeze(1).to_broadcast([m, 4, 8]),
                                          ts_[0:m, t].unsqueeze(1).to_broadcast([m, 4, 8])))
                    for x1, x2, tv, co, si in parts:
                        v.tensor_tensor(tv[0], x1, co, ALU.mult)
                        v.tensor_tensor(tv[1], x2, si, ALU.mult)
                        v.tensor_tensor(tv[2], x2, co, ALU.mult)
                        ins = v.tensor_tensor(tv[3], x1, si, ALU.mult)
                    link(ins)
                    for x1, x2, tv, co, si in parts:
                        v.tensor_tensor(x1, tv[0], tv[1], ALU.subtract)
                        ins = v.tensor_tensor(x2, tv[2], tv[3], ALU.add)
                    ins.then_inc(s_rope_done, 1)
                    v.wait_ge(s_rope_done, 3 * grp + t + 1)
            v.wait_ge(s_gate_exp, 3)
            for t, (_, m) in enumerate(TOK):
                gv = vP[0:m, t, 512:560]
                link(v.tensor_scalar_add(gv, gv, 1.0))
                link(v.reciprocal(gv, gv))
            for t, (_, m) in enumerate(TOK):
                v.tensor_copy(vP[0:m, t, 0:256], proj[0:m, t, 1792:2048])
                ins = v.tensor_copy(vP[0:m, t, 256:512], proj[0:m, t, 2304:2560])
            ins.then_inc(s_vp_ready, 1)
            for kv in range(2):
                ins = v.tensor_copy(Ttail[kv][:, 512:544], peT[:, kv, :])
            ins.then_inc(s_tail_pe, 1)
            for i in range(12):
                v.wait_ge(s_qk_prompt, i + 1)
                if i < 8:
                    gp, r = i // 4, i % 4
                    for g2 in range(2):
                        dst = qbd[64 * g2:64 * g2 + 64].rearrange("p b (g k r t) -> p b g k r t", g=2, k=2, r=4)
                        ins = v.tensor_copy(dst[:, :, gp, g2, r, :],
                                            ps[64 * g2:64 * g2 + 64, i % 6, SEQ:NTOK].rearrange("p (b t) -> p b t", t=NT))
                else:
                    ins = v.tensor_copy(kTn[:, (i - 8) % 2, (i - 8) // 2, :], ps[:, i % 6, SEQ:NTOK])
                ins.then_inc(s_qk_sample, 1)

            def take(j, dst):
                v.wait_ge(s_bank_turned, j + 1)
                v.tensor_copy(dst, turned(j, dst)).then_inc(s_bank_dve, 1)

            v.wait_ge(s_kv_stored, 1)
            v.wait_ge(s_vp_ready, 1)
            for kv in range(2):
                for b in range(NB):
                    if b % 4 == 0 and (kv or b):
                        v.wait_ge(s_cmp_done, 2 * kv + b // 4)
                    for h in range(2):
                        take(32 * kv + 4 * b + 2 * h + 1, Tmain[:, 1, b % 4, 512 * h:512 * h + 512])
            v.wait_ge(s_cmp_done, 4)
            v.tensor_copy(peb[:, 0:1], ps[:, 4, 16:17])
            link(v.tensor_copy(peb[:, 1:2], ps[:, 6, 272:273]))
            v.tensor_scalar(praw[:, 0], ps[:, 4, 0:16], peb[:, 0:1], None, ALU.add)
            v.tensor_scalar(kraw[:, 0], ps[:, 4, 17:273], peb[:, 0:1], None, ALU.add)
            v.tensor_scalar(kraw[:, 1], ps[:, 5, 0:256], peb[:, 0:1], None, ALU.add)
            v.tensor_scalar(praw[:, 1], ps[:, 6, 256:272], peb[:, 1:2], None, ALU.add)
            v.tensor_scalar(vraw[:, 0], ps[:, 6, 0:256], peb[:, 1:2], None, ALU.add)
            v.tensor_scalar(vraw[:, 1], ps[:, 7, 0:256], peb[:, 1:2], None, ALU.add).then_inc(s_craw_ready, 1)
            v.wait_ge(s_craw_ready, 1)
            v.wait_ge(s_rot_done, 1)

            def rope_cmp(dst, raw, rot, g, n, o):
                co = C("ckcos")[:, 0:n].unsqueeze(1).to_broadcast([128, g, n])
                si = C("cksin")[:, 0:n].unsqueeze(1).to_broadcast([128, g, n])
                f = lambda x: x.rearrange("p (g n) -> p g n", g=g)
                v.tensor_tensor(f(dst), f(raw), co, ALU.mult)
                link(v.tensor_tensor(f(ckt[:, o:o + g * n]), f(rot), si, ALU.mult))
                return v.tensor_tensor(f(dst), f(dst), f(ckt[:, o:o + g * n]), ALU.add)

            rope_cmp(ckP, praw[:, 0], ps[:, 1, 0:16], 2, 8, 512)
            rope_cmp(ckS[:], kraw[:].rearrange("p h n -> p (h n)"), ps[:, 0, :], 16, 32, 0)
            v.tensor_copy(cvn, ps[0:8, 1, 128:384]).then_inc(s_ck_ready, 1)
            for q in range(4):
                v.tensor_copy(cvS[:, 2 * q:2 * q + 2, :], ps[0:32, 2 + q, :].rearrange("p (b n) -> p b n", b=2)
                              ).then_inc(s_cv_ready, 1)
            v.wait_ge(s_cv_spread, 1)
            vm = C("vbdmask").rearrange("p (c g) -> p c g", c=8)
            for gp in range(2):
                for g2 in range(2):
                    ins = v.tensor_tensor(Vbd[:, 4 * gp:4 * gp + 4, 64 * g2:64 * g2 + 64],
                                          ps[:, 0, gp * 128 + g2 * 64:gp * 128 + g2 * 64 + 64].unsqueeze(1).to_broadcast([128, 4, 64]),
                                          vm[:, 4 * gp:4 * gp + 4, g2].unsqueeze(2).to_broadcast([128, 4, 64]), ALU.mult)
            ins.then_inc(s_vbd_ready, 1)
            v.wait_ge(s_sc_done, 1)
            link(v.tensor_copy(PcG, ps[:, 1, 0:128].rearrange("p (t n) -> p t n", t=4)))
            link(v.tensor_tensor(gtmp, ps[:, 1, 128:320].rearrange("p (t h b) -> p t h b", t=4, b=3),
                                 C("rowhead").unsqueeze(1).unsqueeze(3).to_broadcast([128, 4, 16, 3]), ALU.mult))
            for t in range(4):
                ins = v.tensor_reduce(grow[:, t, :], gtmp[:, t].rearrange("p h b -> p b h"), AX, ALU.add)
            link(ins)
            link(v.tensor_reduce(mx4, PcG, AX, ALU.max))
            v.tensor_tensor(PcG, PcG, mx4.unsqueeze(2).to_broadcast([128, 4, 32]), ALU.subtract).then_inc(s_sc_shift, 1)
            v.wait_ge(s_sc_exp, 1)
            link(v.tensor_reduce(sm4, PcG, AX, ALU.add))
            link(v.reciprocal(sm4, sm4))
            v.tensor_tensor(PcG, PcG, sm4.unsqueeze(2).to_broadcast([128, 4, 32]), ALU.mult).then_inc(s_cprobs, 1)
            v.wait_ge(s_importance, 1)
            link(v.memset(score[:, :, 16:17], 0.0))
            link(v.tensor_reduce(score[:, :, 0:16], ps[:, 2, 0:128].rearrange("p (t n c) -> p t n c", t=4, c=2), AX, ALU.add))
            link(v.tensor_tensor(score, score, C("bonus").unsqueeze(1).to_broadcast([128, 4, 17]), ALU.add))
            for t in range(4):
                si_ = score[:, t].unsqueeze(1).to_broadcast([128, 17, 17])
                sj_ = score[:, t].unsqueeze(2).to_broadcast([128, 17, 17])
                v.tensor_tensor(rank[:, 0, t], si_, sj_, ALU.is_gt)
                ins = v.tensor_tensor(rank[:, 1, t], si_, sj_, ALU.is_equal)
            link(ins)
            bf = C("before").rearrange("p (j i) -> p j i", j=17)
            for t in range(4):
                ins = v.tensor_tensor(rank[:, 1, t], rank[:, 1, t], bf, ALU.mult)
            link(ins)
            rf = [rank[:, i].rearrange("p t j i -> p (t j) i") for i in range(2)]
            link(v.tensor_tensor(rf[0], rf[0], rf[1], ALU.add))
            sn = selneg.rearrange("p t j -> p (t j)")
            link(v.tensor_reduce(sn, rf[0], AX, ALU.add))
            v.tensor_scalar(sn, sn, 7.5, -BIG, ALU.is_gt, ALU.mult)
            link(v.tensor_tensor(PcG, PcG, grow[:, :, 0].unsqueeze(2).to_broadcast([128, 4, 32]), ALU.mult))
            ca, cm = (C(x).rearrange("p (t n) -> p t n", t=2) for x in ("cmpadd", "cmpmul"))
            mxc, smc = small[:, 96:112], small[:, 112:128]
            v.wait_ge(s_cscore_done, 1)
            for t in range(2):
                sc = ScP[:, t, :].rearrange("p (c g n) -> p c g n", c=8, g=2)
                s16 = ScP[:, t, :].rearrange("p (h n) -> p h n", h=16)
                for g2 in range(2):
                    ins = v.tensor_tensor(sc[:, :, g2, :], ps[:, 6 + g2, 256 + 64 * t:320 + 64 * t].rearrange("p (c n) -> p c n", c=8),
                                          ca[:, t].unsqueeze(1).to_broadcast([128, 8, 8]), ALU.add)
                link(ins)
                link(v.tensor_reduce(mxc, s16, AX, ALU.max))
                v.tensor_tensor(s16, s16, mxc.unsqueeze(2).to_broadcast([128, 16, 8]), ALU.subtract).then_inc(s_cscore_shift, 1)
                v.wait_ge(s_cscore_exp, t + 1)
                link(v.tensor_tensor(s16, s16, cm[:, t].unsqueeze(1).to_broadcast([128, 16, 8]), ALU.mult))
                link(v.tensor_reduce(smc, s16, AX, ALU.add))
                link(v.tensor_scalar_max(smc, smc, 1e-30))
                link(v.reciprocal(smc, smc))
                gv = vP[:, t, 512:560].rearrange("p (g k r b) -> p g k r b", g=2, k=2, r=4)
                for gp in range(2):
                    for k in range(2):
                        mv = smc.rearrange("p (g r k) -> p g r k", g=2, k=2)[:, gp, :, k]
                        ins = v.tensor_tensor(mv, mv, gv[:, gp, k, :, 0], ALU.mult)
                link(ins)
                v.tensor_tensor(s16, s16, smc.unsqueeze(2).to_broadcast([128, 16, 8]), ALU.mult).then_inc(s_cprob_ready, 1)
            v.wait_ge(s_cprob_turned, 1)
            v.tensor_copy(PTc[:], ps[:, 5, 0:256].rearrange("p (t n) -> p t n", t=2)).then_inc(s_cprobT_ready, 1)
            for i in range(35):
                if i < 32:
                    t = i // 16
                    w = 128 * (t + 1)
                    Sv = Ssb[:, i % 3, 0:2 * w].rearrange("p (k n) -> p k n", k=2)
                    mx, nm = small[:, 8 * (i % 3):8 * (i % 3) + 2], small[:, 8 * (i % 3) + 2:8 * (i % 3) + 4]
                    v.wait_ge(s_scores_done, i + 1)
                    if i >= 3:
                        v.wait_ge(s_probs_turned, i - 2)
                    v.tensor_tensor(Sv, ps[:, i % 3, 0:2 * w].rearrange("p (k n) -> p k n", k=2),
                                    C("causal")[:, 256 - w:256].unsqueeze(1).to_broadcast([128, 2, w]), ALU.add
                                    ).then_inc(s_scores_taken, 1)
                    v.wait_ge(s_scores_taken, i + 1)
                    link(v.tensor_reduce(mx, Sv, AX, ALU.max))
                    v.tensor_scalar_mul(nm, mx, -SCALE).then_inc(s_negmax_ready, 1)
                if 1 <= i < 33:
                    u = i - 1
                    t, hh = u // 16, u % 16
                    gp, r, g2 = hh // 8, (hh // 2) % 4, hh % 2
                    w = 128 * (t + 1)
                    Sv = Ssb[:, u % 3, 0:2 * w].rearrange("p (k n) -> p k n", k=2)
                    sm, rg = small[:, 8 * (u % 3) + 4:8 * (u % 3) + 6], small[:, 8 * (u % 3) + 6:8 * (u % 3) + 8]
                    v.wait_ge(s_exp_ready, 2 * (u + 1))
                    link(v.reciprocal(rg, sm))
                    h = gp * 8 + g2 * 4 + r
                    link(v.tensor_tensor(rg, rg, vP[:, t, 512 + 3 * h + 1:512 + 3 * h + 3], ALU.mult))
                    v.tensor_tensor(Sv, Sv, rg.unsqueeze(2).to_broadcast([128, 2, w]), ALU.mult).then_inc(s_probs_ready, 1)
                if i >= 3 and (i - 3) % 2 == 1:
                    u = i - 3
                    t, c = u // 16, (u % 16) // 2
                    v.wait_ge(s_pv_done, u + 1)
                    v.tensor_copy(oT[:, c, 128 * t:128 * t + 128], ps[:, 5 + (u // 2) % 2, 0:128]).then_inc(s_o_taken, 1)

            def take_keys(tau):
                j = j_keys(tau)
                for b2 in range(2):
                    if tau >= 2:
                        v.wait_ge(s_seq_scores, 2 * (tau - 2) + b2 + 1)
                    for q in range(4):
                        if (j + 4 * b2 + q) % 2 == 1:
                            take(j + 4 * b2 + q, TS[:, tau % 2, b2, q // 2, 512 * (q % 2):512 * (q % 2) + 512])
                for q in range(4):
                    if (j + 8 + q) % 2 == 1:
                        take(j + 8 + q, TW[:, tau % 2, q // 2, q % 2, :])

            take_keys(0)
            for tau in range(4):
                nm_ = C("newmask").rearrange("p (t n) -> p t n", t=4)[:, tau]
                v.wait_ge(s_group_scores, tau + 1)
                v.tensor_tensor(SS[:, 0:1024].rearrange("p (j n) -> p j n", j=16),
                                ps[:, 0:2, :].rearrange("p a (j n) -> p (a j) n", n=64),
                                selneg[:, tau, 0:16].unsqueeze(2).to_broadcast([128, 16, 64]), ALU.add)
                v.scalar_tensor_tensor(out=SS[:, 1024:1056], in0=ps[:, 3, 0:32], scalar=selneg[:, tau, 16:17], in1=nm_,
                                       op0=ALU.add, op1=ALU.add)
                v.tensor_copy(SS[:, 1060:1568], ps[:, 2, 4:512])
                v.tensor_tensor(SS[:, 1056:1060], ps[:, 2, 0:4], C("winmask"), ALU.add)
                link(v.tensor_tensor(SS[:, 1568:1600], ps[:, 3, 32:64], nm_, ALU.add))
                v.tensor_reduce(small[:, 36:37], SS[:, 0:1056], AX, ALU.max)
                link(v.tensor_reduce(small[:, 37:38], SS[:, 1056:1600], AX, ALU.max))
                v.tensor_scalar_mul(small[:, 38:40], small[:, 36:38], -SCALE).then_inc(s_snegmax, 1)
                if tau < 3:
                    take_keys(tau + 1)
                v.wait_ge(s_sexp_ready, 2 * (tau + 1))
                link(v.reciprocal(small[:, 42:44], small[:, 40:42]))
                link(v.tensor_tensor(small[:, 42:44], small[:, 42:44], grow[:, tau, 1:3], ALU.mult))
                v.tensor_scalar(SS[:, 0:1056], SS[:, 0:1056], small[:, 42:43], None, ALU.mult)
                v.tensor_scalar(SS[:, 1056:1600], SS[:, 1056:1600], small[:, 43:44], None, ALU.mult).then_inc(s_group_probs, 1)
                if tau:
                    v.wait_ge(s_group_pv, tau)
                take(j_probs(tau) + 1, PT[:, 4:8, :])
                take(j_probs(tau) + 3, PT[0:32, 12:15, :])
                v.wait_ge(s_group_pv, tau + 1)
                v.tensor_copy(osb, ps[:, 7, 0:128]).then_inc(s_osb_ready, 1)
                v.wait_ge(s_osb_turned, tau + 1)
                for g2 in range(2):
                    for gp in range(2):
                        for b2 in range(2):
                            p_ = slice(64 * g2, 64 * g2 + 64)
                            c0 = 128 + b2 * 64 + gp * 32 + g2 * 16
                            t0 = SEQ + (2 * tau + b2) * NT
                            ins = v.tensor_copy(oT[p_, 4 * gp:4 * gp + 4, t0:t0 + NT],
                                                ps[p_, 7, c0:c0 + 16].rearrange("p (r t) -> p r t", t=NT))
                ins.then_inc(s_group_o, 1)

            def from_wo(c):
                v.wait_ge(s_wo_done, c + 1)
                return ps[:, c % 6, :]
            v.wait_ge(s_group_o, 4)
            residual(0, 2, from_wo)
            norm(1)
            for m in range(28):
                v.wait_ge(s_gexp_ready, m + 1)
                t_, g_ = sgF[:, m % 2, 0, :], sgF[:, m % 2, 1, :]
                link(v.tensor_scalar_add(t_, t_, 1.0))
                link(v.reciprocal(t_, t_))
                link(v.tensor_tensor(g_, t_, ps[:, 2 * (m % 3), 0:NTOK], ALU.mult))
                v.tensor_tensor(actF[:, m, :], g_, ps[:, 2 * (m % 3) + 1, 0:NTOK], ALU.mult).then_inc(s_act_ready, 1)

            def from_dn(c):
                v.wait_ge(s_down_done, c // 4 + 1)
                return ps[:, c, :]
            residual(0, 5, from_dn)
            norm(2)
            v.wait_ge(s_down_done, 2)
            link(v.memset(uP[:, :, 0:2], 0.0))
            v.wait_ge(s_state_turned, 1)
            link(v.tensor_copy(uS[:, :, :, 0:2], ps[:, 7, 0:128].rearrange("p (c b j) -> p c b j", c=8, b=8)))
            for c in range(DC):
                B = 12 * (c // 4) + 8 + c % 4
                v.wait_ge(s_conv_done, B + 1)
                v.wait_ge(s_conv_copied, 8 * (c // 4) + 4 + c % 4 + 1)
                v.tensor_tensor(uP[:, c, 2:258], ps[:, B % 6, 0:SEQ], cgT[:, c, 0:SEQ], ALU.mult)
                ins = v.tensor_tensor(uS[:, c, :, 2:6], ps[:, B % 6, SEQ:NTOK].rearrange("p (b t) -> p b t", t=NT),
                                      cgT[:, c, SEQ:].rearrange("p (b t) -> p b t", t=NT), ALU.mult)
                ins.then_inc(s_u_ready, 1)
                v.wait_ge(s_u_ready, c + 1)
                ct_ = ctmp[:, c % 2]
                cS = ct_[:, SEQ:].rearrange("p (b t) -> p b t", t=NT)
                v.tensor_scalar(ct_[:, 0:SEQ], uP[:, c, 0:SEQ], w_convT[:, 0, c:c + 1], None, ALU.mult)
                link(v.tensor_scalar(cS, uS[:, c, :, 0:NT], w_convT[:, 0, c:c + 1], None, ALU.mult))
                for j in (1, 2):
                    v.scalar_tensor_tensor(out=ct_[:, 0:SEQ], in0=uP[:, c, j:j + SEQ], scalar=w_convT[:, j, c:c + 1],
                                           in1=ct_[:, 0:SEQ], op0=ALU.mult, op1=ALU.add)
                    link(v.scalar_tensor_tensor(out=cS, in0=uS[:, c, :, j:j + NT], scalar=w_convT[:, j, c:c + 1],
                                                in1=cS, op0=ALU.mult, op1=ALU.add))
                v.tensor_tensor(zT[:, c, :], ct_, bgT[:, c, :], ALU.mult).then_inc(s_z_ready, 1)
            v.tensor_copy(tail[:, :, 0:2], uP[:, :, 256:258])
            for j in range(2):
                ins = v.tensor_copy(tail[:, :, 2:18].rearrange("p c (b j) -> p c b j", j=2)[:, :, :, j], uS[:, :, :, 4 + j])
            ins.then_inc(s_tail_ready, 1)
            for i in range(2):
                v.wait_ge(s_tail_turned, i + 1)
                v.tensor_copy(tailrow[:, 512 * i:512 * i + 512], ps[0:18, 6 + i, :]).then_inc(s_tail_rows, 1)

            def from_co(c):
                v.wait_ge(s_conv_done, 24 + c + 1)
                return ps[:, (24 + c) % 6, :]
            residual(1, 2, from_co)
            norm(3)
            v.wait_ge(s_logits_done, 1)
            v.wait_ge(s_tail_rows, 2)
            v.wait_ge(s_router_in, 32)
            v.wait_ge(s_tail_stored, 1)
            v.memset(nine, 0.0)
            link(v.memset(lg[:], 0.0))
            v.tensor_tensor(lg[:, 0:2, :], ps[:, 7, 0:16].rearrange("p (t e) -> p t e", t=2),
                            br[:].unsqueeze(1).to_broadcast([128, 2, 8]), ALU.add)
            link(v.tensor_tensor(lg[0:32, 2, :], ps[0:32, 7, 16:24], br[0:32, :], ALU.add))
            bef = C("before").rearrange("p (j i) -> p j i", j=17)[:, 0:8, 0:8]
            for t in range(3):
                li, lj = lg[:, t].unsqueeze(1).to_broadcast([128, 8, 8]), lg[:, t].unsqueeze(2).to_broadcast([128, 8, 8])
                v.tensor_tensor(rkA[:, t], li, lj, ALU.is_gt)
                link(v.tensor_tensor(rkB[:, t], li, lj, ALU.is_equal))
                ins = v.tensor_tensor(rkB[:, t], rkB[:, t], bef, ALU.mult)
            link(ins)
            link(v.tensor_tensor(rkA[:], rkA[:], rkB[:], ALU.add))
            link(v.tensor_reduce(selE, rkA[:], AX, ALU.add))
            link(v.tensor_scalar(selE, selE, 1.5, None, ALU.is_lt))
            v.tensor_tensor(selE, selE, C("valid").unsqueeze(2).to_broadcast([128, 3, 8]), ALU.mult).then_inc(s_sel_ready, 1)
            v.wait_ge(s_sel_ready, 1)
            link(v.tensor_reduce(mE[:, 0:3], lg[:], AX, ALU.max))
            v.tensor_tensor(lg[:], lg[:], mE[:, 0:3].unsqueeze(2).to_broadcast([128, 3, 8]), ALU.subtract).then_inc(s_logits_shift, 1)
            v.wait_ge(s_logits_exp, 1)
            link(v.tensor_tensor(cw, lg[:], selE, ALU.mult))
            link(v.tensor_reduce(mE[:, 4:7], cw, AX, ALU.add))
            link(v.tensor_scalar_max(mE[:, 4:7], mE[:, 4:7], 1e-30))
            link(v.reciprocal(mE[:, 8:11], mE[:, 4:7]))
            link(v.tensor_tensor(cw, cw, mE[:, 8:11].unsqueeze(2).to_broadcast([128, 3, 8]), ALU.mult))
            v.wait_ge(s_pos_done, 1)
            v.tensor_copy(pos, ps[:, 7, 32:56].rearrange("p (t e) -> p t e", t=3))
            link(v.tensor_reduce(mE[:, 12:13], ps[:, 7, 56:64], AX, ALU.max))
            v.tensor_copy(cnti[:], mE[0:1, 12:13]).then_inc(s_count_ready, 1)
            for i in range(6):
                v.wait_ge(s_rows_done, i + 1)
                t, h = i // 2, i % 2
                m = TOK[t][1]
                v.tensor_copy(hN[0:m, t, 512 * h:512 * h + 512], ps[0:m, i, :]).then_inc(s_rows_taken, 1)
            link(v.memset(yacc[:], 0.0))

            def matrices(rnd, e0, chain):
                n = 0
                for i, src in enumerate((posP, selP, cwP)):
                    ins = v.tensor_copy(cur[:, i, 0:3], src[:, :, bass.ds(e0, 1)].rearrange("p t o -> p (t o)"))
                ins.then_inc(s_moe_chain, 1)
                v.wait_ge(s_moe_chain, chain + 1)
                if rnd:
                    v.tensor_scalar_add(cur[:, 0, 0:3], cur[:, 0, 0:3], -float(SLOTS_E * rnd)).then_inc(s_moe_chain, 1)
                    v.wait_ge(s_moe_chain, chain + 2)
                for t in range(3):
                    ins = v.tensor_scalar(Dm[:, t, :], C("iota"), cur[:, 0, t:t + 1], cur[:, 1, t:t + 1],
                                          ALU.is_equal, ALU.mult)
                ins.then_inc(s_moe_chain, 1)
                v.wait_ge(s_moe_chain, chain + (3 if rnd else 2))
                for t in range(3):
                    ins = v.tensor_scalar(Dw[:, t, :], Dm[:, t, :], cur[:, 2, t:t + 1], None, ALU.mult)
                ins.then_inc(s_gather_ready, 1)

            def experts(rnd):
                L = 3 if rnd else 2
                base = {0: 0, 1: 18, 2: 45}[rnd]
                if rnd:
                    v.wait_ge(s_gather_ready, 9 * rnd)
                matrices(rnd, 0, base)
                with v.Fori(0, NE) as e0:
                    e = e0 + NE * rnd
                    for i in range(TILES_E):
                        v.wait_ge(s_split_hi, e * TILES_E + (i + 1))
                        v.tensor_tensor(wlo[:, i % SPLIT, :], ring[:, (T_MOE + i) % RING, :],
                                        whi[:, i % SPLIT, :].bitcast(F32), ALU.subtract).then_inc(s_used, 1)
                        if i == 2:
                            for h in range(2):
                                v.wait_ge(s_xt_hi, e * 2 + (h + 1))
                                v.tensor_tensor(XTl[:, 4 * h:4 * h + 4, :], ps[:, 4 + h, :].rearrange("p (c s) -> p c s", c=4),
                                                XTh[:, 4 * h:4 * h + 4, :].bitcast(F32), ALU.subtract).then_inc(s_xt_lo, 1)
                            v.wait_ge(s_gathered, e * 3 + 3)
                            v.tensor_copy(DT, ps[:, 6, 0:NTOK]).then_inc(s_scatter_ready, 1)
                            matrices(rnd, e0 + 1, e0 * L + (base + L))
                        if i % 4 == 2 and 6 <= i <= 30:
                            j = (i - 6) // 4
                            v.wait_ge(s_silu_ready, e * 7 + (j + 1))
                            if j >= 2:
                                v.wait_ge(s_eact_turned, e * 7 + (j - 1))
                            v.tensor_tensor(actM[:, j % 2, :], siluM[:], ps[:, 2 * (j % 2) + 1, :], ALU.mult
                                            ).then_inc(s_eact_ready, 1)
                        if i % 4 == 2 and 10 <= i <= 34:
                            j = (i - 10) // 4
                            v.wait_ge(s_eactT_hi, e * 7 + (j + 1))
                            v.tensor_tensor(actTl[:, 4 * j:4 * j + 4, :], ps[:, 4 + j % 2, :].rearrange("p (k s) -> p k s", k=4),
                                            actTh[:, 4 * j:4 * j + 4, :].bitcast(F32), ALU.subtract).then_inc(s_eactT_lo, 1)
                    v.wait_ge(s_tile_done, e * TILES_E + (TILES_E + SPLIT))
                    v.tensor_copy(ysb[:, 512:1024], ps[:, 7, :]).then_inc(s_y_dve, 1)
                    for c in range(DC):
                        v.wait_ge(s_share_done, e * 8 + (c + 1))
                        v.tensor_tensor(yacc[:, c, :], yacc[:, c, :], ps[:, c % 4, 0:NTOK], ALU.add).then_inc(s_share_added, 1)
                    v.wait_ge(s_share_added, e * 8 + 8)

            experts(0)
            c_ = v.value_load(cnti[0:1, 0:1], min_val=0, max_val=NTOK)
            for rnd in (1, 2):
                with v.If(c_ > SLOTS_E * rnd):
                    experts(rnd)
            residual(1, 5, lambda c: yacc[:, c, :])
            norm(4)
            for c in range(DC):
                ins = v.tensor_scalar(nT[:, c, :], nT[:, c, :], g_finT[:, c:c + 1], None, ALU.mult)
            ins.then_inc(s_final_ready, 1)
            for i in range(6):
                v.wait_ge(s_rows_done, 6 + i + 1)
                t, h = i // 2, i % 2
                m = TOK[t][1]
                v.tensor_copy(outN[0:m, t, 512 * h:512 * h + 512], ps[0:m, i, :]).then_inc(s_final_rows, 1)

        @block.tensor
        def _(pe):
            ident = C("ident")

            def mm(out, l, r, k, n, **kw):
                return pe.matmul(out, l, r, start=(k == 0), stop=(k == n - 1), **kw)

            used = Count(s_used)

            pe.wait_ge(s_consts_in, 16)
            pe.wait_ge(s_rows_in, 16 * 9)
            pe.wait_ge(s_csilu, 1)
            pe.transpose(ps[:, 7, 0:96], rowsA, ident[0:96, 0:96])
            pe.transpose(ps[:, 7, 96:160], rowsB, ident[0:64, 0:64])
            pe.transpose(ps[:, 7, 160:232], rowsC, ident[0:72, 0:72])
            pe.transpose(ps[:, 7, 232:264], rowsP[:, 0:128], ident[0:32, 0:32])
            pe.transpose(ps[:, 7, 264:296], rowsP[:, 128:256], ident[0:32, 0:32]).then_inc(s_rows_turned, 1)
            pe.wait_ge(s_x_in, 32)
            for c in range(DC):
                if c >= 4:
                    pe.wait_ge(s_x_ready, c - 3)
                for t, (t0, m) in enumerate(TOK):
                    ins = pe.transpose(ps[:, 2 + c % 4, t0:t0 + m], xrow[0:m, t, 128 * c:128 * c + 128], ident[0:m, 0:m])
                ins.then_inc(s_x_turned, 1)
            pe.wait_ge(s_rowsT_ready, 1)
            pe.wait_ge(s_x_ready, 8)

            def turn_mod(k):
                pe.wait_ge(s_modrow, k + 1)
                for b in range(4):
                    o = ((k % 12) * 4 + b) * 9
                    ins = pe.transpose(ps[:, 2 + k // 12, o:o + 9], modrow[:, k % 2, 128 * b:128 * b + 128], ident[0:9, 0:9])
                ins.then_inc(s_mod_turned, 1)

            for k in range(24):
                n = 2 * k
                if k >= 2:
                    pe.wait_ge(s_modrow, k - 1)
                for kc in range(8):
                    if kc % 4 == 0:
                        wait_tile(pe, n + kc // 4)
                    ins = mm(ps[0:9, k % 2, :], csT[:, :, kc], slot(n + kc // 4)[:, kc % 4, :], kc, 8)
                    if kc % 4 == 3:
                        ins.then_inc(s_used, 1)
                if k:
                    turn_mod(k - 1)
            turn_mod(23)

            def norm(n):
                for c in range(DC):
                    if n and c == 0:
                        pe.wait_ge(s_std_ready, n)
                    pe.wait_ge(s_sq_ready, 8 * n + c + 1)
                    ins = mm(ps[:, 6, 0:NTOK], C("ones"), nT[:, c, :], c, DC)
                ins.then_inc(s_ss_done, 1)

            def h_ready(n):
                pe.wait_ge(s_h_prompt, 8 * (n + 1))
                pe.wait_ge(s_h_sample, n + 1)

            norm(0)
            h_ready(0)
            pe.wait_ge(s_mod_ready, 2)
            for ct in range(6):
                n = T_NSA + 2 * ct
                last = ct == 5
                wait_tile(pe, n)
                if not last:
                    wait_tile(pe, n + 1)
                if ct >= 2:
                    pe.wait_ge(s_proj_dve, ct - 1)
                    pe.wait_ge(s_proj_act, ct - 1)
                for t, (t0, m) in enumerate(TOK):
                    for kc in range(8):
                        if last:
                            rhs, out = slot(n, 8)[:, kc, :], ps[0:m, 3 + t, 0:48]
                        else:
                            rhs, out = slot(n + kc // 4)[:, kc % 4, :], ps[0:m, 3 * (ct % 2) + t, :]
                        ins = mm(out, hT[:, kc, t0:t0 + m], rhs, kc, 8)
                        if t == 2 and kc == 3 and not last:
                            ins.then_inc(s_used, 1)
                ins.then_inc(s_proj_done, 1)
                pe.wait_ge(s_proj_done, ct + 1)
                pe.sem_inc(s_used, 1)
            cols = [128 * i for i in range(8)] + [1536, 1664, 2048, 2176, 1024, 1152, 1280, 1408]
            pe.wait_ge(s_rope_done, 6)
            pe.wait_ge(s_gate_exp, 3)
            for i, c0 in enumerate(cols):
                if i >= 6:
                    pe.wait_ge(s_qk_prompt, i - 5)
                    pe.wait_ge(s_qk_sample, min(i - 5, 12))
                for t, (t0, m) in enumerate(TOK if i < 12 else TOK[:2]):
                    ins = pe.transpose(ps[:, i % 6, t0:t0 + m], proj[0:m, t, c0:c0 + 128], ident[0:m, 0:m])
                ins.then_inc(s_qk_turned, 1)
            pe.wait_ge(s_wbd_in, 64)
            pe.wait_ge(s_tail_pe, 1)
            pe.wait_ge(s_qk_prompt, 16)
            pe.wait_ge(s_qk_sample, 12)
            jb = [0]

            def bank_free():
                j = jb[0]
                jb[0] += 1
                back = 4 if j < J_SEL else 3
                if j >= J_SEL + 3 or 4 <= j < J_SEL:
                    q = j - back
                    pe.wait_ge(s_bank_act if q % 2 == 0 else s_bank_dve, q // 2 + 1)
                return j % 4 if j < J_SEL else 4 + (j - J_SEL) % 3

            def copied():
                pe.wait_ge(s_bank_act, (jb[0] + 1) // 2)
                pe.wait_ge(s_bank_dve, jb[0] // 2)

            for kv in range(2):
                for half in range(2):
                    for b4 in range(4):
                        n = T_CACHE + 8 * kv + 4 * half + b4
                        wait_tile(pe, n)
                        for h in range(2):
                            for gp in range(2):
                                bk = bank_free()
                                for j in range(4):
                                    ins = pe.transpose(ps[:, bk, 128 * j:128 * j + 128],
                                                       pages(n)[:, 4 * h + j, 128 * gp:128 * gp + 128], ident)
                                ins.then_inc(s_bank_turned, 1)
                        pe.wait_ge(s_bank_turned, jb[0])
                        pe.sem_inc(s_used, 1)
                    copied()
                    lo = (TAIL if half or kv else 0)
                    nblk = 256 if half else 273
                    src = work[:, lo:lo + 32 * nblk].rearrange("p (n l) -> p n l", l=32)
                    for l in range(32):
                        ins = mm(ps[:, 4 + 2 * kv + half, 0:nblk], wbd[:, kv, l, :], src[:, :, l], l, 32)
                    ins.then_inc(s_cmp_done, 1)
            pe.wait_ge(s_craw_ready, 1)
            mm(ps[:, 1, 0:16], C("rot"), praw[:, 0], 0, 1)
            mm(ps[:, 0, :], C("rot"), kraw[:].rearrange("p h n -> p (h n)"), 0, 1)
            for gp in range(2):
                pe.transpose(ps[0:8, 1, 128 + 128 * gp:256 + 128 * gp], praw[:, 1, 8 * gp:8 * gp + 8], ident)
            for b in range(NB):
                for gp in range(2):
                    o = 128 * gp + 32 * (b % 4)
                    ins = pe.transpose(ps[0:32, 2 + b // 2, 256 * (b % 2) + 128 * gp:256 * (b % 2) + 128 * gp + 128],
                                       vraw[:, b // 4, o:o + 32], ident)
            ins.then_inc(s_rot_done, 1)
            pe.wait_ge(s_ck_ready, 1)
            mm(ps[:, 0, 0:256], C("repn", 8), cvn, 0, 1).then_inc(s_cv_spread, 1)
            for t in range(2):
                for hh in range(16):
                    c, g2 = hh // 2, hh % 2
                    p_ = slice(64 * g2, 64 * g2 + 64)
                    o = 256 + 64 * t + 8 * c
                    ins = mm(ps[:, 6 + g2, o:o + 8], qT[p_, c, 128 * t:128 * t + 128],
                             ckP[p_, 8 * (c // 4):8 * (c // 4) + 8], 0, 1)
            ins.then_inc(s_cscore_done, 1)
            for tau in range(4):
                for st in range(4):
                    b, gp = 2 * tau + st // 2, st % 2
                    o = (b // 4) * 256 + gp * 128 + (b % 4) * 32
                    mm(ps[32 * st:32 * st + 32, 1, 32 * tau:32 * tau + 32], qbd[:, b, 32 * gp:32 * gp + 32],
                       ckS[:, o:o + 32], 0, 1)
            for tau in range(4):
                ins = mm(ps[:, 1, 128 + 48 * tau:176 + 48 * tau], C("rowtok", 32)[:, 128 * tau:128 * tau + 128],
                         vP[0:32, 2, 512:560], 0, 1)
            ins.then_inc(s_sc_done, 1)
            pe.wait_ge(s_cprobs, 1)
            pe.wait_ge(s_cv_ready, 4)
            mm(ps[:, 2, 0:128], C("headsum"), PcG.rearrange("p t n -> p (t n)"), 0, 1).then_inc(s_importance, 1)
            for t in range(2):
                pe.wait_ge(s_cprob_ready, t + 1)
                ins = pe.transpose(ps[:, 5, 128 * t:128 * t + 128], ScP[:, t, :], ident)
            ins.then_inc(s_cprob_turned, 1)
            pe.wait_ge(s_cprobT_ready, 1)
            for i in range(35):
                if i < 32:
                    t, hh = i // 16, i % 16
                    c, g2 = hh // 2, hh % 2
                    p_ = slice(64 * g2, 64 * g2 + 64)
                    w = 128 * (t + 1)
                    if i >= 3:
                        pe.wait_ge(s_scores_taken, i - 2)
                    mm(ps[:, i % 3, 0:2 * w], qT[p_, c, 128 * t:128 * t + 128], kTp[p_, c // 4, :, 0:w], 0, 1
                       ).then_inc(s_scores_done, 1)
                if 2 <= i < 34:
                    u = i - 2
                    w = 128 * (u // 16 + 1)
                    pe.wait_ge(s_probs_ready, u + 1)
                    if u >= 2:
                        pe.wait_ge(s_probsT_ready, u - 1)
                    for k in range(2 * w // 128):
                        ins = pe.transpose(ps[:, 3 + u % 2, 128 * k:128 * k + 128],
                                           Ssb[:, u % 3, 128 * k:128 * k + 128], ident)
                    ins.then_inc(s_probs_turned, 1)
                if i >= 3:
                    u = i - 3
                    t, hh = u // 16, u % 16
                    c, g2 = hh // 2, hh % 2
                    bank = 5 + (u // 2) % 2
                    pe.wait_ge(s_probsT_ready, u + 1)
                    if g2 == 0:
                        if u >= 4:
                            pe.wait_ge(s_o_taken, u // 2 - 1)
                        pe.matmul(ps[:, bank, 0:128], Vbd[:, c, :], PTc[:, t, :], start=True, stop=False,
                                  skip_group_check=True)
                    g_ = 2 * (c // 4) + g2
                    for k in range(2):
                        for kt in range(t + 1):
                            c0 = 256 * k + 64 * g_
                            ins = pe.matmul(ps[64 * g2:64 * g2 + 64, bank, 0:128], vP[:, kt, c0:c0 + 64],
                                            PTs[:, u % 2, (k * (t + 1) + kt) * 128:(k * (t + 1) + kt) * 128 + 128],
                                            start=False, stop=(k == 1 and kt == t), skip_group_check=True)
                    ins.then_inc(s_pv_done, 1)
            pe.wait_ge(s_o_taken, 16)

            def turn_keys(tau):
                for i in range(3):
                    n = tile_k[tau] + i
                    wait_tile(pe, n)
                    for q in range(4):
                        bk = bank_free()
                        for j in range(4):
                            page, gp = (4 * (q % 2) + j, q // 2) if i < 2 else (4 * (q // 2) + j, q % 2)
                            ins = pe.transpose(ps[:, bk, 128 * j:128 * j + 128],
                                               pages(n)[:, page, 128 * gp:128 * gp + 128], ident)
                        ins.then_inc(s_bank_turned, 1)
                    pe.wait_ge(s_bank_turned, jb[0])
                    pe.sem_inc(s_used, 1)

            def turn_out(tau):
                pe.wait_ge(s_osb_ready, tau + 1)
                pe.transpose(ps[:, 7, 128:256], osb, ident).then_inc(s_osb_turned, 1)

            turn_keys(0)
            for tau in range(4):
                copied()
                if tau:
                    pe.wait_ge(s_snegmax, tau)
                for b2 in range(2):
                    b = 2 * tau + b2
                    for gp in range(2):
                        o_ = slice(32 * (2 * b2 + gp), 32 * (2 * b2 + gp) + 32)
                        q_ = qbd[:, b, 32 * gp:32 * gp + 32]
                        mm(ps[o_, 3, 0:32], q_, kTn[:, gp, 0, :], 0, 1)
                        mm(ps[o_, 3, 32:64], q_, kTn[:, gp, 1, :], 0, 1)
                        mm(ps[o_, 0, :], q_, TS[:, tau % 2, b2, gp, 0:512], 0, 1)
                        mm(ps[o_, 1, :], q_, TS[:, tau % 2, b2, gp, 512:1024], 0, 1)
                        ins = mm(ps[o_, 2, :], q_, TW[:, tau % 2, b2, gp, :], 0, 1)
                    ins.then_inc(s_seq_scores, 1)
                pe.wait_ge(s_seq_scores, 2 * tau + 2)
                pe.sem_inc(s_group_scores, 1)
                if tau:
                    turn_out(tau - 1)
                if tau < 3:
                    turn_keys(tau + 1)
                pe.wait_ge(s_group_probs, tau + 1)
                for i in range(3):
                    bk = bank_free()
                    for k in range(4):
                        c0 = (0, 512, 1056)[i] + 128 * k
                        ins = pe.transpose(ps[:, bk, 128 * k:128 * k + 128], SS[:, c0:c0 + 128], ident)
                    ins.then_inc(s_bank_turned, 1)
                bk = bank_free()
                for k, src in enumerate((SS[:, 1024:1056], SS[:, 1568:1600], PcG[:, tau, :])):
                    ins = pe.transpose(ps[0:32, bk, 128 * k:128 * k + 128], src, ident)
                ins.then_inc(s_bank_turned, 1)
                copied()
                if tau:
                    pe.wait_ge(s_group_o, tau)
                for i in range(3):
                    wait_tile(pe, tile_v[tau] + i)
                for st in range(4):
                    b2, gp = st // 2, st % 2
                    m_ = slice(32 * st, 32 * st + 32)
                    c_ = slice(128 * gp, 128 * gp + 128)
                    for k in range(12):
                        val = pages(tile_v[tau] + b2)[:, k, c_] if k < 8 else pages(tile_v[tau] + 2)[:, 4 * b2 + k - 8, c_]
                        mm(ps[m_, 7, 0:128], PT[:, k, m_], val, k, 15)
                    for k, val in ((12, vP[0:32, 2, c_]), (13, vP[0:32, 2, 256 + 128 * gp:384 + 128 * gp]),
                                   (14, cvS[:, 2 * tau + b2, c_])):
                        ins = mm(ps[m_, 7, 0:128], PT[0:32, k, m_], val, k, 15)
                ins.then_inc(s_group_pv, 1)
                pe.wait_ge(s_group_pv, tau + 1)
                pe.sem_inc(s_used, 3)
            turn_out(3)
            pe.wait_ge(s_group_o, 4)

            def dense(n, mov, out, done, ntile=2):
                wait_tile(pe, n)
                wait_tile(pe, n + 1)
                for b in range(4):
                    o = out(b)
                    for kc in range(8):
                        ins = mm(o, slot(n + kc // 4)[:, kc % 4, 128 * b:128 * b + 128], mov(kc), kc, 8)
                        if b == 3 and kc == 3:
                            ins.then_inc(s_used, 1)
                    ins.then_inc(done, 1)
                    nd[done] = nd.get(done, 0) + 1
                pe.wait_ge(done, nd[done])
                pe.sem_inc(s_used, 1)

            nd = {}

            def wo_bank(ch):
                def f(b):
                    c = 4 * ch + b
                    if c >= 6:
                        pe.wait_ge(s_x_ready, 8 + c - 5)
                    return ps[:, c % 6, 0:NTOK]
                return f
            for ch in range(2):
                dense(T_WO + 2 * ch, lambda kc: oT[:, kc, :], wo_bank(ch), s_wo_done)
            norm(1)
            h_ready(1)
            for j in range(7):
                n = T_FU + 4 * j
                for i in range(4):
                    wait_tile(pe, n + i)
                for b in range(4):
                    m = 4 * j + b
                    if m >= 3:
                        pe.wait_ge(s_act_ready, m - 2)
                    for u in range(2):
                        for kc in range(8):
                            ins = mm(ps[:, 2 * (m % 3) + u, 0:NTOK],
                                     slot(n + 2 * u + kc // 4)[:, kc % 4, 128 * b:128 * b + 128], hT[:, kc, :], kc, 8)
                            if b == 3 and kc % 4 == 3 and (u, kc) != (1, 7):
                                ins.then_inc(s_used, 1)
                    ins.then_inc(s_gu_done, 1)
                pe.wait_ge(s_gu_done, 4 * j + 4)
                pe.sem_inc(s_used, 1)
            pe.wait_ge(s_act_ready, 28)
            for ch in range(2):
                for i in range(7):
                    n = T_FD + 7 * ch + i
                    wait_tile(pe, n)
                    for kc in range(4):
                        m = 4 * i + kc
                        for b in range(4):
                            ins = mm(ps[:, 4 * ch + b, 0:NTOK], slot(n)[:, kc, 128 * b:128 * b + 128], actF[:, m, :], m, 28)
                    if i < 6:
                        ins.then_inc(s_used, 1)
                    else:
                        ins.then_inc(s_down_done, 1)
                        pe.wait_ge(s_down_done, ch + 1)
                        pe.sem_inc(s_used, 1)
            pe.wait_ge(s_x_ready, 24)
            norm(2)
            h_ready(2)
            pe.wait_ge(s_state_in, 16)
            for c in range(DC):
                ins = pe.transpose(ps[:, 7, 16 * c:16 * c + 16], strow[:, 128 * c:128 * c + 128], ident[0:16, 0:16])
            ins.then_inc(s_state_turned, 1)

            def ci_bank(B0):
                def f(b):
                    B = B0 + b
                    if B >= 6:
                        q = B - 6
                        if q >= 24:
                            pe.wait_ge(s_x_ready, 24 + q - 24 + 1)
                        elif (q // 4) % 3 < 2:
                            pe.wait_ge(s_conv_copied, 8 * (q // 12) + 4 * ((q // 4) % 3) + q % 4 + 1)
                        else:
                            pe.wait_ge(s_u_ready, 4 * (q // 12) + q % 4 + 1)
                    return ps[:, B % 6, 0:NTOK]
                return f
            for k in range(6):
                dense(T_CI + 2 * k, lambda kc: hT[:, kc, :], ci_bank(4 * k), s_conv_done)
            pe.wait_ge(s_z_ready, 8)
            dense(T_CO, lambda kc: zT[:, kc, :], ci_bank(24), s_conv_done)
            pe.wait_ge(s_tail_ready, 1)
            for c in range(DC):
                ins = pe.transpose(ps[0:18, 6 + c // 4, 128 * (c % 4):128 * (c % 4) + 128], tail[:, c, :], ident)
                if c % 4 == 3:
                    ins.then_inc(s_tail_turned, 1)
            dense(T_CO + 2, lambda kc: zT[:, kc, :], ci_bank(28), s_conv_done)
            pe.wait_ge(s_tail_rows, 2)
            norm(3)
            h_ready(3)
            pe.wait_ge(s_router_in, 32)
            for t, (t0, m) in enumerate(TOK):
                for kc in range(DC):
                    ins = mm(ps[0:m, 7, 8 * t:8 * t + 8], hT[:, kc, t0:t0 + m], wr[:, kc, :], kc, DC)
            ins.then_inc(s_logits_done, 1)

            def to_tokens(src, base):
                for i in range(6):
                    t, h = i // 2, i % 2
                    t0, m = TOK[t]
                    for q in range(4):
                        ins = pe.transpose(ps[0:m, i, 128 * q:128 * q + 128], src[:, 4 * h + q, t0:t0 + m], ident)
                    ins.then_inc(s_rows_done, 1)
            pe.wait_ge(s_x_ready, 32)
            to_tokens(hT, 0)
            pe.wait_ge(s_sel_ready, 1)
            for t in range(3):
                for k in range(t):
                    mm(ps[:, 7, 32 + 8 * t:40 + 8 * t], C("ones"), selE[:, k, :], k, t + 1)
                mm(ps[:, 7, 32 + 8 * t:40 + 8 * t], C("earlier"), selE[:, t, :], t, t + 1)
            for t in range(3):
                ins = mm(ps[:, 7, 56:64], C("ones"), selE[:, t, :], t, 3)
            ins.then_inc(s_pos_done, 1)
            pe.wait_ge(s_rows_taken, 6)
            pe.wait_ge(s_count_ready, 1)

            for _ in range(SPLIT):
                pe.sem_inc(s_tile_done, 1)

            def experts(rnd):
                with pe.Fori(0, NE) as e0:
                    e = e0 + NE * rnd
                    pe.wait_ge(s_gather_ready, e0 + (9 * rnd + 1))
                    for h in range(2):
                        for c in range(4 * h, 4 * h + 4):
                            for t, (_, m) in enumerate(TOK):
                                ins = mm(ps[:, 4 + h, 128 * (c % 4):128 * (c % 4) + 128],
                                         hN[0:m, t, 128 * c:128 * c + 128], Dm[0:m, t, :], t, 3)
                        ins.then_inc(s_gathered, 1)
                    for t, (t0, m) in enumerate(TOK):
                        ins = pe.transpose(ps[:, 6, t0:t0 + m], Dw[0:m, t, :], ident[0:m, 0:m])
                    ins.then_inc(s_gathered, 1)

                    def split_wait(i):
                        pe.wait_ge(s_used, e * TILES_E + (T_MOE + i + 1))

                    def turn(j):
                        pe.wait_ge(s_eact_ready, e * 7 + (j + 1))
                        if j >= 2:
                            pe.wait_ge(s_eactT_lo, e * 7 + (j - 1))
                        for q in range(4):
                            ins = pe.transpose(ps[:, 4 + j % 2, 128 * q:128 * q + 128],
                                               actM[:, j % 2, 128 * q:128 * q + 128], ident)
                        ins.then_inc(s_eact_turned, 1)
                    for j in range(7):
                        if j >= 2:
                            pe.wait_ge(s_eact_ready, e * 7 + (j - 1))
                        for u in range(2):
                            out = ps[:, 2 * (j % 2) + u, :]
                            for kc in range(8):
                                i = 4 * j + 2 * u + kc // 4
                                if kc % 4 == 0:
                                    split_wait(i)
                                if i < 2 and kc % 4 == 0:
                                    pe.wait_ge(s_xt_lo, e * 2 + (i + 1))
                                hi = whi[:, i % SPLIT, 512 * (kc % 4):512 * (kc % 4) + 512]
                                lo = wlo[:, i % SPLIT, 512 * (kc % 4):512 * (kc % 4) + 512]
                                pe.matmul(out, XTh[:, kc, :], hi, start=kc == 0, stop=False)
                                pe.matmul(out, XTh[:, kc, :], lo, start=False, stop=False)
                                ins = pe.matmul(out, XTl[:, kc, :], hi, start=False, stop=kc == 7)
                                if kc % 4 == 3:
                                    ins.then_inc(s_tile_done, 1)
                        if j:
                            turn(j - 1)
                    pe.wait_ge(s_scatter_ready, e + 1)
                    for i in range(14):
                        if i == 4:
                            turn(6)
                        split_wait(28 + i)
                        hi = whi[:, (28 + i) % SPLIT, :].rearrange("p (k n) -> p k n", k=2)
                        lo = wlo[:, (28 + i) % SPLIT, :].rearrange("p (k n) -> p k n", k=2)
                        for kk in range(2):
                            k = 2 * i + kk
                            if k % 4 == 0:
                                pe.wait_ge(s_eactT_lo, e * 7 + (k // 4 + 1))
                            for a_, w_, first, last in ((actTh, hi, True, False), (actTh, lo, False, False),
                                                        (actTl, hi, False, True)):
                                for h in range(2):
                                    ins = pe.matmul(ps[:, 6 + h, :], a_[:, k, :], w_[:, kk, 512 * h:512 * h + 512],
                                                    start=first and k == 0, stop=last and k == 27)
                        ins.then_inc(s_tile_done, 1)
                    pe.wait_ge(s_y_act, e + 1)
                    pe.wait_ge(s_y_dve, e + 1)
                    for c in range(DC):
                        if c >= 4:
                            pe.wait_ge(s_share_added, e * 8 + (c - 3))
                        mm(ps[:, c % 4, 0:NTOK], ysb[:, 128 * c:128 * c + 128], DT, 0, 1).then_inc(s_share_done, 1)
                    pe.wait_ge(s_share_added, e * 8 + 8)

            experts(0)
            c_ = pe.value_load(cnti[0:1, 0:1], min_val=0, max_val=NTOK)
            for rnd in (1, 2):
                with pe.If(c_ > SLOTS_E * rnd):
                    experts(rnd)
            norm(4)
            pe.wait_ge(s_final_ready, 1)
            to_tokens(nT, 6)


def constants():
    import numpy as np
    t = {n: np.zeros((128, w), np.float32) for n, w in CONSTS}
    p = np.arange(128)
    t["ident"][:] = np.eye(128)
    t["causal"][:, 128:] = np.where(p[None, :] <= p[:, None], 0.0, -BIG)
    d = p % 64
    for q in range(128):
        if d[q] < 8:
            t["rot"][q + 8, q] = -1.0
        elif d[q] < 16:
            t["rot"][q - 8, q] = 1.0
    inv = (1.0 / (np.float32(500000.0) ** (np.arange(8, dtype=np.float32) * np.float32(2.0 / 16)))).astype(np.float32)
    cend = (np.arange(32) * 32 + 31).astype(np.float32)
    ang = (cend[:, None] * inv[None, :]).astype(np.float32)
    for q in range(128):
        if d[q] < 16:
            t["ckcos"][q] = np.cos(ang[:, d[q] % 8])
            t["cksin"][q] = np.sin(ang[:, d[q] % 8])
        else:
            t["ckcos"][q] = 1.0
    posn = np.stack([p, 128 + p, 1024 + p % 4], 1).astype(np.float32)
    ang = (posn[:, :, None] * inv).astype(np.float32)
    t["tcos"][:] = np.cos(ang).reshape(128, 24)
    t["tsin"][:] = np.sin(ang).reshape(128, 24)
    ce = np.arange(8) * 32 + 31
    for k in range(2):
        vis = ce[None, :] <= (128 * k + p)[:, None]
        t["cmpadd"][:, 8 * k:8 * k + 8] = np.where(vis, 0.0, -BIG)
        t["cmpmul"][:, 8 * k:8 * k + 8] = vis
    b2, gp, g2, r, tt = p // 64, (p // 32) % 2, (p // 16) % 2, (p // 4) % 4, p % 4
    key = (b2 * 2 + gp) * 8 + g2 * 4 + tt
    t["headsum"][:] = key[:, None] == key[None, :]
    t["bonus"][:, 0] = 5.0
    t["bonus"][:, 16] = 5.0
    t["winmask"][:] = np.where(np.arange(4)[None, :] >= tt[:, None], 0.0, -BIG)
    n = np.arange(32)
    for tau in range(4):
        ok = (n[None, :] // 4 == (2 * tau + b2)[:, None]) & (n[None, :] % 4 <= tt[:, None])
        t["newmask"][:, 32 * tau:32 * tau + 32] = np.where(ok, 0.0, -BIG)
        t["rowtok"][0:32, 128 * tau:128 * tau + 128] = n[:, None] == ((2 * tau + b2) * 4 + tt)[None, :]
    t["rowhead"][:] = np.arange(16)[None, :] == (gp * 8 + g2 * 4 + r)[:, None]
    j = np.arange(17)
    t["before"][:] = (j[None, :] < j[:, None]).reshape(1, 289)
    t["repn"][0:8, :] = np.arange(8)[:, None] == (p % 8)[None, :]
    for c in range(8):
        for g in range(2):
            t["vbdmask"][:, 2 * c + g] = (p // 8) == (2 * c + g)
    t["earlier"][:] = p[:, None] < p[None, :]
    t["ones"][:] = 1.0
    t["iota"][:] = p[None, :]
    t["valid"][:, 0:2] = 1.0
    t["valid"][0:32, 2] = 1.0
    t["eps"][:] = EPS
    return np.concatenate([t[n] for n, _ in CONSTS], 1)


_INS = ["x_prompt", "x_sample", "cache_cmp_kv", "cache_sel_kv", "cache_win_kv", "state_conv", "page_table", "c_prompt",
        "c_sample", "w_ada", "b_ada", "g_norm_mix", "g_norm_ffn", "g_norm_final", "w_nsa_in", "w_nsa_out", "w_cmp_k",
        "pe_cmp_k", "w_cmp_v", "pe_cmp_v", "w_conv_in", "w_conv", "w_conv_out", "w_ff_gu", "w_ff_down", "w_router",
        "b_router", "w_moe_gu", "w_moe_down"]
_OUTS = [(1, 256, 1024), (8, 4, 1024), (1, 1, 256, 2, 4, 64), (1, 8, 4, 2, 4, 64), (1, 1, 256, 2, 4, 64),
         (1, 8, 4, 2, 4, 64), (1, 1, 256, 2, 4, 64), (1, 8, 512, 2, 4, 64), (1, 1, 2, 1024), (1, 8, 2, 1024)]


def kernel(**inputs):
    import numpy as _np
    import concourse.bacc as _bacc
    from concourse.bass_utils import run_bass_kernel_spmd as _run

    nc = _bacc.Bacc("TRN2", target_bir_lowering=False, num_devices=1)
    arrays, A = {}, {}
    for name in _INS + ["consts"]:
        a = constants() if name == "consts" else _np.ascontiguousarray(inputs[name])
        arrays[f"in_{name}"] = a
        A[name] = nc.dram_tensor(f"in_{name}", a.shape, mybir.dt.from_np(a.dtype), kind="ExternalInput").ap()
    O = [nc.dram_tensor(f"out_{i}", sh, F32, kind="ExternalOutput").ap() for i, sh in enumerate(_OUTS)]
    trunk(nc, A, O)
    r = _run(nc, [arrays], core_ids=[0])
    return tuple(r.results[0][f"out_{i}"] for i in range(len(_OUTS)))
```

```python
from contextlib import ExitStack

import concourse.bass as bass
from concourse import mybir

F32 = mybir.dt.float32
F32R = mybir.dt.float32r
I32 = mybir.dt.int32
ALU = mybir.AluOpType
ACT = mybir.ActivationFunctionType
AX = mybir.AxisListType.X

D = 1024
DC = D // 128
SEQ = 256
NB, NT = 8, 4
NTOK = SEQ + NB * NT
HD = 64
FF = 3584
NE = 8
KVW = 256
PROJ = 2560
TAIL = 544
SCALE = HD ** -0.5
BIG = 1.0e30
EPS = 1e-6
RING = 6
SLOT = 2048
SLOTS_E = 128
TILES_E = 42
SPLIT = 3
SPLIT_F = 2
TILES_A = 48
TILES_F = 42
SPLIT_AT_F = TILES_A
SPLIT_AT_C = TILES_A + TILES_F
TILES_C = 16
SPLIT_AT_M = SPLIT_AT_C + TILES_C
TOK = [(0, 128), (128, 128), (256, 32)]

CONSTS = [("ident", 128), ("causal", 256), ("rot", 128), ("ckcos", 32), ("cksin", 32), ("tcos", 24), ("tsin", 24),
          ("cmpadd", 16), ("cmpmul", 16), ("headsum", 128), ("bonus", 17), ("winmask", 4), ("newmask", 128),
          ("rowtok", 512), ("rowhead", 16), ("before", 289), ("repn", 128), ("vbdmask", 16), ("earlier", 128),
          ("ones", 128), ("iota", 128), ("valid", 3), ("eps", 1), ("fold", 9)]
AT = {}
_o = 0
for _n, _w in CONSTS:
    AT[_n] = (_o, _w)
    _o += _w
NCONST = _o


class Count:

    def __init__(self, sem):
        self.sem, self.n = sem, 0

    def inc(self, ins):
        ins.then_inc(self.sem, 1)
        self.n += 1

    def wait(self, eng):
        eng.wait_ge(self.sem, self.n)


def trunk(nc, A, O):
    with ExitStack() as ctx:
        def sb(name, shape, dt=F32):
            return ctx.enter_context(nc.sbuf_tensor(name, shape, dt))

        def sem(name):
            return ctx.enter_context(nc.semaphore(name))

        ps = ctx.enter_context(nc.psum_tensor("ps", [128, 8, 512], F32))
        ring = sb("ring", [128, RING, SLOT])
        con = sb("con", [128, NCONST])
        xT = sb("xT", [128, DC, NTOK])
        hT = sb("hT", [128, DC, NTOK])
        oT = hT
        nT = sb("nT", [128, DC, NTOK])
        std = sb("std", [128, NTOK])
        rstd = std
        modT = sb("modT", [128, 2, 6, DC, 9])
        rowsT = sb("rowsT", [128, 296])
        small = sb("small", [128, 128])
        pgt = sb("pgt", [1, 64], I32)
        cnti = sb("cnti", [1, 1], I32)
        wr = sb("wr", [128, DC, 8])
        br = sb("br", [128, 8])

        ada_ctx = ExitStack()

        def ada_sb(name, shape, dt=F32R):
            return ada_ctx.enter_context(nc.sbuf_tensor(name, shape, dt))

        ada_sb("rows_place", [128, 5120], F32)
        csHL = ada_sb("csHL", [128, DC, 18])
        ahi = ada_sb("ahi", [128, SPLIT, SLOT])
        alo = ada_sb("alo", [128, SPLIT, SLOT])
        ada_ctx.close()

        early = ExitStack()

        def early_sb(name, shape):
            return early.enter_context(nc.sbuf_tensor(name, shape, F32))

        work = early_sb("work", [128, 17472])
        qT = early_sb("qT", [128, 8, SEQ])
        kTp = early_sb("kTp", [128, 2, 2, SEQ])
        qbd = early_sb("qbd", [128, NB, 64])
        kTn = early_sb("kTn", [128, 2, 2, 32])
        vP = early_sb("vP", [128, 3, 560])
        ckS = early_sb("ckS", [128, 512])
        smp = early_sb("smp", [128, 320])
        attn = early_sb("attn", [128, 1632 + 15 * 128])
        early.close()

        dense_ctx = ExitStack()

        def dense_sb(name, shape, dt=F32R):
            return dense_ctx.enter_context(nc.sbuf_tensor(name, shape, dt))

        hTh = dense_sb("hTh", [128, DC, NTOK])
        hTl = dense_sb("hTl", [128, DC, NTOK])
        actFh = dense_sb("actFh", [128, 28, NTOK])
        actFl = dense_sb("actFl", [128, 28, NTOK])
        fhi = dense_sb("fhi", [128, SPLIT_F, SLOT])
        flo = dense_sb("flo", [128, SPLIT_F, SLOT])
        dense_ctx.close()

        conv_ctx = ExitStack()

        def conv_sb(name, shape, dt=F32R):
            return conv_ctx.enter_context(nc.sbuf_tensor(name, shape, dt))

        conv_sb("conv_place", [128, 8352], F32)
        cTh = conv_sb("cTh", [128, DC, NTOK])
        cTl = conv_sb("cTl", [128, DC, NTOK])
        zTh = conv_sb("zTh", [128, DC, NTOK])
        zTl = conv_sb("zTl", [128, DC, NTOK])
        chi = conv_sb("chi", [128, SPLIT_F, SLOT])
        clo = conv_sb("clo", [128, SPLIT_F, SLOT])
        convrows = conv_sb("convrows", [18, 2048], F32)
        conv_ctx.close()

        hN = sb("hN", [128, 3, D])
        XTh = sb("XTh", [128, DC, 128], F32R)
        XTl = sb("XTl", [128, DC, 128], F32R)
        actM = sb("actM", [128, 2, 512])
        siluM = sb("siluM", [128, 512])
        actTh = sb("actTh", [128, 28, 128], F32R)
        actTl = sb("actTl", [128, 28, 128], F32R)
        whi = sb("whi", [128, SPLIT, SLOT], F32R)
        wlo = sb("wlo", [128, SPLIT, SLOT], F32R)
        route = sb("route", [128, 552])

        def C(name, p=128):
            o, w = AT[name]
            return con[0:p, o:o + w]

        b_adaT = rowsT[:, 0:96].rearrange("p (l c) -> p l c", l=2)
        g_mixT = rowsT[:, 96:112].rearrange("p (l c) -> p l c", l=2)
        g_ffnT = rowsT[:, 112:128].rearrange("p (l c) -> p l c", l=2)
        g_finT = rowsT[:, 128:136]
        w_convT = rowsT[:, 136:160].rearrange("p (j c) -> p j c", j=3)
        csT = rowsT[:, 160:232].rearrange("p (s c) -> p s c", s=9)
        peT = rowsT[:, 232:296].rearrange("p (k l) -> p k l", k=2)

        xrow = work[:, 0:3072].rearrange("p (t d) -> p t d", t=3)
        rowsA = work[0:96, 3072:3200]
        rowsB = work[0:64, 3200:3328]
        rowsC = work[0:72, 3328:3456]
        rowsCe = work[0:72, 3456:3584]
        rowsP = work[0:32, 3584:3840]
        modrow = work[0:18, 4096:5120].rearrange("s (i n) -> s i n", i=2)
        Tmain = work[:, TAIL:TAIL + 8192].rearrange("p (g b n) -> p g b n", g=2, b=4)
        Ttail = [work[:, 0:TAIL], work[:, TAIL + 8192:2 * TAIL + 8192]]
        proj = work[:, TAIL:TAIL + 3 * PROJ].rearrange("p (t n) -> p t n", t=3)
        wbd = work[:, 9280:17472].rearrange("p (k l e) -> p k l e", k=2, l=32)
        Vbd = work[:, 0:1024].rearrange("p (c n) -> p c n", c=8)
        TS = work[:, 0:8192].rearrange("p (i b g n) -> p i b g n", i=2, b=2, g=2)
        TW = work[:, 8192:12288].rearrange("p (i b g n) -> p i b g n", i=2, b=2, g=2)
        cvS = nT[0:32].rearrange("p c t -> p (c t)")[:, 0:2048].rearrange("p (b n) -> p b n", b=8)
        cvn = nT[0:8].rearrange("p c t -> p (c t)")[:, 2048:2304]
        sgF = hT.rearrange("p c t -> p (c t)").rearrange("p (i b t) -> p i b t", i=2, b=4)
        bgT = work[:, 0:2304].rearrange("p (c t) -> p c t", c=8)
        cgT = work[:, 2304:4608].rearrange("p (c t) -> p c t", c=8)
        uP = work[:, 4608:4608 + 8 * 258].rearrange("p (c t) -> p c t", c=8)
        uS = work[:, 6672:6672 + 8 * 48].rearrange("p (c b t) -> p c b t", c=8, b=8)
        ctmp = work[:, 7056:7056 + 2 * 288].rearrange("p (i t) -> p i t", i=2)
        ztmp = work[:, 7632:7632 + 2 * 288].rearrange("p (i t) -> p i t", i=2)
        tail = work[:, 8208:8208 + 8 * 18].rearrange("p (c j) -> p c j", c=8)
        strow = convrows[0:16, 0:1024]
        tailrow = convrows[0:18, 1024:2048]
        SSBANK = [6, 6, 0, 0, 6]
        yacc = hT
        outN = hN
        spare = nT.rearrange("p c t -> p (c t)")
        ysb = spare[:, 0:1024]
        Dm = spare[:, 1024:1408].rearrange("p (t s) -> p t s", t=3)
        Dw = spare[:, 1408:1792].rearrange("p (t s) -> p t s", t=3)
        DT = spare[:, 1792:2080]
        nine = route[:, 0:81]
        selP, cwP, posP = [nine[:, 27 * i:27 * i + 27].rearrange("p (t e) -> p t e", t=3) for i in range(3)]
        selE, cw, pos = [x[:, :, 0:8] for x in (selP, cwP, posP)]
        lg = route[:, 84:108].rearrange("p (t e) -> p t e", t=3)
        mE = route[:, 108:124]
        cur = route[:, 124:140].rearrange("p (a t) -> p a t", a=4)
        rkA = route[:, 140:332].rearrange("p (t j i) -> p t j i", t=3, j=8)
        rkB = route[:, 332:524].rearrange("p (t j i) -> p t j i", t=3, j=8)
        Ssb = attn[:, 0:1536].rearrange("p (i n) -> p i n", i=3)
        PTs = attn[:, 1536:2560].rearrange("p (i n) -> p i n", i=2)
        ScP = attn[:, 2560:2816].rearrange("p (t n) -> p t n", t=2)
        PTc = attn[:, 2816:3072].rearrange("p (t n) -> p t n", t=2)
        SS = attn[:, 0:1632]
        PT = attn[:, 1632:1632 + 1920].rearrange("p (k n) -> p k n", k=15)
        ropet = attn[:, 0:512].rearrange("p (k n) -> p k n", k=4)
        kraw = attn[:, 0:512].rearrange("p (h n) -> p h n", h=2)
        vraw = attn[:, 512:1024].rearrange("p (h n) -> p h n", h=2)
        praw = attn[:, 1024:1056].rearrange("p (k n) -> p k n", k=2)
        ckt = attn[:, 1056:1584]
        rank = attn[:, 0:2312].rearrange("p (k t j i) -> p k t j i", k=2, t=4, j=17)
        gtmp = attn[:, 2312:2504].rearrange("p (t h b) -> p t h b", t=4, b=3)
        osb = qT[:, 0, 0:128]
        selneg = smp[:, 0:68].rearrange("p (t j) -> p t j", t=4)
        score = smp[:, 68:136].rearrange("p (t j) -> p t j", t=4)
        PcG = smp[:, 136:264].rearrange("p (t n) -> p t n", t=4)
        grow = smp[:, 264:276].rearrange("p (t b) -> p t b", t=4)
        ckP = smp[:, 276:292]
        peb = smp[:, 292:294]
        mx4, sm4 = smp[:, 296:300], smp[:, 300:304]
        s_slot = [sem(f"s_slot{i}") for i in range(RING)]
        s_used = sem("s_used")
        s_consts_in = sem("s_consts_in")
        s_rows_in = sem("s_rows_in")
        s_c_in = sem("s_c_in")
        s_x_in = sem("s_x_in")
        s_router_in = sem("s_router_in")
        s_pages_in = sem("s_pages_in")
        s_wbd_clear = sem("s_wbd_clear")
        s_wbd_in = sem("s_wbd_in")
        s_cexp = sem("s_cexp")
        s_cs_split = sem("s_cs_split")
        s_csilu = sem("s_csilu")
        s_rows_turned = sem("s_rows_turned")
        s_rowsT_ready = sem("s_rowsT_ready")
        s_x_turned = sem("s_x_turned")
        s_x_ready = sem("s_x_ready")
        s_mod_ready = sem("s_mod_ready")
        s_sq_ready = sem("s_sq_ready")
        s_ss_done = sem("s_ss_done")
        s_std_ready = sem("s_std_ready")
        s_rstd_ready = sem("s_rstd_ready")
        s_xhat_ready = sem("s_xhat_ready")
        s_h_prompt = sem("s_h_prompt")
        s_h_sample = sem("s_h_sample")
        s_proj_done = sem("s_proj_done")
        s_proj_dve = sem("s_proj_dve")
        s_proj_act = sem("s_proj_act")
        s_gate_exp = sem("s_gate_exp")
        s_rope_done = sem("s_rope_done")
        s_qk_turned = sem("s_qk_turned")
        s_qk_prompt = sem("s_qk_prompt")
        s_qk_sample = sem("s_qk_sample")
        s_cv_spread = sem("s_cv_spread")
        s_vbd_ready = sem("s_vbd_ready")
        s_cscore_done = sem("s_cscore_done")
        s_cscore_shift = sem("s_cscore_shift")
        s_cscore_exp = sem("s_cscore_exp")
        s_cprob_ready = sem("s_cprob_ready")
        s_cprob_turned = sem("s_cprob_turned")
        s_cprobT_ready = sem("s_cprobT_ready")
        s_scores_done = sem("s_scores_done")
        s_scores_taken = sem("s_scores_taken")
        s_dve_chain = sem("s_dve_chain")
        s_negmax_ready = sem("s_negmax_ready")
        s_exp_ready = sem("s_exp_ready")
        s_probs_ready = sem("s_probs_ready")
        s_probs_turned = sem("s_probs_turned")
        s_probsT_ready = sem("s_probsT_ready")
        s_pv_done = sem("s_pv_done")
        s_o_taken = sem("s_o_taken")
        s_bank_turned = sem("s_bank_turned")
        s_bank_act = sem("s_bank_act")
        s_bank_dve = sem("s_bank_dve")
        s_cmp_done = sem("s_cmp_done")
        s_craw_ready = sem("s_craw_ready")
        s_rot_done = sem("s_rot_done")
        s_ck_ready = sem("s_ck_ready")
        s_seq_scores = sem("s_seq_scores")
        s_group_scores = sem("s_group_scores")
        s_cprobs = sem("s_cprobs")
        s_importance = sem("s_importance")
        s_snegmax = sem("s_snegmax")
        s_sexp_ready = sem("s_sexp_ready")
        s_group_probs = sem("s_group_probs")
        s_group_pv = sem("s_group_pv")
        s_group_o = sem("s_group_o")
        s_wo_done = sem("s_wo_done")
        s_h_split = sem("s_h_split")
        s_ffn_silu = sem("s_ffn_silu")
        s_ffn_taken = sem("s_ffn_taken")
        s_ffn_act = sem("s_ffn_act")
        s_conv_copied = sem("s_conv_copied")
        s_state_taken = sem("s_state_taken")
        s_u_ready = sem("s_u_ready")
        s_tail_ready = sem("s_tail_ready")
        s_z_ready = sem("s_z_ready")
        s_state_in = sem("s_state_in")
        s_state_turned = sem("s_state_turned")
        s_tail_turned = sem("s_tail_turned")
        s_tail_rows = sem("s_tail_rows")
        s_kv_stored = sem("s_kv_stored")
        s_logits_done = sem("s_logits_done")
        s_logits_shift = sem("s_logits_shift")
        s_logits_exp = sem("s_logits_exp")
        s_sel_ready = sem("s_sel_ready")
        s_pos_done = sem("s_pos_done")
        s_count_ready = sem("s_count_ready")
        s_rows_done = sem("s_rows_done")
        s_rows_taken = sem("s_rows_taken")
        s_gathered = sem("s_gathered")
        s_split_hi = sem("s_split_hi")
        s_tile_done = sem("s_tile_done")
        s_xt_hi = sem("s_xt_hi")
        s_xt_lo = sem("s_xt_lo")
        s_tail_stored = sem("s_tail_stored")
        s_scatter_ready = sem("s_scatter_ready")
        s_silu_ready = sem("s_silu_ready")
        s_moe_chain = sem("s_moe_chain")
        s_eact_ready = sem("s_eact_ready")
        s_eact_turned = sem("s_eact_turned")
        s_eactT_hi = sem("s_eactT_hi")
        s_eactT_lo = sem("s_eactT_lo")
        s_y_act = sem("s_y_act")
        s_y_dve = sem("s_y_dve")
        s_share_done = sem("s_share_done")
        s_share_added = sem("s_share_added")
        s_gather_ready = sem("s_gather_ready")
        s_final_ready = sem("s_final_ready")
        s_final_rows = sem("s_final_rows")
        s_stored = sem("s_stored")
        s_vp_ready = sem("s_vp_ready")
        s_tail_pe = sem("s_tail_pe")
        s_sc_done = sem("s_sc_done")
        s_sc_shift = sem("s_sc_shift")
        s_sc_exp = sem("s_sc_exp")
        s_cv_ready = sem("s_cv_ready")
        s_modrow = sem("s_modrow")
        s_mod_turned = sem("s_mod_turned")
        s_osb_ready = sem("s_osb_ready")
        s_osb_turned = sem("s_osb_turned")

        def quarter(w, r0, c0, kcs, width):
            return w[r0:r0 + 128 * kcs, c0:c0 + width].rearrange("(k p) n -> p k n", p=128)

        stream = []

        def pair(w, c0, width=512):
            for h in range(2):
                stream.append([(0, 128, quarter(w, 512 * h, c0, 4, width), 4)])

        for k in range(24):
            pair(A["w_ada"][k // 12], (k % 12) * 512)
        T_NSA = len(stream)
        for ct in range(5):
            pair(A["w_nsa_in"][0], ct * 512)
        stream.append([(0, 128, quarter(A["w_nsa_in"][0], 0, 2560, 8, 48), 8)])
        T_CACHE = len(stream)
        for kv in range(2):
            for b in range(NB):
                stream.append(("page", "cmp", b, kv))
        T_SEL = len(stream)
        tile_k, tile_v = {}, {}
        for kv, tau in ((0, 0), (0, 1), (1, 0), (0, 2), (1, 1), (0, 3), (1, 2), (1, 3)):
            (tile_k, tile_v)[kv][tau] = len(stream)
            for b in (2 * tau, 2 * tau + 1):
                stream.append(("page", "sel", b, kv))
            stream.append(("win", tau, kv))
        T_WO = len(stream)
        for ch in range(2):
            for gp in range(2):
                w = A["w_nsa_out"][0].rearrange("(g r d) n -> g d r n", g=4, r=4)
                stream.append([(64 * g2, 64, w[2 * gp + g2][:, :, ch * 512:ch * 512 + 512], 4) for g2 in range(2)])
        T_FU = len(stream)
        for j in range(7):
            pair(A["w_ff_gu"][0], j * 512)
            pair(A["w_ff_gu"][0], FF + j * 512)
        T_FD = len(stream)
        for ch in range(2):
            for i in range(7):
                stream.append([(0, 128, quarter(A["w_ff_down"][0], 512 * i, ch * 512, 4, 512), 4)])
        T_CI = len(stream)
        for jt in range(2):
            for wh in range(3):
                pair(A["w_conv_in"][0], wh * 1024 + jt * 512)
        T_CO = len(stream)
        for ch in range(2):
            pair(A["w_conv_out"][0], ch * 512)
        T_MOE = len(stream)
        total = [0] * RING
        need = []
        for n, ent in enumerate(stream):
            q = n % RING
            total[q] += 16 * ({"page": 8, "win": 2}[ent[0]] if isinstance(ent, tuple) else len(ent))
            need.append(total[q])

        def wait_tile(pe, n):
            pe.wait_ge(s_slot[n % RING], need[n])

        def wait_expert_tile(eng, e, i):
            q = (T_MOE + i) % RING
            eng.wait_ge(s_slot[q], e * (16 * TILES_E // RING) + (total[q] + 16 * (i // RING + 1)))

        def slot(n, kc=4):
            w = {4: 512, 8: 48}[kc]
            return ring[:, n % RING, 0:kc * w].rearrange("p (k n) -> p k n", k=kc)

        def dst_n(ap):
            n = 1
            for d_ in ap.shape[1:]:
                n *= d_
            return n

        def turned(j, dst):
            np_, n = dst.shape[0], dst_n(dst)
            src = ps[0:np_, j % 4 if j < 64 else 4 + (j - 64) % 3, 0:n]
            return src if len(dst.shape) == 2 else src.rearrange("p (k n) -> p k n", n=128)

        J_SEL = 64

        def j_keys(tau):
            return J_SEL + 12 * tau + 4 * max(tau - 1, 0)

        def j_probs(tau):
            return J_SEL + 12 * min(tau + 2, 4) + 4 * tau

        def pages(n):
            return ring[:, n % RING, :].rearrange("p (k n) -> p k n", k=8)

        block = ctx.enter_context(nc.Block())

        @block.sync
        def _(sp):
            sp.dma_start(pgt[:], A["page_table"].rearrange("(o b) p -> o (b p)", o=1)).then_inc(s_pages_in, 16)
            for n, ent in enumerate(stream):
                if n == T_CACHE:
                    sp.wait_ge(s_pages_in, 16)
                if isinstance(ent, tuple) and ent[0] == "page":
                    _, kind, b, kv = ent
                    src = A["cache_cmp_kv"] if kind == "cmp" else A["cache_sel_kv"]
                    for j in range(8):
                        pg = sp.value_load(pgt[0:1, b * 8 + j:b * 8 + j + 1], min_val=0, max_val=src.shape[1] - 1)
                        if j == 0:
                            sp.wait_ge(s_used, n - RING + 1)
                        sp.dma_start(pages(n)[:, j, :], src[0, bass.ds(pg, 1), :, kv].rearrange("o r g d -> (o r) (g d)")
                                     ).then_inc(s_slot[n % RING], 16)
                    continue
                if n >= RING:
                    sp.wait_ge(s_used, n - RING + 1)
                if isinstance(ent, tuple):
                    _, tau, kv = ent
                    for b2 in range(2):
                        sp.dma_start(pages(n)[:, 4 * b2:4 * b2 + 4, :],
                                     A["cache_win_kv"][0, 2 * tau + b2, :, kv].rearrange("(j p) g d -> p j (g d)", p=128)
                                     ).then_inc(s_slot[n % RING], 16)
                    continue
                for p0, pn, src, kc in ent:
                    sp.dma_start(slot(n, kc)[p0:p0 + pn], src).then_inc(s_slot[n % RING], 16)

            def experts(rnd):
                with sp.Fori(0, NE) as e:
                    for i in range(TILES_E):
                        sp.wait_ge(s_used, (e + NE * rnd) * TILES_E + (T_MOE + i - RING + 1))
                        if i < 28:
                            j, u, h = i // 4, (i // 2) % 2, i % 2
                            src = A["w_moe_gu"][0, bass.ds(e, 1), 512 * h:512 * h + 512,
                                                u * FF + j * 512:u * FF + j * 512 + 512
                                                ].rearrange("o (k p) n -> p (o k) n", p=128)
                            dst = slot(T_MOE + i)
                        else:
                            src = A["w_moe_down"][0, bass.ds(e, 1), 256 * (i - 28):256 * (i - 27), :
                                                  ].rearrange("o (k p) n -> p (o k) n", p=128)
                            dst = ring[:, (T_MOE + i) % RING, :].rearrange("p (k n) -> p k n", k=2)
                        sp.dma_start(dst, src).then_inc(s_slot[(T_MOE + i) % RING], 16)

            experts(0)
            sp.wait_ge(s_count_ready, 1)
            c = sp.value_load(cnti[0:1, 0:1], min_val=0, max_val=NTOK)
            for rnd in (1, 2):
                with sp.If(c > SLOTS_E * rnd):
                    experts(rnd)

        @block.gpsimd
        def _(g):
            g.wait_ge(s_wbd_clear, 1)
            for kv, nm_ in enumerate(("w_cmp_k", "w_cmp_v")):
                for g2 in range(2):
                    g.dma_start(wbd[64 * g2:64 * g2 + 64, kv, :, 64 * g2:64 * g2 + 64],
                                A[nm_][0].rearrange("l d e -> d l e")).then_inc(s_wbd_in, 16)
            n = 0
            g.wait_ge(s_rope_done, 6)
            for o_p, o_s, c0 in ((2, 3, 1024), (4, 5, 1536), (6, None, 2048)):
                g.dma_start(O[o_p][0, 0].rearrange("(t p) k g d -> p t (k g d)", p=128),
                            proj[:, 0:2, c0:c0 + 512]).then_inc(s_stored, 16)
                n += 1
                if o_s is not None:
                    g.dma_start(O[o_s][0].rearrange("b t k g d -> (b t) (k g d)"),
                                proj[0:32, 2, c0:c0 + 512]).then_inc(s_stored, 16)
                    n += 1
                else:
                    for b in range(NB):
                        g.dma_start(O[7][0, b, 508:512].rearrange("t k g d -> t (k g d)"),
                                    proj[4 * b:4 * b + 4, 2, c0:c0 + 512]).then_inc(s_stored, 16)
                        n += 1
            g.wait_ge(s_stored, 16 * n)
            g.sem_inc(s_kv_stored, 1)
            g.wait_ge(s_x_ready, 16)
            g.dma_start(O[7][0, :, 0:508].rearrange("b r k g d -> b (r k g d)"),
                        A["cache_win_kv"][0, :, 4:512].rearrange("b r k g d -> b (r k g d)")).then_inc(s_stored, 16)
            n += 1
            g.wait_ge(s_tail_rows, 2)
            g.dma_start(O[8][0, 0], tailrow[0:2, :]).then_inc(s_stored, 16)
            g.dma_start(O[9][0].rearrange("b j d -> (b j) d"), tailrow[2:18, :]).then_inc(s_stored, 16)
            n += 2
            g.wait_ge(s_stored, 16 * n)
            g.sem_inc(s_tail_stored, 1)
            g.wait_ge(s_final_rows, 6)
            g.dma_start(O[0][0].rearrange("(t p) d -> p t d", p=128), outN[:, 0:2, :]).then_inc(s_stored, 16)
            g.dma_start(O[1].rearrange("b t d -> (b t) d"), outN[0:32, 2, :]).then_inc(s_stored, 16)
            n += 2
            g.wait_ge(s_stored, 16 * n)

        @block.scalar
        def _(a):
            a.dma_start(rowsC[0:8, :], A["c_prompt"].rearrange("s (c p) -> (s c) p", p=128)).then_inc(s_c_in, 16)
            a.dma_start(rowsC[8:72, :], A["c_sample"].rearrange("s (c p) -> (s c) p", p=128)).then_inc(s_c_in, 16)
            a.dma_start(con[:], A["consts"]).then_inc(s_consts_in, 16)
            a.dma_start(rowsA, A["b_ada"].rearrange("l (c p) -> (l c) p", p=128)).then_inc(s_rows_in, 16)
            a.dma_start(rowsB[0:16, :], A["g_norm_mix"].rearrange("l (c p) -> (l c) p", p=128)).then_inc(s_rows_in, 16)
            a.dma_start(rowsB[16:32, :], A["g_norm_ffn"].rearrange("l (c p) -> (l c) p", p=128)).then_inc(s_rows_in, 16)
            a.dma_start(rowsB[32:40, :], A["g_norm_final"].rearrange("(c p) -> c p", p=128)).then_inc(s_rows_in, 16)
            a.dma_start(rowsB[40:64, :], A["w_conv"][0].rearrange("j (c p) -> (j c) p", p=128)).then_inc(s_rows_in, 16)
            for kv, nm_ in enumerate(("pe_cmp_k", "pe_cmp_v")):
                for g2 in range(2):
                    a.dma_start(rowsP[:, kv * 128 + g2 * 64:kv * 128 + g2 * 64 + 64], A[nm_][0]).then_inc(s_rows_in, 16)
            a.dma_start(xrow[:, 0:2, :], A["x_prompt"][0].rearrange("(t p) d -> p t d", p=128)).then_inc(s_x_in, 16)
            a.dma_start(xrow[0:32, 2, :], A["x_sample"].rearrange("b t d -> (b t) d")).then_inc(s_x_in, 16)
            a.dma_start(wr[:], A["w_router"][0].rearrange("(c p) e -> p c e", p=128)).then_inc(s_router_in, 16)
            a.dma_start(br[:], A["b_router"].to_broadcast([128, 8])).then_inc(s_router_in, 16)

            a.wait_ge(s_c_in, 32)
            a.activation(rowsCe, rowsC, ACT.Exp, scale=-1.0).then_inc(s_cexp, 1)

            def ada_hi(i):
                wait_tile(a, i)
                if i >= SPLIT:
                    a.wait_ge(s_tile_done, i - SPLIT + 1)
                a.activation(ahi[:, i % SPLIT, :], ring[:, i % RING, :], ACT.Copy).then_inc(s_split_hi, 1)

            def ffn_hi(i):
                wait_tile(a, T_FU + i)
                if i >= SPLIT_F:
                    a.wait_ge(s_tile_done, SPLIT_AT_F + i - SPLIT_F + 1)
                a.activation(fhi[:, i % SPLIT_F, :], ring[:, (T_FU + i) % RING, :], ACT.Copy).then_inc(s_split_hi, 1)

            def conv_hi(i):
                wait_tile(a, T_CI + i)
                if i >= SPLIT_F:
                    a.wait_ge(s_tile_done, SPLIT_AT_C + i - SPLIT_F + 1)
                a.activation(chi[:, i % SPLIT_F, :], ring[:, (T_CI + i) % RING, :], ACT.Copy).then_inc(s_split_hi, 1)

            def norm(n):
                for c in range(DC):
                    a.wait_ge(s_x_ready, 8 * n + c + 1)
                    if n and c == 0:
                        a.wait_ge(s_h_sample, n)
                    a.activation(nT[:, c, :], xT[:, c, :], ACT.Square).then_inc(s_sq_ready, 1)
                if n:
                    a.wait_ge(s_xhat_ready, 8 * n)
                if n == 0:
                    for i in range(SPLIT, TILES_A):
                        ada_hi(i)
                if n == 1:
                    ffn_hi(0)
                if n == 2:
                    conv_hi(0)
                a.wait_ge(s_ss_done, n + 1)
                a.activation(std[:], ps[:, SSBANK[n], 0:NTOK], ACT.Sqrt, bias=C("eps"), scale=1.0 / D).then_inc(s_std_ready, 1)
                if n < 4:
                    lay, v = n // 2, 3 * (n % 2)
                    a.wait_ge(s_mod_ready, lay + 1)
                    for c in range(DC):
                        a.wait_ge(s_xhat_ready, 8 * n + c + 1)
                        a.activation(hT[:, c, 0:SEQ], nT[:, c, 0:SEQ], ACT.Identity, bias=modT[:, lay, v, c, 0:1],
                                     scale=modT[:, lay, v + 1, c, 0:1]).then_inc(s_h_prompt, 1)

            for i in range(SPLIT):
                ada_hi(i)
            norm(0)
            for ct in range(5):
                a.wait_ge(s_proj_done, ct + 1)
                src, dst = ps[:, 3 * (ct % 2) + 1, :], proj[:, 1, ct * 512:ct * 512 + 512]
                for g2 in range(2 if ct < 2 else 1):
                    if ct < 2:
                        ins = a.activation(dst.rearrange("p (r g d) -> p g r d", r=4, g=2)[:, g2],
                                           src.rearrange("p (g r d) -> p g r d", g=2, r=4)[:, g2], ACT.Copy)
                    else:
                        ins = a.activation(dst, src, ACT.Copy)
                ins.then_inc(s_proj_act, 1)
            a.wait_ge(s_proj_done, 6)
            for t, (_, m) in enumerate(TOK):
                a.activation(vP[0:m, t, 512:560], ps[0:m, 3 + t, 0:48], ACT.Exp, scale=-1.0).then_inc(s_gate_exp, 1)
            for i in range(16):
                a.wait_ge(s_qk_turned, i + 1)
                src = ps[:, i % 6, 0:SEQ]
                if i < 8:
                    dst = qT[:, i, :]
                elif i < 12:
                    dst = kTp[:, (i - 8) % 2, (i - 8) // 2, :]
                else:
                    dst = Ttail[(i - 12) // 2][:, SEQ * ((i - 12) % 2):SEQ * ((i - 12) % 2) + SEQ]
                a.activation(dst, src, ACT.Copy).then_inc(s_qk_prompt, 1)
            def take(j, dst):
                a.wait_ge(s_bank_turned, j + 1)
                a.activation(dst, turned(j, dst), ACT.Copy).then_inc(s_bank_act, 1)

            a.wait_ge(s_kv_stored, 1)
            a.wait_ge(s_qk_turned, 16)
            a.wait_ge(s_vp_ready, 1)
            for kv in range(2):
                for b in range(NB):
                    if b % 4 == 0 and (kv or b):
                        a.wait_ge(s_cmp_done, 2 * kv + b // 4)
                    for h in range(2):
                        take(32 * kv + 4 * b + 2 * h, Tmain[:, 0, b % 4, 512 * h:512 * h + 512])
            a.wait_ge(s_sc_shift, 1)
            a.activation(PcG, PcG, ACT.Exp, scale=SCALE).then_inc(s_sc_exp, 1)
            for t in range(2):
                a.wait_ge(s_cscore_shift, t + 1)
                a.activation(ScP[:, t, :], ScP[:, t, :], ACT.Exp, scale=SCALE).then_inc(s_cscore_exp, 1)
            for i in range(34):
                if i < 32:
                    w = 128 * (i // 16 + 1)
                    a.wait_ge(s_negmax_ready, i + 1)
                    for k in range(2):
                        a.activation(Ssb[:, i % 3, k * w:k * w + w], Ssb[:, i % 3, k * w:k * w + w], ACT.Exp,
                                     bias=small[:, 8 * (i % 3) + 2 + k:8 * (i % 3) + 3 + k], scale=SCALE,
                                     accum_out=small[:, 8 * (i % 3) + 4 + k:8 * (i % 3) + 5 + k]).then_inc(s_exp_ready, 1)
                if i >= 2:
                    u = i - 2
                    w = 128 * (u // 16 + 1)
                    a.wait_ge(s_probs_turned, u + 1)
                    if u >= 2:
                        a.wait_ge(s_pv_done, u - 1)
                    a.activation(PTs[:, u % 2, 0:2 * w], ps[:, 3 + u % 2, 0:2 * w], ACT.Copy).then_inc(s_probsT_ready, 1)
            a.wait_ge(s_pv_done, 32)

            def take_keys(tau):
                j = j_keys(tau)
                for b2 in range(2):
                    if tau >= 2:
                        a.wait_ge(s_seq_scores, 2 * (tau - 2) + b2 + 1)
                    for q in range(4):
                        if (j + 4 * b2 + q) % 2 == 0:
                            take(j + 4 * b2 + q, TS[:, tau % 2, b2, q // 2, 512 * (q % 2):512 * (q % 2) + 512])
                for q in range(4):
                    if (j + 8 + q) % 2 == 0:
                        take(j + 8 + q, TW[:, tau % 2, q // 2, q % 2, :])

            take_keys(0)
            for tau in range(4):
                if tau < 3:
                    take_keys(tau + 1)
                a.wait_ge(s_snegmax, tau + 1)
                for k, (lo, hi) in enumerate(((0, 1056), (1056, 1600))):
                    a.activation(SS[:, lo:hi], SS[:, lo:hi], ACT.Exp, bias=small[:, 38 + k:39 + k], scale=SCALE,
                                 accum_out=small[:, 40 + k:41 + k]).then_inc(s_sexp_ready, 1)
                if tau:
                    a.wait_ge(s_group_pv, tau)
                take(j_probs(tau), PT[:, 0:4, :])
                take(j_probs(tau) + 2, PT[:, 8:12, :])
            norm(1)
            for i in range(1, TILES_F):
                ffn_hi(i)
                if i < 28 and i % 4 == 3:
                    j = i // 4
                    a.wait_ge(s_tile_done, SPLIT_AT_F + 4 * j + 2)
                    if j >= 2:
                        a.wait_ge(s_ffn_act, j - 1)
                    else:
                        a.wait_ge(s_h_split, 8)
                    a.activation(sgF[:, j % 2], ps[:, 0:4, 0:NTOK], ACT.Silu).then_inc(s_ffn_silu, 1)
            norm(2)
            a.dma_start(strow, A["state_conv"][0].rearrange("b j d -> (b j) d")).then_inc(s_state_in, 16)
            for i in range(1, TILES_C):
                conv_hi(i)
                k = (i - 3) // 2
                if i % 2 == 1 and k in (0, 1, 3, 4):
                    wh, jt = k % 3, k // 3
                    a.wait_ge(s_tile_done, SPLIT_AT_C + 2 * k + 2)
                    b0 = 4 * (k % 2)
                    a.activation((bgT, cgT)[wh][:, 4 * jt:4 * jt + 4, :], ps[:, b0:b0 + 4, 0:NTOK], ACT.Copy
                                 ).then_inc(s_conv_copied, 1)
            norm(3)
            a.wait_ge(s_logits_shift, 1)
            a.activation(lg[:], lg[:], ACT.Exp).then_inc(s_logits_exp, 1)

            def experts(rnd):
                with a.Fori(0, NE) as e0:
                    e = e0 + NE * rnd
                    for i in range(TILES_E):
                        wait_expert_tile(a, e, i)
                        a.wait_ge(s_tile_done, e * TILES_E + (SPLIT_AT_M + i + 1 - SPLIT))
                        a.activation(whi[:, i % SPLIT, :], ring[:, (T_MOE + i) % RING, :], ACT.Copy).then_inc(s_split_hi, 1)
                        if i == 2:
                            for h in range(2):
                                a.wait_ge(s_gathered, e * 3 + (h + 1))
                                a.activation(XTh[:, 4 * h:4 * h + 4, :], ps[:, 4 + h, :].rearrange("p (c s) -> p c s", c=4),
                                             ACT.Copy).then_inc(s_xt_hi, 1)
                        if i % 4 == 2 and 6 <= i <= 30:
                            j = (i - 6) // 4
                            a.wait_ge(s_tile_done, e * TILES_E + (SPLIT_AT_M + 4 * j + 4))
                            if j:
                                a.wait_ge(s_eact_ready, e * 7 + j)
                            a.activation(siluM[:], ps[:, 2 * (j % 2), :], ACT.Silu).then_inc(s_silu_ready, 1)
                        if i % 4 == 2 and 10 <= i <= 34:
                            j = (i - 10) // 4
                            a.wait_ge(s_eact_turned, e * 7 + (j + 1))
                            a.activation(actTh[:, 4 * j:4 * j + 4, :], ps[:, 4 + j % 2, :].rearrange("p (k s) -> p k s", k=4),
                                         ACT.Copy).then_inc(s_eactT_hi, 1)
                    a.wait_ge(s_tile_done, e * TILES_E + (SPLIT_AT_M + TILES_E))
                    a.activation(ysb[:, 0:512], ps[:, 6, :], ACT.Copy).then_inc(s_y_act, 1)

            experts(0)
            a.wait_ge(s_count_ready, 1)
            c = a.value_load(cnti[0:1, 0:1], min_val=0, max_val=NTOK)
            for rnd in (1, 2):
                with a.If(c > SLOTS_E * rnd):
                    experts(rnd)
            norm(4)

        @block.vector
        def _(v):
            ch = Count(s_dve_chain)

            def link(ins):
                ch.inc(ins)
                ch.wait(v)

            def ada_lo(i):
                v.wait_ge(s_split_hi, i + 1)
                v.tensor_tensor(alo[:, i % SPLIT, :], ring[:, i % RING, :], ahi[:, i % SPLIT, :].bitcast(F32),
                                ALU.subtract).then_inc(s_used, 1)

            v.wait_ge(s_cexp, 1)
            link(v.tensor_scalar_add(rowsCe, rowsCe, 1.0))
            link(v.reciprocal(rowsCe, rowsCe))
            v.tensor_tensor(rowsC, rowsC, rowsCe, ALU.mult).then_inc(s_csilu, 1)
            for i in range(SPLIT):
                ada_lo(i)
            v.wait_ge(s_rows_turned, 1)
            v.tensor_copy(rowsT[:], ps[:, 7, 0:296]).then_inc(s_rowsT_ready, 1)
            v.wait_ge(s_rowsT_ready, 1)
            cs_ = csT.rearrange("p s c -> p c s")
            link(v.tensor_copy(csHL[:, :, 0:9], cs_))
            v.tensor_tensor(csHL[:, :, 9:18], cs_, csHL[:, :, 0:9].bitcast(F32), ALU.subtract).then_inc(s_cs_split, 1)
            for c in range(DC):
                v.wait_ge(s_x_turned, c + 1)
                v.tensor_copy(xT[:, c, :], ps[:, 2 + c % 4, 0:NTOK]).then_inc(s_x_ready, 1)

            for k in range(24):
                for i in (2 * k + 3, 2 * k + 4):
                    if i < TILES_A:
                        ada_lo(i)
                v.wait_ge(s_tile_done, 2 * k + 2)
                if k >= 2:
                    v.wait_ge(s_mod_turned, k - 1)
                v.tensor_copy(modrow[:, k % 2, :], ps[0:18, k % 2, :]).then_inc(s_modrow, 1)

            def modulation(lay):
                v.wait_ge(s_mod_turned, 12 * lay + 12)
                m = modT[:, lay].rearrange("p v c s -> p (v c) s")
                link(v.tensor_tensor(m, ps[:, 2 + lay, 0:432].rearrange("p (c s) -> p c s", s=9),
                                     b_adaT[:, lay].unsqueeze(2).to_broadcast([128, 48, 9]), ALU.add))
                for k, g_ in ((1, g_mixT), (4, g_ffnT)):
                    ins = v.scalar_tensor_tensor(out=modT[:, lay, k], in0=modT[:, lay, k], scalar=1.0,
                                                 in1=g_[:, lay].unsqueeze(2).to_broadcast([128, 8, 9]),
                                                 op0=ALU.add, op1=ALU.mult)
                    if k == 1:
                        link(ins)
                ins.then_inc(s_mod_ready, 1)
                v.wait_ge(s_mod_ready, lay + 1)

            def norm(n):
                v.wait_ge(s_std_ready, n + 1)
                v.reciprocal(rstd[:], std[:]).then_inc(s_rstd_ready, 1)
                v.wait_ge(s_rstd_ready, n + 1)
                for c in range(DC):
                    v.tensor_tensor(nT[:, c, :], xT[:, c, :], rstd[:], ALU.mult).then_inc(s_xhat_ready, 1)
                v.wait_ge(s_xhat_ready, 8 * n + 8)
                if n < 4:
                    lay, k = n // 2, 3 * (n % 2)
                    nS = nT[:, :, SEQ:].rearrange("p c (b t) -> p c b t", t=NT)
                    hS = hT[:, :, SEQ:].rearrange("p c (b t) -> p c b t", t=NT)
                    for t in range(NT):
                        ins = v.tensor_tensor(nS[:, :, :, t], nS[:, :, :, t], modT[:, lay, k + 1, :, 1:9], ALU.mult)
                    link(ins)
                    for t in range(NT):
                        ins = v.tensor_tensor(hS[:, :, :, t], nS[:, :, :, t], modT[:, lay, k, :, 1:9], ALU.add)
                    ins.then_inc(s_h_sample, 1)

            def residual(lay, k, src):
                for c in range(DC):
                    y = src(c)
                    ys = small[:, 64 + 32 * (c % 2):96 + 32 * (c % 2)]
                    v.scalar_tensor_tensor(out=xT[:, c, 0:SEQ], in0=y[:, 0:SEQ], scalar=modT[:, lay, k, c, 0:1],
                                           in1=xT[:, c, 0:SEQ], op0=ALU.mult, op1=ALU.add)
                    link(v.tensor_tensor(ys.rearrange("p (b t) -> p b t", t=NT),
                                         y[:, SEQ:NTOK].rearrange("p (b t) -> p b t", t=NT),
                                         modT[:, lay, k, c, 1:9].unsqueeze(2).to_broadcast([128, NB, NT]), ALU.mult))
                    v.tensor_tensor(xT[:, c, SEQ:], xT[:, c, SEQ:], ys, ALU.add).then_inc(s_x_ready, 1)

            modulation(0)
            modulation(1)
            norm(0)
            v.memset(wbd[:], 0.0).then_inc(s_wbd_clear, 1)
            link(v.memset(qbd[:], 0.0))
            for ct in range(5):
                v.wait_ge(s_proj_done, ct + 1)
                for t in (0, 2):
                    m = TOK[t][1]
                    src, dst = ps[0:m, 3 * (ct % 2) + t, :], proj[0:m, t, ct * 512:ct * 512 + 512]
                    if ct < 2:
                        for g2 in range(2):
                            ins = v.tensor_copy(dst.rearrange("p (r g d) -> p g r d", r=4, g=2)[:, g2],
                                                src.rearrange("p (g r d) -> p g r d", g=2, r=4)[:, g2])
                    else:
                        ins = v.tensor_copy(dst, src)
                ins.then_inc(s_proj_dve, 1)
            v.wait_ge(s_proj_act, 5)
            v.wait_ge(s_proj_dve, 5)
            tc, ts_ = (C(x).rearrange("p (t n) -> p t n", t=3) for x in ("tcos", "tsin"))
            for grp in range(2):
                for t, (_, m) in enumerate(TOK):
                    if grp == 0:
                        xv = proj[0:m, t, 0:1024].rearrange("p (h d) -> p h d", h=16)
                        x1, x2 = xv[:, :, 0:8], xv[:, :, 8:16]
                        tv = [ropet[0:m, i, 0:128].rearrange("p (h n) -> p h n", n=8) for i in range(4)]
                        co = tc[0:m, t].unsqueeze(1).to_broadcast([m, 16, 8])
                        si = ts_[0:m, t].unsqueeze(1).to_broadcast([m, 16, 8])
                        parts = [(x1, x2, tv, co, si)]
                    else:
                        parts = []
                        for q_, c0 in enumerate((1536, 2048)):
                            xv = proj[0:m, t, c0:c0 + 256].rearrange("p (h d) -> p h d", h=4)
                            tv = [ropet[0:m, i, 32 * q_:32 * q_ + 32].rearrange("p (h n) -> p h n", n=8) for i in range(4)]
                            parts.append((xv[:, :, 0:8], xv[:, :, 8:16], tv,
                                          tc[0:m, t].unsqueeze(1).to_broadcast([m, 4, 8]),
                                          ts_[0:m, t].unsqueeze(1).to_broadcast([m, 4, 8])))
                    for x1, x2, tv, co, si in parts:
                        v.tensor_tensor(tv[0], x1, co, ALU.mult)
                        v.tensor_tensor(tv[1], x2, si, ALU.mult)
                        v.tensor_tensor(tv[2], x2, co, ALU.mult)
                        ins = v.tensor_tensor(tv[3], x1, si, ALU.mult)
                    link(ins)
                    for x1, x2, tv, co, si in parts:
                        v.tensor_tensor(x1, tv[0], tv[1], ALU.subtract)
                        ins = v.tensor_tensor(x2, tv[2], tv[3], ALU.add)
                    ins.then_inc(s_rope_done, 1)
                    v.wait_ge(s_rope_done, 3 * grp + t + 1)
            v.wait_ge(s_gate_exp, 3)
            for t, (_, m) in enumerate(TOK):
                gv = vP[0:m, t, 512:560]
                link(v.tensor_scalar_add(gv, gv, 1.0))
                link(v.reciprocal(gv, gv))
            for t, (_, m) in enumerate(TOK):
                v.tensor_copy(vP[0:m, t, 0:256], proj[0:m, t, 1792:2048])
                ins = v.tensor_copy(vP[0:m, t, 256:512], proj[0:m, t, 2304:2560])
            ins.then_inc(s_vp_ready, 1)
            for kv in range(2):
                ins = v.tensor_copy(Ttail[kv][:, 512:544], peT[:, kv, :])
            ins.then_inc(s_tail_pe, 1)
            for i in range(12):
                v.wait_ge(s_qk_prompt, i + 1)
                if i < 8:
                    gp, r = i // 4, i % 4
                    for g2 in range(2):
                        dst = qbd[64 * g2:64 * g2 + 64].rearrange("p b (g k r t) -> p b g k r t", g=2, k=2, r=4)
                        ins = v.tensor_copy(dst[:, :, gp, g2, r, :],
                                            ps[64 * g2:64 * g2 + 64, i % 6, SEQ:NTOK].rearrange("p (b t) -> p b t", t=NT))
                else:
                    ins = v.tensor_copy(kTn[:, (i - 8) % 2, (i - 8) // 2, :], ps[:, i % 6, SEQ:NTOK])
                ins.then_inc(s_qk_sample, 1)

            def take(j, dst):
                v.wait_ge(s_bank_turned, j + 1)
                v.tensor_copy(dst, turned(j, dst)).then_inc(s_bank_dve, 1)

            v.wait_ge(s_kv_stored, 1)
            v.wait_ge(s_vp_ready, 1)
            for kv in range(2):
                for b in range(NB):
                    if b % 4 == 0 and (kv or b):
                        v.wait_ge(s_cmp_done, 2 * kv + b // 4)
                    for h in range(2):
                        take(32 * kv + 4 * b + 2 * h + 1, Tmain[:, 1, b % 4, 512 * h:512 * h + 512])
            v.wait_ge(s_cmp_done, 4)
            v.tensor_copy(peb[:, 0:1], ps[:, 4, 16:17])
            link(v.tensor_copy(peb[:, 1:2], ps[:, 6, 272:273]))
            v.tensor_scalar(praw[:, 0], ps[:, 4, 0:16], peb[:, 0:1], None, ALU.add)
            v.tensor_scalar(kraw[:, 0], ps[:, 4, 17:273], peb[:, 0:1], None, ALU.add)
            v.tensor_scalar(kraw[:, 1], ps[:, 5, 0:256], peb[:, 0:1], None, ALU.add)
            v.tensor_scalar(praw[:, 1], ps[:, 6, 256:272], peb[:, 1:2], None, ALU.add)
            v.tensor_scalar(vraw[:, 0], ps[:, 6, 0:256], peb[:, 1:2], None, ALU.add)
            v.tensor_scalar(vraw[:, 1], ps[:, 7, 0:256], peb[:, 1:2], None, ALU.add).then_inc(s_craw_ready, 1)
            v.wait_ge(s_craw_ready, 1)
            v.wait_ge(s_rot_done, 1)

            def rope_cmp(dst, raw, rot, g, n, o):
                co = C("ckcos")[:, 0:n].unsqueeze(1).to_broadcast([128, g, n])
                si = C("cksin")[:, 0:n].unsqueeze(1).to_broadcast([128, g, n])
                f = lambda x: x.rearrange("p (g n) -> p g n", g=g)
                v.tensor_tensor(f(dst), f(raw), co, ALU.mult)
                link(v.tensor_tensor(f(ckt[:, o:o + g * n]), f(rot), si, ALU.mult))
                return v.tensor_tensor(f(dst), f(dst), f(ckt[:, o:o + g * n]), ALU.add)

            rope_cmp(ckP, praw[:, 0], ps[:, 1, 0:16], 2, 8, 512)
            rope_cmp(ckS[:], kraw[:].rearrange("p h n -> p (h n)"), ps[:, 0, :], 16, 32, 0)
            v.tensor_copy(cvn, ps[0:8, 1, 128:384]).then_inc(s_ck_ready, 1)
            for q in range(4):
                v.tensor_copy(cvS[:, 2 * q:2 * q + 2, :], ps[0:32, 2 + q, :].rearrange("p (b n) -> p b n", b=2)
                              ).then_inc(s_cv_ready, 1)
            v.wait_ge(s_cv_spread, 1)
            vm = C("vbdmask").rearrange("p (c g) -> p c g", c=8)
            for gp in range(2):
                for g2 in range(2):
                    ins = v.tensor_tensor(Vbd[:, 4 * gp:4 * gp + 4, 64 * g2:64 * g2 + 64],
                                          ps[:, 0, gp * 128 + g2 * 64:gp * 128 + g2 * 64 + 64].unsqueeze(1).to_broadcast([128, 4, 64]),
                                          vm[:, 4 * gp:4 * gp + 4, g2].unsqueeze(2).to_broadcast([128, 4, 64]), ALU.mult)
            ins.then_inc(s_vbd_ready, 1)
            v.wait_ge(s_sc_done, 1)
            link(v.tensor_copy(PcG, ps[:, 1, 0:128].rearrange("p (t n) -> p t n", t=4)))
            link(v.tensor_tensor(gtmp, ps[:, 1, 128:320].rearrange("p (t h b) -> p t h b", t=4, b=3),
                                 C("rowhead").unsqueeze(1).unsqueeze(3).to_broadcast([128, 4, 16, 3]), ALU.mult))
            for t in range(4):
                ins = v.tensor_reduce(grow[:, t, :], gtmp[:, t].rearrange("p h b -> p b h"), AX, ALU.add)
            link(ins)
            link(v.tensor_reduce(mx4, PcG, AX, ALU.max))
            v.tensor_tensor(PcG, PcG, mx4.unsqueeze(2).to_broadcast([128, 4, 32]), ALU.subtract).then_inc(s_sc_shift, 1)
            v.wait_ge(s_sc_exp, 1)
            link(v.tensor_reduce(sm4, PcG, AX, ALU.add))
            link(v.reciprocal(sm4, sm4))
            v.tensor_tensor(PcG, PcG, sm4.unsqueeze(2).to_broadcast([128, 4, 32]), ALU.mult).then_inc(s_cprobs, 1)
            v.wait_ge(s_importance, 1)
            link(v.memset(score[:, :, 16:17], 0.0))
            link(v.tensor_reduce(score[:, :, 0:16], ps[:, 2, 0:128].rearrange("p (t n c) -> p t n c", t=4, c=2), AX, ALU.add))
            link(v.tensor_tensor(score, score, C("bonus").unsqueeze(1).to_broadcast([128, 4, 17]), ALU.add))
            for t in range(4):
                si_ = score[:, t].unsqueeze(1).to_broadcast([128, 17, 17])
                sj_ = score[:, t].unsqueeze(2).to_broadcast([128, 17, 17])
                v.tensor_tensor(rank[:, 0, t], si_, sj_, ALU.is_gt)
                ins = v.tensor_tensor(rank[:, 1, t], si_, sj_, ALU.is_equal)
            link(ins)
            bf = C("before").rearrange("p (j i) -> p j i", j=17)
            for t in range(4):
                ins = v.tensor_tensor(rank[:, 1, t], rank[:, 1, t], bf, ALU.mult)
            link(ins)
            rf = [rank[:, i].rearrange("p t j i -> p (t j) i") for i in range(2)]
            link(v.tensor_tensor(rf[0], rf[0], rf[1], ALU.add))
            sn = selneg.rearrange("p t j -> p (t j)")
            link(v.tensor_reduce(sn, rf[0], AX, ALU.add))
            v.tensor_scalar(sn, sn, 7.5, -BIG, ALU.is_gt, ALU.mult)
            link(v.tensor_tensor(PcG, PcG, grow[:, :, 0].unsqueeze(2).to_broadcast([128, 4, 32]), ALU.mult))
            ca, cm = (C(x).rearrange("p (t n) -> p t n", t=2) for x in ("cmpadd", "cmpmul"))
            mxc, smc = small[:, 96:112], small[:, 112:128]
            v.wait_ge(s_cscore_done, 1)
            for t in range(2):
                sc = ScP[:, t, :].rearrange("p (c g n) -> p c g n", c=8, g=2)
                s16 = ScP[:, t, :].rearrange("p (h n) -> p h n", h=16)
                for g2 in range(2):
                    ins = v.tensor_tensor(sc[:, :, g2, :], ps[:, 6 + g2, 256 + 64 * t:320 + 64 * t].rearrange("p (c n) -> p c n", c=8),
                                          ca[:, t].unsqueeze(1).to_broadcast([128, 8, 8]), ALU.add)
                link(ins)
                link(v.tensor_reduce(mxc, s16, AX, ALU.max))
                v.tensor_tensor(s16, s16, mxc.unsqueeze(2).to_broadcast([128, 16, 8]), ALU.subtract).then_inc(s_cscore_shift, 1)
                v.wait_ge(s_cscore_exp, t + 1)
                link(v.tensor_tensor(s16, s16, cm[:, t].unsqueeze(1).to_broadcast([128, 16, 8]), ALU.mult))
                link(v.tensor_reduce(smc, s16, AX, ALU.add))
                link(v.tensor_scalar_max(smc, smc, 1e-30))
                link(v.reciprocal(smc, smc))
                gv = vP[:, t, 512:560].rearrange("p (g k r b) -> p g k r b", g=2, k=2, r=4)
                for gp in range(2):
                    for k in range(2):
                        mv = smc.rearrange("p (g r k) -> p g r k", g=2, k=2)[:, gp, :, k]
                        ins = v.tensor_tensor(mv, mv, gv[:, gp, k, :, 0], ALU.mult)
                link(ins)
                v.tensor_tensor(s16, s16, smc.unsqueeze(2).to_broadcast([128, 16, 8]), ALU.mult).then_inc(s_cprob_ready, 1)
            v.wait_ge(s_cprob_turned, 1)
            v.tensor_copy(PTc[:], ps[:, 5, 0:256].rearrange("p (t n) -> p t n", t=2)).then_inc(s_cprobT_ready, 1)
            for i in range(35):
                if i < 32:
                    t = i // 16
                    w = 128 * (t + 1)
                    Sv = Ssb[:, i % 3, 0:2 * w].rearrange("p (k n) -> p k n", k=2)
                    mx, nm = small[:, 8 * (i % 3):8 * (i % 3) + 2], small[:, 8 * (i % 3) + 2:8 * (i % 3) + 4]
                    v.wait_ge(s_scores_done, i + 1)
                    if i >= 3:
                        v.wait_ge(s_probs_turned, i - 2)
                    v.tensor_tensor(Sv, ps[:, i % 3, 0:2 * w].rearrange("p (k n) -> p k n", k=2),
                                    C("causal")[:, 256 - w:256].unsqueeze(1).to_broadcast([128, 2, w]), ALU.add
                                    ).then_inc(s_scores_taken, 1)
                    v.wait_ge(s_scores_taken, i + 1)
                    link(v.tensor_reduce(mx, Sv, AX, ALU.max))
                    v.tensor_scalar_mul(nm, mx, -SCALE).then_inc(s_negmax_ready, 1)
                if 1 <= i < 33:
                    u = i - 1
                    t, hh = u // 16, u % 16
                    gp, r, g2 = hh // 8, (hh // 2) % 4, hh % 2
                    w = 128 * (t + 1)
                    Sv = Ssb[:, u % 3, 0:2 * w].rearrange("p (k n) -> p k n", k=2)
                    sm, rg = small[:, 8 * (u % 3) + 4:8 * (u % 3) + 6], small[:, 8 * (u % 3) + 6:8 * (u % 3) + 8]
                    v.wait_ge(s_exp_ready, 2 * (u + 1))
                    link(v.reciprocal(rg, sm))
                    h = gp * 8 + g2 * 4 + r
                    link(v.tensor_tensor(rg, rg, vP[:, t, 512 + 3 * h + 1:512 + 3 * h + 3], ALU.mult))
                    v.tensor_tensor(Sv, Sv, rg.unsqueeze(2).to_broadcast([128, 2, w]), ALU.mult).then_inc(s_probs_ready, 1)
                if i >= 3 and (i - 3) % 2 == 1:
                    u = i - 3
                    t, c = u // 16, (u % 16) // 2
                    v.wait_ge(s_pv_done, u + 1)
                    v.tensor_copy(oT[:, c, 128 * t:128 * t + 128], ps[:, 5 + (u // 2) % 2, 0:128]).then_inc(s_o_taken, 1)

            def take_keys(tau):
                j = j_keys(tau)
                for b2 in range(2):
                    if tau >= 2:
                        v.wait_ge(s_seq_scores, 2 * (tau - 2) + b2 + 1)
                    for q in range(4):
                        if (j + 4 * b2 + q) % 2 == 1:
                            take(j + 4 * b2 + q, TS[:, tau % 2, b2, q // 2, 512 * (q % 2):512 * (q % 2) + 512])
                for q in range(4):
                    if (j + 8 + q) % 2 == 1:
                        take(j + 8 + q, TW[:, tau % 2, q // 2, q % 2, :])

            take_keys(0)
            for tau in range(4):
                nm_ = C("newmask").rearrange("p (t n) -> p t n", t=4)[:, tau]
                v.wait_ge(s_group_scores, tau + 1)
                v.tensor_tensor(SS[:, 0:1024].rearrange("p (j n) -> p j n", j=16),
                                ps[:, 0:2, :].rearrange("p a (j n) -> p (a j) n", n=64),
                                selneg[:, tau, 0:16].unsqueeze(2).to_broadcast([128, 16, 64]), ALU.add)
                v.scalar_tensor_tensor(out=SS[:, 1024:1056], in0=ps[:, 3, 0:32], scalar=selneg[:, tau, 16:17], in1=nm_,
                                       op0=ALU.add, op1=ALU.add)
                v.tensor_copy(SS[:, 1060:1568], ps[:, 2, 4:512])
                v.tensor_tensor(SS[:, 1056:1060], ps[:, 2, 0:4], C("winmask"), ALU.add)
                link(v.tensor_tensor(SS[:, 1568:1600], ps[:, 3, 32:64], nm_, ALU.add))
                v.tensor_reduce(small[:, 36:37], SS[:, 0:1056], AX, ALU.max)
                link(v.tensor_reduce(small[:, 37:38], SS[:, 1056:1600], AX, ALU.max))
                v.tensor_scalar_mul(small[:, 38:40], small[:, 36:38], -SCALE).then_inc(s_snegmax, 1)
                if tau < 3:
                    take_keys(tau + 1)
                v.wait_ge(s_sexp_ready, 2 * (tau + 1))
                link(v.reciprocal(small[:, 42:44], small[:, 40:42]))
                link(v.tensor_tensor(small[:, 42:44], small[:, 42:44], grow[:, tau, 1:3], ALU.mult))
                v.tensor_scalar(SS[:, 0:1056], SS[:, 0:1056], small[:, 42:43], None, ALU.mult)
                v.tensor_scalar(SS[:, 1056:1600], SS[:, 1056:1600], small[:, 43:44], None, ALU.mult).then_inc(s_group_probs, 1)
                if tau:
                    v.wait_ge(s_group_pv, tau)
                take(j_probs(tau) + 1, PT[:, 4:8, :])
                take(j_probs(tau) + 3, PT[0:32, 12:15, :])
                v.wait_ge(s_group_pv, tau + 1)
                v.tensor_copy(osb, ps[:, 7, 0:128]).then_inc(s_osb_ready, 1)
                v.wait_ge(s_osb_turned, tau + 1)
                for g2 in range(2):
                    for gp in range(2):
                        for b2 in range(2):
                            p_ = slice(64 * g2, 64 * g2 + 64)
                            c0 = 128 + b2 * 64 + gp * 32 + g2 * 16
                            t0 = SEQ + (2 * tau + b2) * NT
                            ins = v.tensor_copy(oT[p_, 4 * gp:4 * gp + 4, t0:t0 + NT],
                                                ps[p_, 7, c0:c0 + 16].rearrange("p (r t) -> p r t", t=NT))
                ins.then_inc(s_group_o, 1)

            def from_wo(c):
                v.wait_ge(s_wo_done, c + 1)
                return ps[:, c % 6, :]
            v.wait_ge(s_group_o, 4)
            residual(0, 2, from_wo)
            norm(1)
            def ffn_lo(i):
                v.wait_ge(s_split_hi, SPLIT_AT_F + i + 1)
                v.tensor_tensor(flo[:, i % SPLIT_F, :], ring[:, (T_FU + i) % RING, :], fhi[:, i % SPLIT_F, :].bitcast(F32),
                                ALU.subtract).then_inc(s_used, 1)

            v.wait_ge(s_used, T_FU)
            ffn_lo(0)
            v.wait_ge(s_h_sample, 2)
            for c in range(DC):
                v.wait_ge(s_h_prompt, 8 + c + 1)
                link(v.tensor_copy(hTh[:, c, :], hT[:, c, :]))
                v.tensor_tensor(hTl[:, c, :], hT[:, c, :], hTh[:, c, :].bitcast(F32), ALU.subtract).then_inc(s_h_split, 1)
            for i in range(1, TILES_F):
                ffn_lo(i)
                if i % 4 == 1 and 5 <= i <= 29:
                    j = (i - 5) // 4
                    sg = sgF[:, j % 2]
                    v.wait_ge(s_ffn_silu, j + 1)
                    v.wait_ge(s_tile_done, SPLIT_AT_F + 4 * j + 4)
                    v.tensor_tensor(sg, sg, ps[:, 4:8, 0:NTOK], ALU.mult).then_inc(s_ffn_taken, 1)
                    v.wait_ge(s_ffn_taken, j + 1)
                    link(v.tensor_copy(actFh[:, 4 * j:4 * j + 4, :], sg))
                    v.tensor_tensor(actFl[:, 4 * j:4 * j + 4, :], sg, actFh[:, 4 * j:4 * j + 4, :].bitcast(F32),
                                    ALU.subtract).then_inc(s_ffn_act, 1)

            def from_dn(c):
                v.wait_ge(s_tile_done, SPLIT_AT_F + 28 + 7 * (c // 4 + 1))
                return ps[:, c, :]
            residual(0, 5, from_dn)
            norm(2)
            def conv_lo(i):
                v.wait_ge(s_split_hi, SPLIT_AT_C + i + 1)
                v.tensor_tensor(clo[:, i % SPLIT_F, :], ring[:, (T_CI + i) % RING, :], chi[:, i % SPLIT_F, :].bitcast(F32),
                                ALU.subtract).then_inc(s_used, 1)

            conv_lo(0)
            v.wait_ge(s_h_sample, 3)
            for c in range(DC):
                v.wait_ge(s_h_prompt, 16 + c + 1)
                link(v.tensor_copy(cTh[:, c, :], hT[:, c, :]))
                v.tensor_tensor(cTl[:, c, :], hT[:, c, :], cTh[:, c, :].bitcast(F32), ALU.subtract).then_inc(s_h_split, 1)
            conv_lo(1)
            link(v.memset(uP[:, :, 0:2], 0.0))
            v.wait_ge(s_state_turned, 1)
            v.tensor_copy(uS[:, :, :, 0:2], ps[:, 7, 0:128].rearrange("p (c b j) -> p c b j", c=8, b=8)).then_inc(s_state_taken, 1)
            v.wait_ge(s_state_taken, 1)
            for c in range(DC):
                for i in {0: range(2, 8), 2: (8,), 4: range(9, 14)}.get(c, ()):
                    conv_lo(i)
                k = 3 * (c // 4) + 2
                B = 4 * (k % 2) + c % 4
                v.wait_ge(s_tile_done, SPLIT_AT_C + 2 * k + 2)
                v.wait_ge(s_conv_copied, 2 * (c // 4) + 2)
                v.tensor_tensor(uP[:, c, 2:258], ps[:, B, 0:SEQ], cgT[:, c, 0:SEQ], ALU.mult)
                ins = v.tensor_tensor(uS[:, c, :, 2:6], ps[:, B, SEQ:NTOK].rearrange("p (b t) -> p b t", t=NT),
                                      cgT[:, c, SEQ:].rearrange("p (b t) -> p b t", t=NT), ALU.mult)
                ins.then_inc(s_u_ready, 1)
                v.wait_ge(s_u_ready, c + 1)
                ct_ = ctmp[:, c % 2]
                cS = ct_[:, SEQ:].rearrange("p (b t) -> p b t", t=NT)
                v.tensor_scalar(ct_[:, 0:SEQ], uP[:, c, 0:SEQ], w_convT[:, 0, c:c + 1], None, ALU.mult)
                link(v.tensor_scalar(cS, uS[:, c, :, 0:NT], w_convT[:, 0, c:c + 1], None, ALU.mult))
                for j in (1, 2):
                    v.scalar_tensor_tensor(out=ct_[:, 0:SEQ], in0=uP[:, c, j:j + SEQ], scalar=w_convT[:, j, c:c + 1],
                                           in1=ct_[:, 0:SEQ], op0=ALU.mult, op1=ALU.add)
                    link(v.scalar_tensor_tensor(out=cS, in0=uS[:, c, :, j:j + NT], scalar=w_convT[:, j, c:c + 1],
                                                in1=cS, op0=ALU.mult, op1=ALU.add))
                zt_ = ztmp[:, c % 2]
                link(v.tensor_tensor(zt_, ct_, bgT[:, c, :], ALU.mult))
                link(v.tensor_copy(zTh[:, c, :], zt_))
                v.tensor_tensor(zTl[:, c, :], zt_, zTh[:, c, :].bitcast(F32), ALU.subtract).then_inc(s_z_ready, 1)
            v.tensor_copy(tail[:, :, 0:2], uP[:, :, 256:258])
            for j in range(2):
                ins = v.tensor_copy(tail[:, :, 2:18].rearrange("p c (b j) -> p c b j", j=2)[:, :, :, j], uS[:, :, :, 4 + j])
            ins.then_inc(s_tail_ready, 1)
            conv_lo(14)
            for i in range(2):
                v.wait_ge(s_tail_turned, i + 1)
                v.tensor_copy(tailrow[:, 512 * i:512 * i + 512], ps[0:18, 6 + i, :]).then_inc(s_tail_rows, 1)
            conv_lo(15)

            def from_co(c):
                v.wait_ge(s_tile_done, SPLIT_AT_C + 12 + 2 * (c // 4) + 2)
                return ps[:, c, :]
            residual(1, 2, from_co)
            norm(3)
            v.wait_ge(s_logits_done, 1)
            v.wait_ge(s_tail_rows, 2)
            v.wait_ge(s_router_in, 32)
            v.wait_ge(s_tail_stored, 1)
            v.memset(nine, 0.0)
            link(v.memset(lg[:], 0.0))
            v.tensor_tensor(lg[:, 0:2, :], ps[:, 7, 0:16].rearrange("p (t e) -> p t e", t=2),
                            br[:].unsqueeze(1).to_broadcast([128, 2, 8]), ALU.add)
            link(v.tensor_tensor(lg[0:32, 2, :], ps[0:32, 7, 16:24], br[0:32, :], ALU.add))
            bef = C("before").rearrange("p (j i) -> p j i", j=17)[:, 0:8, 0:8]
            for t in range(3):
                li, lj = lg[:, t].unsqueeze(1).to_broadcast([128, 8, 8]), lg[:, t].unsqueeze(2).to_broadcast([128, 8, 8])
                v.tensor_tensor(rkA[:, t], li, lj, ALU.is_gt)
                link(v.tensor_tensor(rkB[:, t], li, lj, ALU.is_equal))
                ins = v.tensor_tensor(rkB[:, t], rkB[:, t], bef, ALU.mult)
            link(ins)
            link(v.tensor_tensor(rkA[:], rkA[:], rkB[:], ALU.add))
            link(v.tensor_reduce(selE, rkA[:], AX, ALU.add))
            link(v.tensor_scalar(selE, selE, 1.5, None, ALU.is_lt))
            v.tensor_tensor(selE, selE, C("valid").unsqueeze(2).to_broadcast([128, 3, 8]), ALU.mult).then_inc(s_sel_ready, 1)
            v.wait_ge(s_sel_ready, 1)
            link(v.tensor_reduce(mE[:, 0:3], lg[:], AX, ALU.max))
            v.tensor_tensor(lg[:], lg[:], mE[:, 0:3].unsqueeze(2).to_broadcast([128, 3, 8]), ALU.subtract).then_inc(s_logits_shift, 1)
            v.wait_ge(s_logits_exp, 1)
            link(v.tensor_tensor(cw, lg[:], selE, ALU.mult))
            link(v.tensor_reduce(mE[:, 4:7], cw, AX, ALU.add))
            link(v.tensor_scalar_max(mE[:, 4:7], mE[:, 4:7], 1e-30))
            link(v.reciprocal(mE[:, 8:11], mE[:, 4:7]))
            link(v.tensor_tensor(cw, cw, mE[:, 8:11].unsqueeze(2).to_broadcast([128, 3, 8]), ALU.mult))
            v.wait_ge(s_pos_done, 1)
            v.tensor_copy(pos, ps[:, 7, 32:56].rearrange("p (t e) -> p t e", t=3))
            link(v.tensor_reduce(mE[:, 12:13], ps[:, 7, 56:64], AX, ALU.max))
            v.tensor_copy(cnti[:], mE[0:1, 12:13]).then_inc(s_count_ready, 1)
            for i in range(6):
                v.wait_ge(s_rows_done, i + 1)
                t, h = i // 2, i % 2
                m = TOK[t][1]
                v.tensor_copy(hN[0:m, t, 512 * h:512 * h + 512], ps[0:m, i, :]).then_inc(s_rows_taken, 1)
            link(v.memset(yacc[:], 0.0))

            def matrices(rnd, e0, chain):
                n = 0
                for i, src in enumerate((posP, selP, cwP)):
                    ins = v.tensor_copy(cur[:, i, 0:3], src[:, :, bass.ds(e0, 1)].rearrange("p t o -> p (t o)"))
                ins.then_inc(s_moe_chain, 1)
                v.wait_ge(s_moe_chain, chain + 1)
                if rnd:
                    v.tensor_scalar_add(cur[:, 0, 0:3], cur[:, 0, 0:3], -float(SLOTS_E * rnd)).then_inc(s_moe_chain, 1)
                    v.wait_ge(s_moe_chain, chain + 2)
                for t in range(3):
                    ins = v.tensor_scalar(Dm[:, t, :], C("iota"), cur[:, 0, t:t + 1], cur[:, 1, t:t + 1],
                                          ALU.is_equal, ALU.mult)
                ins.then_inc(s_moe_chain, 1)
                v.wait_ge(s_moe_chain, chain + (3 if rnd else 2))
                for t in range(3):
                    ins = v.tensor_scalar(Dw[:, t, :], Dm[:, t, :], cur[:, 2, t:t + 1], None, ALU.mult)
                ins.then_inc(s_gather_ready, 1)

            def experts(rnd):
                L = 3 if rnd else 2
                base = {0: 0, 1: 18, 2: 45}[rnd]
                if rnd:
                    v.wait_ge(s_gather_ready, 9 * rnd)
                matrices(rnd, 0, base)
                with v.Fori(0, NE) as e0:
                    e = e0 + NE * rnd
                    for i in range(TILES_E):
                        v.wait_ge(s_split_hi, e * TILES_E + (SPLIT_AT_M + i + 1))
                        v.tensor_tensor(wlo[:, i % SPLIT, :], ring[:, (T_MOE + i) % RING, :],
                                        whi[:, i % SPLIT, :].bitcast(F32), ALU.subtract).then_inc(s_used, 1)
                        if i == 2:
                            for h in range(2):
                                v.wait_ge(s_xt_hi, e * 2 + (h + 1))
                                v.tensor_tensor(XTl[:, 4 * h:4 * h + 4, :], ps[:, 4 + h, :].rearrange("p (c s) -> p c s", c=4),
                                                XTh[:, 4 * h:4 * h + 4, :].bitcast(F32), ALU.subtract).then_inc(s_xt_lo, 1)
                            v.wait_ge(s_gathered, e * 3 + 3)
                            v.tensor_copy(DT, ps[:, 6, 0:NTOK]).then_inc(s_scatter_ready, 1)
                            matrices(rnd, e0 + 1, e0 * L + (base + L))
                        if i % 4 == 2 and 6 <= i <= 30:
                            j = (i - 6) // 4
                            v.wait_ge(s_silu_ready, e * 7 + (j + 1))
                            if j >= 2:
                                v.wait_ge(s_eact_turned, e * 7 + (j - 1))
                            v.tensor_tensor(actM[:, j % 2, :], siluM[:], ps[:, 2 * (j % 2) + 1, :], ALU.mult
                                            ).then_inc(s_eact_ready, 1)
                        if i % 4 == 2 and 10 <= i <= 34:
                            j = (i - 10) // 4
                            v.wait_ge(s_eactT_hi, e * 7 + (j + 1))
                            v.tensor_tensor(actTl[:, 4 * j:4 * j + 4, :], ps[:, 4 + j % 2, :].rearrange("p (k s) -> p k s", k=4),
                                            actTh[:, 4 * j:4 * j + 4, :].bitcast(F32), ALU.subtract).then_inc(s_eactT_lo, 1)
                    v.wait_ge(s_tile_done, e * TILES_E + (SPLIT_AT_M + TILES_E))
                    v.tensor_copy(ysb[:, 512:1024], ps[:, 7, :]).then_inc(s_y_dve, 1)
                    for c in range(DC):
                        v.wait_ge(s_share_done, e * 8 + (c + 1))
                        v.tensor_tensor(yacc[:, c, :], yacc[:, c, :], ps[:, c % 4, 0:NTOK], ALU.add).then_inc(s_share_added, 1)
                    v.wait_ge(s_share_added, e * 8 + 8)

            experts(0)
            c_ = v.value_load(cnti[0:1, 0:1], min_val=0, max_val=NTOK)
            for rnd in (1, 2):
                with v.If(c_ > SLOTS_E * rnd):
                    experts(rnd)
            residual(1, 5, lambda c: yacc[:, c, :])
            norm(4)
            for c in range(DC):
                ins = v.tensor_scalar(nT[:, c, :], nT[:, c, :], g_finT[:, c:c + 1], None, ALU.mult)
            ins.then_inc(s_final_ready, 1)
            for i in range(6):
                v.wait_ge(s_rows_done, 6 + i + 1)
                t, h = i // 2, i % 2
                m = TOK[t][1]
                v.tensor_copy(outN[0:m, t, 512 * h:512 * h + 512], ps[0:m, i, :]).then_inc(s_final_rows, 1)

        @block.tensor
        def _(pe):
            ident = C("ident")

            def mm(out, l, r, k, n, **kw):
                return pe.matmul(out, l, r, start=(k == 0), stop=(k == n - 1), **kw)

            used = Count(s_used)

            pe.wait_ge(s_consts_in, 16)
            pe.wait_ge(s_rows_in, 16 * 9)
            pe.wait_ge(s_csilu, 1)
            pe.transpose(ps[:, 7, 0:96], rowsA, ident[0:96, 0:96])
            pe.transpose(ps[:, 7, 96:160], rowsB, ident[0:64, 0:64])
            pe.transpose(ps[:, 7, 160:232], rowsC, ident[0:72, 0:72])
            pe.transpose(ps[:, 7, 232:264], rowsP[:, 0:128], ident[0:32, 0:32])
            pe.transpose(ps[:, 7, 264:296], rowsP[:, 128:256], ident[0:32, 0:32]).then_inc(s_rows_turned, 1)
            pe.wait_ge(s_x_in, 32)
            for c in range(DC):
                if c >= 4:
                    pe.wait_ge(s_x_ready, c - 3)
                for t, (t0, m) in enumerate(TOK):
                    ins = pe.transpose(ps[:, 2 + c % 4, t0:t0 + m], xrow[0:m, t, 128 * c:128 * c + 128], ident[0:m, 0:m])
                ins.then_inc(s_x_turned, 1)
            pe.wait_ge(s_cs_split, 1)
            pe.wait_ge(s_x_ready, 8)

            def turn_mod(k):
                pe.wait_ge(s_modrow, k + 1)
                for b in range(4):
                    o = ((k % 12) * 4 + b) * 9
                    ins = mm(ps[:, 2 + k // 12, o:o + 9], modrow[:, k % 2, 128 * b:128 * b + 128], C("fold", 18), 0, 1)
                ins.then_inc(s_mod_turned, 1)

            for k in range(24):
                n = 2 * k
                if k >= 2:
                    pe.wait_ge(s_modrow, k - 1)
                for kc in range(8):
                    i = n + kc // 4
                    if kc % 4 == 0:
                        pe.wait_ge(s_used, i + 1)
                    c0 = 512 * (kc % 4)
                    pe.matmul(ps[0:18, k % 2, :], csHL[:, kc, :], ahi[:, i % SPLIT, c0:c0 + 512], start=kc == 0, stop=False)
                    ins = pe.matmul(ps[0:18, k % 2, :], csHL[:, kc, :], alo[:, i % SPLIT, c0:c0 + 512], start=False,
                                    stop=kc == 7)
                    if kc % 4 == 3:
                        ins.then_inc(s_tile_done, 1)
                if k:
                    turn_mod(k - 1)
            turn_mod(23)

            def norm(n):
                for c in range(DC):
                    if n and c == 0:
                        pe.wait_ge(s_std_ready, n)
                    pe.wait_ge(s_sq_ready, 8 * n + c + 1)
                    ins = mm(ps[:, SSBANK[n], 0:NTOK], C("ones"), nT[:, c, :], c, DC)
                ins.then_inc(s_ss_done, 1)

            def h_ready(n):
                pe.wait_ge(s_h_prompt, 8 * (n + 1))
                pe.wait_ge(s_h_sample, n + 1)

            norm(0)
            h_ready(0)
            pe.wait_ge(s_mod_ready, 2)
            for ct in range(6):
                n = T_NSA + 2 * ct
                last = ct == 5
                wait_tile(pe, n)
                if not last:
                    wait_tile(pe, n + 1)
                if ct >= 2:
                    pe.wait_ge(s_proj_dve, ct - 1)
                    pe.wait_ge(s_proj_act, ct - 1)
                for t, (t0, m) in enumerate(TOK):
                    for kc in range(8):
                        if last:
                            rhs, out = slot(n, 8)[:, kc, :], ps[0:m, 3 + t, 0:48]
                        else:
                            rhs, out = slot(n + kc // 4)[:, kc % 4, :], ps[0:m, 3 * (ct % 2) + t, :]
                        ins = mm(out, hT[:, kc, t0:t0 + m], rhs, kc, 8)
                        if t == 2 and kc == 3 and not last:
                            ins.then_inc(s_used, 1)
                ins.then_inc(s_proj_done, 1)
                pe.wait_ge(s_proj_done, ct + 1)
                pe.sem_inc(s_used, 1)
            cols = [128 * i for i in range(8)] + [1536, 1664, 2048, 2176, 1024, 1152, 1280, 1408]
            pe.wait_ge(s_rope_done, 6)
            pe.wait_ge(s_gate_exp, 3)
            for i, c0 in enumerate(cols):
                if i >= 6:
                    pe.wait_ge(s_qk_prompt, i - 5)
                    pe.wait_ge(s_qk_sample, min(i - 5, 12))
                for t, (t0, m) in enumerate(TOK if i < 12 else TOK[:2]):
                    ins = pe.transpose(ps[:, i % 6, t0:t0 + m], proj[0:m, t, c0:c0 + 128], ident[0:m, 0:m])
                ins.then_inc(s_qk_turned, 1)
            pe.wait_ge(s_wbd_in, 64)
            pe.wait_ge(s_tail_pe, 1)
            pe.wait_ge(s_qk_prompt, 16)
            pe.wait_ge(s_qk_sample, 12)
            jb = [0]

            def bank_free():
                j = jb[0]
                jb[0] += 1
                back = 4 if j < J_SEL else 3
                if j >= J_SEL + 3 or 4 <= j < J_SEL:
                    q = j - back
                    pe.wait_ge(s_bank_act if q % 2 == 0 else s_bank_dve, q // 2 + 1)
                return j % 4 if j < J_SEL else 4 + (j - J_SEL) % 3

            def copied():
                pe.wait_ge(s_bank_act, (jb[0] + 1) // 2)
                pe.wait_ge(s_bank_dve, jb[0] // 2)

            for kv in range(2):
                for half in range(2):
                    for b4 in range(4):
                        n = T_CACHE + 8 * kv + 4 * half + b4
                        wait_tile(pe, n)
                        for h in range(2):
                            for gp in range(2):
                                bk = bank_free()
                                for j in range(4):
                                    ins = pe.transpose(ps[:, bk, 128 * j:128 * j + 128],
                                                       pages(n)[:, 4 * h + j, 128 * gp:128 * gp + 128], ident)
                                ins.then_inc(s_bank_turned, 1)
                        pe.wait_ge(s_bank_turned, jb[0])
                        pe.sem_inc(s_used, 1)
                    copied()
                    lo = (TAIL if half or kv else 0)
                    nblk = 256 if half else 273
                    src = work[:, lo:lo + 32 * nblk].rearrange("p (n l) -> p n l", l=32)
                    for l in range(32):
                        ins = mm(ps[:, 4 + 2 * kv + half, 0:nblk], wbd[:, kv, l, :], src[:, :, l], l, 32)
                    ins.then_inc(s_cmp_done, 1)
            pe.wait_ge(s_craw_ready, 1)
            mm(ps[:, 1, 0:16], C("rot"), praw[:, 0], 0, 1)
            mm(ps[:, 0, :], C("rot"), kraw[:].rearrange("p h n -> p (h n)"), 0, 1)
            for gp in range(2):
                pe.transpose(ps[0:8, 1, 128 + 128 * gp:256 + 128 * gp], praw[:, 1, 8 * gp:8 * gp + 8], ident)
            for b in range(NB):
                for gp in range(2):
                    o = 128 * gp + 32 * (b % 4)
                    ins = pe.transpose(ps[0:32, 2 + b // 2, 256 * (b % 2) + 128 * gp:256 * (b % 2) + 128 * gp + 128],
                                       vraw[:, b // 4, o:o + 32], ident)
            ins.then_inc(s_rot_done, 1)
            pe.wait_ge(s_ck_ready, 1)
            mm(ps[:, 0, 0:256], C("repn", 8), cvn, 0, 1).then_inc(s_cv_spread, 1)
            for t in range(2):
                for hh in range(16):
                    c, g2 = hh // 2, hh % 2
                    p_ = slice(64 * g2, 64 * g2 + 64)
                    o = 256 + 64 * t + 8 * c
                    ins = mm(ps[:, 6 + g2, o:o + 8], qT[p_, c, 128 * t:128 * t + 128],
                             ckP[p_, 8 * (c // 4):8 * (c // 4) + 8], 0, 1)
            ins.then_inc(s_cscore_done, 1)
            for tau in range(4):
                for st in range(4):
                    b, gp = 2 * tau + st // 2, st % 2
                    o = (b // 4) * 256 + gp * 128 + (b % 4) * 32
                    mm(ps[32 * st:32 * st + 32, 1, 32 * tau:32 * tau + 32], qbd[:, b, 32 * gp:32 * gp + 32],
                       ckS[:, o:o + 32], 0, 1)
            for tau in range(4):
                ins = mm(ps[:, 1, 128 + 48 * tau:176 + 48 * tau], C("rowtok", 32)[:, 128 * tau:128 * tau + 128],
                         vP[0:32, 2, 512:560], 0, 1)
            ins.then_inc(s_sc_done, 1)
            pe.wait_ge(s_cprobs, 1)
            pe.wait_ge(s_cv_ready, 4)
            mm(ps[:, 2, 0:128], C("headsum"), PcG.rearrange("p t n -> p (t n)"), 0, 1).then_inc(s_importance, 1)
            for t in range(2):
                pe.wait_ge(s_cprob_ready, t + 1)
                ins = pe.transpose(ps[:, 5, 128 * t:128 * t + 128], ScP[:, t, :], ident)
            ins.then_inc(s_cprob_turned, 1)
            pe.wait_ge(s_cprobT_ready, 1)
            for i in range(35):
                if i < 32:
                    t, hh = i // 16, i % 16
                    c, g2 = hh // 2, hh % 2
                    p_ = slice(64 * g2, 64 * g2 + 64)
                    w = 128 * (t + 1)
                    if i >= 3:
                        pe.wait_ge(s_scores_taken, i - 2)
                    mm(ps[:, i % 3, 0:2 * w], qT[p_, c, 128 * t:128 * t + 128], kTp[p_, c // 4, :, 0:w], 0, 1
                       ).then_inc(s_scores_done, 1)
                if 2 <= i < 34:
                    u = i - 2
                    w = 128 * (u // 16 + 1)
                    pe.wait_ge(s_probs_ready, u + 1)
                    if u >= 2:
                        pe.wait_ge(s_probsT_ready, u - 1)
                    for k in range(2 * w // 128):
                        ins = pe.transpose(ps[:, 3 + u % 2, 128 * k:128 * k + 128],
                                           Ssb[:, u % 3, 128 * k:128 * k + 128], ident)
                    ins.then_inc(s_probs_turned, 1)
                if i >= 3:
                    u = i - 3
                    t, hh = u // 16, u % 16
                    c, g2 = hh // 2, hh % 2
                    bank = 5 + (u // 2) % 2
                    pe.wait_ge(s_probsT_ready, u + 1)
                    if g2 == 0:
                        if u >= 4:
                            pe.wait_ge(s_o_taken, u // 2 - 1)
                        pe.matmul(ps[:, bank, 0:128], Vbd[:, c, :], PTc[:, t, :], start=True, stop=False,
                                  skip_group_check=True)
                    g_ = 2 * (c // 4) + g2
                    for k in range(2):
                        for kt in range(t + 1):
                            c0 = 256 * k + 64 * g_
                            ins = pe.matmul(ps[64 * g2:64 * g2 + 64, bank, 0:128], vP[:, kt, c0:c0 + 64],
                                            PTs[:, u % 2, (k * (t + 1) + kt) * 128:(k * (t + 1) + kt) * 128 + 128],
                                            start=False, stop=(k == 1 and kt == t), skip_group_check=True)
                    ins.then_inc(s_pv_done, 1)
            pe.wait_ge(s_o_taken, 16)

            def turn_keys(tau):
                for i in range(3):
                    n = tile_k[tau] + i
                    wait_tile(pe, n)
                    for q in range(4):
                        bk = bank_free()
                        for j in range(4):
                            page, gp = (4 * (q % 2) + j, q // 2) if i < 2 else (4 * (q // 2) + j, q % 2)
                            ins = pe.transpose(ps[:, bk, 128 * j:128 * j + 128],
                                               pages(n)[:, page, 128 * gp:128 * gp + 128], ident)
                        ins.then_inc(s_bank_turned, 1)
                    pe.wait_ge(s_bank_turned, jb[0])
                    pe.sem_inc(s_used, 1)

            def turn_out(tau):
                pe.wait_ge(s_osb_ready, tau + 1)
                pe.transpose(ps[:, 7, 128:256], osb, ident).then_inc(s_osb_turned, 1)

            turn_keys(0)
            for tau in range(4):
                copied()
                if tau:
                    pe.wait_ge(s_snegmax, tau)
                for b2 in range(2):
                    b = 2 * tau + b2
                    for gp in range(2):
                        o_ = slice(32 * (2 * b2 + gp), 32 * (2 * b2 + gp) + 32)
                        q_ = qbd[:, b, 32 * gp:32 * gp + 32]
                        mm(ps[o_, 3, 0:32], q_, kTn[:, gp, 0, :], 0, 1)
                        mm(ps[o_, 3, 32:64], q_, kTn[:, gp, 1, :], 0, 1)
                        mm(ps[o_, 0, :], q_, TS[:, tau % 2, b2, gp, 0:512], 0, 1)
                        mm(ps[o_, 1, :], q_, TS[:, tau % 2, b2, gp, 512:1024], 0, 1)
                        ins = mm(ps[o_, 2, :], q_, TW[:, tau % 2, b2, gp, :], 0, 1)
                    ins.then_inc(s_seq_scores, 1)
                pe.wait_ge(s_seq_scores, 2 * tau + 2)
                pe.sem_inc(s_group_scores, 1)
                if tau:
                    turn_out(tau - 1)
                if tau < 3:
                    turn_keys(tau + 1)
                pe.wait_ge(s_group_probs, tau + 1)
                for i in range(3):
                    bk = bank_free()
                    for k in range(4):
                        c0 = (0, 512, 1056)[i] + 128 * k
                        ins = pe.transpose(ps[:, bk, 128 * k:128 * k + 128], SS[:, c0:c0 + 128], ident)
                    ins.then_inc(s_bank_turned, 1)
                bk = bank_free()
                for k, src in enumerate((SS[:, 1024:1056], SS[:, 1568:1600], PcG[:, tau, :])):
                    ins = pe.transpose(ps[0:32, bk, 128 * k:128 * k + 128], src, ident)
                ins.then_inc(s_bank_turned, 1)
                copied()
                if tau:
                    pe.wait_ge(s_group_o, tau)
                for i in range(3):
                    wait_tile(pe, tile_v[tau] + i)
                for st in range(4):
                    b2, gp = st // 2, st % 2
                    m_ = slice(32 * st, 32 * st + 32)
                    c_ = slice(128 * gp, 128 * gp + 128)
                    for k in range(12):
                        val = pages(tile_v[tau] + b2)[:, k, c_] if k < 8 else pages(tile_v[tau] + 2)[:, 4 * b2 + k - 8, c_]
                        mm(ps[m_, 7, 0:128], PT[:, k, m_], val, k, 15)
                    for k, val in ((12, vP[0:32, 2, c_]), (13, vP[0:32, 2, 256 + 128 * gp:384 + 128 * gp]),
                                   (14, cvS[:, 2 * tau + b2, c_])):
                        ins = mm(ps[m_, 7, 0:128], PT[0:32, k, m_], val, k, 15)
                ins.then_inc(s_group_pv, 1)
                pe.wait_ge(s_group_pv, tau + 1)
                pe.sem_inc(s_used, 3)
            turn_out(3)
            pe.wait_ge(s_group_o, 4)

            def dense(n, mov, out, done, ntile=2):
                wait_tile(pe, n)
                wait_tile(pe, n + 1)
                for b in range(4):
                    o = out(b)
                    for kc in range(8):
                        ins = mm(o, slot(n + kc // 4)[:, kc % 4, 128 * b:128 * b + 128], mov(kc), kc, 8)
                        if b == 3 and kc == 3:
                            ins.then_inc(s_used, 1)
                    ins.then_inc(done, 1)
                    nd[done] = nd.get(done, 0) + 1
                pe.wait_ge(done, nd[done])
                pe.sem_inc(s_used, 1)

            nd = {}

            def wo_bank(ch):
                def f(b):
                    c = 4 * ch + b
                    if c >= 6:
                        pe.wait_ge(s_x_ready, 8 + c - 5)
                    return ps[:, c % 6, 0:NTOK]
                return f
            for ch in range(2):
                dense(T_WO + 2 * ch, lambda kc: oT[:, kc, :], wo_bank(ch), s_wo_done)
            norm(1)
            def split_mm(out, hi, lo, xh, xl, first, last):
                pe.matmul(out, hi, xh, start=first, stop=False)
                pe.matmul(out, hi, xl, start=False, stop=False)
                return pe.matmul(out, lo, xh, start=False, stop=last)

            def w_block(hi, lo, i, k, b):
                c0 = 512 * k + 128 * b
                return hi[:, i % SPLIT_F, c0:c0 + 128], lo[:, i % SPLIT_F, c0:c0 + 128]

            for i in range(28):
                j, u, half = i // 4, (i // 2) % 2, i % 2
                pe.wait_ge(s_used, T_FU + i + 1)
                if j and half == 0:
                    pe.wait_ge(s_ffn_taken if u else s_ffn_silu, j)
                for k in range(4):
                    kc = 4 * half + k
                    if i < 2:
                        pe.wait_ge(s_h_split, kc + 1)
                    for b in range(4):
                        ins = split_mm(ps[:, 4 * u + b, 0:NTOK], *w_block(fhi, flo, i, k, b), hTh[:, kc, :], hTl[:, kc, :],
                                       kc == 0, kc == 7)
                ins.then_inc(s_tile_done, 1)
            for ch in range(2):
                pe.wait_ge(s_ffn_taken if ch else s_ffn_silu, 7)
                for i in range(7):
                    t = 28 + 7 * ch + i
                    pe.wait_ge(s_used, T_FU + t + 1)
                    if ch == 0:
                        pe.wait_ge(s_ffn_act, i + 1)
                    for kc in range(4):
                        m = 4 * i + kc
                        for b in range(4):
                            ins = split_mm(ps[:, 4 * ch + b, 0:NTOK], *w_block(fhi, flo, t, kc, b), actFh[:, m, :], actFl[:, m, :],
                                           m == 0, m == 27)
                    ins.then_inc(s_tile_done, 1)
            norm(2)
            h_ready(2)
            pe.wait_ge(s_state_in, 16)
            for c in range(DC):
                ins = pe.transpose(ps[:, 7, 16 * c:16 * c + 16], strow[:, 128 * c:128 * c + 128], ident[0:16, 0:16])
            ins.then_inc(s_state_turned, 1)

            for i in range(TILES_C):
                k, half = i // 2, i % 2
                if i == 14:
                    pe.wait_ge(s_tail_ready, 1)
                    for c in range(DC):
                        ins = pe.transpose(ps[0:18, 6 + c // 4, 128 * (c % 4):128 * (c % 4) + 128], tail[:, c, :], ident)
                        if c % 4 == 3:
                            ins.then_inc(s_tail_turned, 1)
                    pe.wait_ge(s_tail_rows, 2)
                pe.wait_ge(s_used, T_CI + i + 1)
                if k == 1 and half == 0:
                    pe.wait_ge(s_state_taken, 1)
                if k >= 2 and half == 0:
                    jt, wh = (k - 2) // 3, (k - 2) % 3
                    if wh < 2:
                        pe.wait_ge(s_conv_copied, 2 * jt + wh + 1)
                    else:
                        pe.wait_ge(s_u_ready, 4 * jt + 4)
                for q in range(4):
                    kc = 4 * half + q
                    if i < 2:
                        pe.wait_ge(s_h_split, 8 + kc + 1)
                    if k == 6:
                        pe.wait_ge(s_z_ready, kc + 1)
                    xh, xl = (cTh, cTl) if k < 6 else (zTh, zTl)
                    for b in range(4):
                        ins = split_mm(ps[:, 4 * (k % 2) + b, 0:NTOK], *w_block(chi, clo, i, q, b), xh[:, kc, :], xl[:, kc, :],
                                       kc == 0, kc == 7)
                ins.then_inc(s_tile_done, 1)
            norm(3)
            h_ready(3)
            pe.wait_ge(s_router_in, 32)
            for t, (t0, m) in enumerate(TOK):
                for kc in range(DC):
                    ins = mm(ps[0:m, 7, 8 * t:8 * t + 8], hT[:, kc, t0:t0 + m], wr[:, kc, :], kc, DC)
            ins.then_inc(s_logits_done, 1)

            def to_tokens(src, base):
                for i in range(6):
                    t, h = i // 2, i % 2
                    t0, m = TOK[t]
                    for q in range(4):
                        ins = pe.transpose(ps[0:m, i, 128 * q:128 * q + 128], src[:, 4 * h + q, t0:t0 + m], ident)
                    ins.then_inc(s_rows_done, 1)
            pe.wait_ge(s_x_ready, 32)
            to_tokens(hT, 0)
            pe.wait_ge(s_sel_ready, 1)
            for t in range(3):
                for k in range(t):
                    mm(ps[:, 7, 32 + 8 * t:40 + 8 * t], C("ones"), selE[:, k, :], k, t + 1)
                mm(ps[:, 7, 32 + 8 * t:40 + 8 * t], C("earlier"), selE[:, t, :], t, t + 1)
            for t in range(3):
                ins = mm(ps[:, 7, 56:64], C("ones"), selE[:, t, :], t, 3)
            ins.then_inc(s_pos_done, 1)
            pe.wait_ge(s_rows_taken, 6)
            pe.wait_ge(s_count_ready, 1)

            def experts(rnd):
                with pe.Fori(0, NE) as e0:
                    e = e0 + NE * rnd
                    pe.wait_ge(s_gather_ready, e0 + (9 * rnd + 1))
                    for h in range(2):
                        for c in range(4 * h, 4 * h + 4):
                            for t, (_, m) in enumerate(TOK):
                                ins = mm(ps[:, 4 + h, 128 * (c % 4):128 * (c % 4) + 128],
                                         hN[0:m, t, 128 * c:128 * c + 128], Dm[0:m, t, :], t, 3)
                        ins.then_inc(s_gathered, 1)
                    for t, (t0, m) in enumerate(TOK):
                        ins = pe.transpose(ps[:, 6, t0:t0 + m], Dw[0:m, t, :], ident[0:m, 0:m])
                    ins.then_inc(s_gathered, 1)

                    def split_wait(i):
                        pe.wait_ge(s_used, e * TILES_E + (T_MOE + i + 1))

                    def turn(j):
                        pe.wait_ge(s_eact_ready, e * 7 + (j + 1))
                        if j >= 2:
                            pe.wait_ge(s_eactT_lo, e * 7 + (j - 1))
                        for q in range(4):
                            ins = pe.transpose(ps[:, 4 + j % 2, 128 * q:128 * q + 128],
                                               actM[:, j % 2, 128 * q:128 * q + 128], ident)
                        ins.then_inc(s_eact_turned, 1)
                    for j in range(7):
                        if j >= 2:
                            pe.wait_ge(s_eact_ready, e * 7 + (j - 1))
                        for u in range(2):
                            out = ps[:, 2 * (j % 2) + u, :]
                            for kc in range(8):
                                i = 4 * j + 2 * u + kc // 4
                                if kc % 4 == 0:
                                    split_wait(i)
                                if i < 2 and kc % 4 == 0:
                                    pe.wait_ge(s_xt_lo, e * 2 + (i + 1))
                                hi = whi[:, i % SPLIT, 512 * (kc % 4):512 * (kc % 4) + 512]
                                lo = wlo[:, i % SPLIT, 512 * (kc % 4):512 * (kc % 4) + 512]
                                pe.matmul(out, XTh[:, kc, :], hi, start=kc == 0, stop=False)
                                pe.matmul(out, XTh[:, kc, :], lo, start=False, stop=False)
                                ins = pe.matmul(out, XTl[:, kc, :], hi, start=False, stop=kc == 7)
                                if kc % 4 == 3:
                                    ins.then_inc(s_tile_done, 1)
                        if j:
                            turn(j - 1)
                    pe.wait_ge(s_scatter_ready, e + 1)
                    for i in range(14):
                        if i == 4:
                            turn(6)
                        split_wait(28 + i)
                        hi = whi[:, (28 + i) % SPLIT, :].rearrange("p (k n) -> p k n", k=2)
                        lo = wlo[:, (28 + i) % SPLIT, :].rearrange("p (k n) -> p k n", k=2)
                        for kk in range(2):
                            k = 2 * i + kk
                            if k % 4 == 0:
                                pe.wait_ge(s_eactT_lo, e * 7 + (k // 4 + 1))
                            for a_, w_, first, last in ((actTh, hi, True, False), (actTh, lo, False, False),
                                                        (actTl, hi, False, True)):
                                for h in range(2):
                                    ins = pe.matmul(ps[:, 6 + h, :], a_[:, k, :], w_[:, kk, 512 * h:512 * h + 512],
                                                    start=first and k == 0, stop=last and k == 27)
                        ins.then_inc(s_tile_done, 1)
                    pe.wait_ge(s_y_act, e + 1)
                    pe.wait_ge(s_y_dve, e + 1)
                    for c in range(DC):
                        if c >= 4:
                            pe.wait_ge(s_share_added, e * 8 + (c - 3))
                        mm(ps[:, c % 4, 0:NTOK], ysb[:, 128 * c:128 * c + 128], DT, 0, 1).then_inc(s_share_done, 1)
                    pe.wait_ge(s_share_added, e * 8 + 8)

            experts(0)
            c_ = pe.value_load(cnti[0:1, 0:1], min_val=0, max_val=NTOK)
            for rnd in (1, 2):
                with pe.If(c_ > SLOTS_E * rnd):
                    experts(rnd)
            norm(4)
            pe.wait_ge(s_final_ready, 1)
            to_tokens(nT, 6)


def constants():
    import numpy as np
    t = {n: np.zeros((128, w), np.float32) for n, w in CONSTS}
    p = np.arange(128)
    t["ident"][:] = np.eye(128)
    t["causal"][:, 128:] = np.where(p[None, :] <= p[:, None], 0.0, -BIG)
    d = p % 64
    for q in range(128):
        if d[q] < 8:
            t["rot"][q + 8, q] = -1.0
        elif d[q] < 16:
            t["rot"][q - 8, q] = 1.0
    inv = (1.0 / (np.float32(500000.0) ** (np.arange(8, dtype=np.float32) * np.float32(2.0 / 16)))).astype(np.float32)
    cend = (np.arange(32) * 32 + 31).astype(np.float32)
    ang = (cend[:, None] * inv[None, :]).astype(np.float32)
    for q in range(128):
        if d[q] < 16:
            t["ckcos"][q] = np.cos(ang[:, d[q] % 8])
            t["cksin"][q] = np.sin(ang[:, d[q] % 8])
        else:
            t["ckcos"][q] = 1.0
    posn = np.stack([p, 128 + p, 1024 + p % 4], 1).astype(np.float32)
    ang = (posn[:, :, None] * inv).astype(np.float32)
    t["tcos"][:] = np.cos(ang).reshape(128, 24)
    t["tsin"][:] = np.sin(ang).reshape(128, 24)
    ce = np.arange(8) * 32 + 31
    for k in range(2):
        vis = ce[None, :] <= (128 * k + p)[:, None]
        t["cmpadd"][:, 8 * k:8 * k + 8] = np.where(vis, 0.0, -BIG)
        t["cmpmul"][:, 8 * k:8 * k + 8] = vis
    b2, gp, g2, r, tt = p // 64, (p // 32) % 2, (p // 16) % 2, (p // 4) % 4, p % 4
    key = (b2 * 2 + gp) * 8 + g2 * 4 + tt
    t["headsum"][:] = key[:, None] == key[None, :]
    t["bonus"][:, 0] = 5.0
    t["bonus"][:, 16] = 5.0
    t["winmask"][:] = np.where(np.arange(4)[None, :] >= tt[:, None], 0.0, -BIG)
    n = np.arange(32)
    for tau in range(4):
        ok = (n[None, :] // 4 == (2 * tau + b2)[:, None]) & (n[None, :] % 4 <= tt[:, None])
        t["newmask"][:, 32 * tau:32 * tau + 32] = np.where(ok, 0.0, -BIG)
        t["rowtok"][0:32, 128 * tau:128 * tau + 128] = n[:, None] == ((2 * tau + b2) * 4 + tt)[None, :]
    t["rowhead"][:] = np.arange(16)[None, :] == (gp * 8 + g2 * 4 + r)[:, None]
    j = np.arange(17)
    t["before"][:] = (j[None, :] < j[:, None]).reshape(1, 289)
    t["repn"][0:8, :] = np.arange(8)[:, None] == (p % 8)[None, :]
    for c in range(8):
        for g in range(2):
            t["vbdmask"][:, 2 * c + g] = (p // 8) == (2 * c + g)
    t["earlier"][:] = p[:, None] < p[None, :]
    t["ones"][:] = 1.0
    t["iota"][:] = p[None, :]
    t["valid"][:, 0:2] = 1.0
    t["valid"][0:32, 2] = 1.0
    t["eps"][:] = EPS
    t["fold"][0:18] = (np.arange(18)[:, None] % 9) == np.arange(9)[None, :]
    return np.concatenate([t[n] for n, _ in CONSTS], 1)


_INS = ["x_prompt", "x_sample", "cache_cmp_kv", "cache_sel_kv", "cache_win_kv", "state_conv", "page_table", "c_prompt",
        "c_sample", "w_ada", "b_ada", "g_norm_mix", "g_norm_ffn", "g_norm_final", "w_nsa_in", "w_nsa_out", "w_cmp_k",
        "pe_cmp_k", "w_cmp_v", "pe_cmp_v", "w_conv_in", "w_conv", "w_conv_out", "w_ff_gu", "w_ff_down", "w_router",
        "b_router", "w_moe_gu", "w_moe_down"]
_OUTS = [(1, 256, 1024), (8, 4, 1024), (1, 1, 256, 2, 4, 64), (1, 8, 4, 2, 4, 64), (1, 1, 256, 2, 4, 64),
         (1, 8, 4, 2, 4, 64), (1, 1, 256, 2, 4, 64), (1, 8, 512, 2, 4, 64), (1, 1, 2, 1024), (1, 8, 2, 1024)]


def kernel(**inputs):
    import numpy as _np
    import concourse.bacc as _bacc
    from concourse.bass_utils import run_bass_kernel_spmd as _run

    nc = _bacc.Bacc("TRN2", target_bir_lowering=False, num_devices=1)
    arrays, A = {}, {}
    for name in _INS + ["consts"]:
        a = constants() if name == "consts" else _np.ascontiguousarray(inputs[name])
        arrays[f"in_{name}"] = a
        A[name] = nc.dram_tensor(f"in_{name}", a.shape, mybir.dt.from_np(a.dtype), kind="ExternalInput").ap()
    O = [nc.dram_tensor(f"out_{i}", sh, F32, kind="ExternalOutput").ap() for i, sh in enumerate(_OUTS)]
    trunk(nc, A, O)
    r = _run(nc, [arrays], core_ids=[0])
    return tuple(r.results[0][f"out_{i}"] for i in range(len(_OUTS)))
```
